# Optimizing a Trainium2 kernel written in Bass

```python
import math
import jax, jax.numpy as jnp
from jax import lax
import numpy as np

D_MODEL = 1024
BATCH = 1
SEQ = 128
DEPTH = 2
DEC_BATCH = 1
DEC_SEQ = 256
PAST_LEN = 128

GRID_W = 64
ROPE_BASE = 10000.0
DIFF_HEADS = 4
DIFF_DH = 64
DIFF_WIDTH = DIFF_HEADS * 2 * DIFF_DH
POOL_GROUPS = 4
POOL_WIDTH = D_MODEL - DIFF_WIDTH
POOL_GC = POOL_WIDTH // POOL_GROUPS
POOL_WINDOWS = (2, 4, 8, 16)
Q_BLOCK = 128
W_IN_A = 3 * DIFF_WIDTH + POOL_WIDTH
MLSTM_HEADS = 8
MLSTM_DH = D_MODEL // MLSTM_HEADS
MLSTM_CHUNK = 64
N_GATES = 4
W_IN_C = 4 * D_MODEL + N_GATES * MLSTM_HEADS
D_FF = 2816
N_EXPERTS = 8
TOP_K = 2
D_FF_EXPERT = 1792
LN_EPS = 1e-5

kernel_name = "diffattn_pool_mlstm_moe_prefix_dit_step"

def _layer_norm(x, g, b):
    xf = x.astype(jnp.float32)
    mu = jnp.mean(xf, axis=-1, keepdims=True)
    var = jnp.mean(jnp.square(xf - mu), axis=-1, keepdims=True)
    y = (xf - mu) * lax.rsqrt(var + LN_EPS)
    return (y * g.astype(jnp.float32) + b.astype(jnp.float32)).astype(x.dtype)

def _modulation(cvec, ada_w, ada_b):
    m = jax.nn.silu(cvec) @ ada_w + ada_b
    return jnp.split(m, 6, axis=-1)

def _modulate(x, shift, scale):
    return x * (1.0 + scale) + shift

def _post_norm(x, out, gate, g, b, alpha):
    return _layer_norm(alpha * x + gate * out, g, b)

def _swiglu(h, w_gu, w_down):
    gate, up = jnp.split(h @ w_gu, 2, axis=-1)
    return (jax.nn.silu(gate) * up) @ w_down

def _axial_rope_tables(n_tokens):
    rows = n_tokens // GRID_W
    row_pos = jnp.repeat(jnp.arange(rows), GRID_W).astype(jnp.float32)
    col_pos = jnp.tile(jnp.arange(GRID_W), rows).astype(jnp.float32)
    n_freq = DIFF_DH // 4
    inv_freq = jnp.power(ROPE_BASE, -jnp.arange(n_freq, dtype=jnp.float32) / n_freq)
    ang = jnp.stack([row_pos[:, None] * inv_freq, col_pos[:, None] * inv_freq], axis=1)
    return jnp.cos(ang), jnp.sin(ang)

def _rope2d(x, cos, sin):
    shp = x.shape
    xr = x.reshape(shp[:-1] + (2, 2, DIFF_DH // 4)).astype(jnp.float32)
    x1, x2 = xr[..., 0, :], xr[..., 1, :]
    c, s = cos[:, None], sin[:, None]
    out = jnp.stack([x1 * c - x2 * s, x2 * c + x1 * s], axis=-2)
    return out.reshape(shp).astype(x.dtype)

def _diff_lambda(lam_p, layer_idx):
    lam_init = 0.8 - 0.6 * math.exp(-0.3 * layer_idx)
    lp = lam_p.astype(jnp.float32)
    lam = jnp.exp(jnp.sum(lp[0] * lp[1])) - jnp.exp(jnp.sum(lp[2] * lp[3])) + lam_init
    return lam, lam_init

def _diff_attention(q, k, v, lam, lam_init, norm_g):
    B, H, Tq = q.shape[:3]
    nb = Tq // Q_BLOCK
    scale = DIFF_DH ** -0.5
    qb = jnp.moveaxis(q.reshape(B, H, nb, Q_BLOCK, 2, DIFF_DH), 2, 0)

    def block(qblk):
        s = jnp.einsum('bhqjd,bhkjd->jbhqk', qblk, k, preferred_element_type=jnp.float32) * scale
        p = jax.nn.softmax(s, axis=-1)
        a = p[0] - lam * p[1]
        return jnp.einsum('bhqk,bhkv->bhqv', a.astype(v.dtype), v)

    o = lax.map(block, qb)
    o = jnp.moveaxis(o, 0, 2).reshape(B, H, Tq, 2 * DIFF_DH).astype(jnp.float32)
    o = o * lax.rsqrt(jnp.mean(jnp.square(o), axis=-1, keepdims=True) + LN_EPS)
    o = o * norm_g.astype(jnp.float32) * (1.0 - lam_init)
    return o.astype(v.dtype).transpose(0, 2, 1, 3).reshape(B, Tq, DIFF_WIDTH)

def _multiscale_pool(u, pool_w, pool_scale):
    B, T, _ = u.shape
    uf = u.astype(jnp.float32).reshape(B, T, POOL_GROUPS, POOL_GC)
    csum = jnp.concatenate([jnp.zeros((B, 1, POOL_GROUPS, POOL_GC), jnp.float32),
                            jnp.cumsum(uf, axis=1)], axis=1)
    t = jnp.arange(T)
    outs = []
    for g, w in enumerate(POOL_WINDOWS):
        lo = jnp.clip(t - w // 2, 0, T - 1)
        hi = jnp.clip(t + w // 2 - 1, 0, T - 1)
        cg = csum[:, :, g]
        win_sum = cg[:, hi + 1] - cg[:, lo]
        cnt = (hi - lo + 1).astype(jnp.float32)[None, :, None]
        outs.append(win_sum / cnt - uf[:, :, g])
    pooled = jnp.stack(outs, axis=2)
    mixed = jnp.einsum('btgc,gcd->btgd', pooled, pool_w.astype(jnp.float32))
    return (mixed.reshape(B, T, POOL_WIDTH) * pool_scale.astype(jnp.float32)).astype(u.dtype)

def _split_attn_pool(proj):
    B, T, _ = proj.shape
    q, k, v, p = jnp.split(proj, [DIFF_WIDTH, 2 * DIFF_WIDTH, 3 * DIFF_WIDTH], axis=-1)
    q = q.reshape(B, T, DIFF_HEADS, 2, DIFF_DH).transpose(0, 2, 1, 3, 4)
    k = k.reshape(B, T, DIFF_HEADS, 2, DIFF_DH).transpose(0, 2, 1, 3, 4)
    v = v.reshape(B, T, DIFF_HEADS, 2 * DIFF_DH).transpose(0, 2, 1, 3)
    return q, k, v, p

def _attn_pool_context(h, w_in, lam, lam_init, norm_g, pool_w, pool_scale, w_out):
    B, T, _ = h.shape
    q, k, v, p = _split_attn_pool(h @ w_in)
    a = _diff_attention(q, k, v, lam, lam_init, norm_g)
    out = jnp.concatenate([a, _multiscale_pool(p, pool_w, pool_scale)], axis=-1) @ w_out
    return out, k.reshape(B, DIFF_HEADS, T, 2 * DIFF_DH), v

def _attn_pool_latent(h, ctx_k, ctx_v, w_in, lam, lam_init, norm_g, pool_w, pool_scale, w_out):
    B, T, _ = h.shape
    Tc = ctx_k.shape[2]
    q, k, v, p = _split_attn_pool(h @ w_in)
    cos, sin = _axial_rope_tables(T)
    q = _rope2d(q, cos, sin)
    k = _rope2d(k, cos, sin)
    k_all = jnp.concatenate([ctx_k.reshape(B, DIFF_HEADS, Tc, 2, DIFF_DH).astype(k.dtype), k], axis=2)
    v_all = jnp.concatenate([ctx_v.astype(v.dtype), v], axis=2)
    a = _diff_attention(q, k_all, v_all, lam, lam_init, norm_g)
    return jnp.concatenate([a, _multiscale_pool(p, pool_w, pool_scale)], axis=-1) @ w_out

def _mlstm_chunkwise(q, k, v, ig, lf, C0, n0, m0):
    B, H, T, d = q.shape
    nc = T // MLSTM_CHUNK

    def chunks(x):
        return jnp.moveaxis(x.reshape(x.shape[:2] + (nc, MLSTM_CHUNK) + x.shape[3:]), 2, 0)

    causal = jnp.tril(jnp.ones((MLSTM_CHUNK, MLSTM_CHUNK), dtype=bool))

    def step(carry, xs):
        C, n, m = carry
        qc, kc, vc, ic, fc = xs
        b = jnp.cumsum(fc, axis=-1)
        dmat = jnp.where(causal, b[..., :, None] - b[..., None, :] + ic[..., None, :], -jnp.inf)
        m_inter = b + m[..., None]
        m_t = jnp.maximum(m_inter, jnp.max(dmat, axis=-1))
        w_inter = jnp.exp(m_inter - m_t)
        s = jnp.einsum('bhtd,bhsd->bhts', qc, kc) * jnp.exp(dmat - m_t[..., None])
        num = w_inter[..., None] * jnp.einsum('bhtd,bhde->bhte', qc, C) + jnp.einsum('bhts,bhse->bhte', s, vc)
        den = w_inter * jnp.einsum('bhtd,bhd->bht', qc, n) + jnp.sum(s, axis=-1)
        h = num / jnp.maximum(jnp.abs(den), jnp.exp(-m_t))[..., None]
        m_new = m_t[..., -1]
        w_c = jnp.exp(b[..., -1] + m - m_new)
        w_s = jnp.exp(b[..., -1:] - b + ic - m_new[..., None])
        C_new = w_c[..., None, None] * C + jnp.einsum('bhs,bhsd,bhse->bhde', w_s, kc, vc)
        n_new = w_c[..., None] * n + jnp.einsum('bhs,bhsd->bhd', w_s, kc)
        return (C_new, n_new, m_new), h

    (C, n, m), h = lax.scan(step, (C0, n0, m0), (chunks(q), chunks(k), chunks(v), chunks(ig), chunks(lf)))
    h = jnp.moveaxis(h, 0, 2).reshape(B, H, T, d)
    return h, C, n, m

def _mlstm_mixer(h, w_in, b_gates, head_g, w_out, C0, n0, m0):
    B, T, _ = h.shape
    proj = h @ w_in
    q, k, v, o, g = jnp.split(proj, [D_MODEL, 2 * D_MODEL, 3 * D_MODEL, 4 * D_MODEL], axis=-1)

    def heads(x):
        return x.reshape(B, T, MLSTM_HEADS, MLSTM_DH).transpose(0, 2, 1, 3).astype(jnp.float32)

    q, k, v = heads(q), heads(k) * (MLSTM_DH ** -0.5), heads(v)
    g = (g.astype(jnp.float32) + b_gates.astype(jnp.float32)).reshape(B, T, N_GATES, MLSTM_HEADS)
    g = g.transpose(2, 0, 3, 1)
    ig = g[0::2]
    lf = jax.nn.log_sigmoid(g[1::2])
    C0, n0, m0 = C0.astype(jnp.float32), n0.astype(jnp.float32), m0.astype(jnp.float32)

    def flip(x):
        return jnp.flip(x, axis=2)

    h_f, Cf, nf, mf = _mlstm_chunkwise(q, k, v, ig[0], lf[0], C0[:, 0], n0[:, 0], m0[:, 0])
    h_b, Cb, nb, mb = _mlstm_chunkwise(flip(q), flip(k), flip(v), flip(ig[1]), flip(lf[1]),
                                       C0[:, 1], n0[:, 1], m0[:, 1])
    hs = h_f + flip(h_b)
    mu = jnp.mean(hs, axis=-1, keepdims=True)
    var = jnp.mean(jnp.square(hs - mu), axis=-1, keepdims=True)
    hn = ((hs - mu) * lax.rsqrt(var + LN_EPS)).transpose(0, 2, 1, 3).reshape(B, T, D_MODEL)
    hn = hn * head_g.astype(jnp.float32)
    out = (jax.nn.sigmoid(o.astype(jnp.float32)) * hn).astype(h.dtype) @ w_out
    return out, jnp.stack([Cf, Cb], axis=1), jnp.stack([nf, nb], axis=1), jnp.stack([mf, mb], axis=1)

def _moe_swiglu(h, router_w, router_b, w_gu, w_down):
    logits = jnp.einsum('btd,de->bte', h, router_w, preferred_element_type=jnp.float32)
    logits = logits + router_b.astype(jnp.float32)
    top_val, top_idx = lax.top_k(logits, TOP_K)
    top_w = jax.nn.softmax(top_val, axis=-1)
    combine = jnp.sum(jax.nn.one_hot(top_idx, N_EXPERTS, dtype=jnp.float32) * top_w[..., None], axis=-2)
    out = jnp.zeros(h.shape, jnp.float32)
    for e in range(N_EXPERTS):
        out = out + combine[..., e:e + 1] * _swiglu(h, w_gu[e], w_down[e]).astype(jnp.float32)
    return out.astype(h.dtype)

def setup_inputs(seed: int = 0) -> dict:
    key = jax.random.key(seed)
    keys = list(jax.random.split(key, 40))
    f32 = jnp.float32
    n_attn = (DEPTH + 1) // 2
    n_rec = DEPTH // 2
    beta = (8.0 * DEPTH) ** -0.25

    def normal(i, shape, scale=1.0):
        return scale * jax.random.normal(keys[i], shape, f32)

    H = MLSTM_HEADS
    igate_b = normal(30, (n_rec, 2, 1, H), 0.1)
    fgate_b = jnp.linspace(3.0, 6.0, H, dtype=f32)[None, None, None, :] + normal(31, (n_rec, 2, 1, H), 0.1)
    b_gates_c = jnp.concatenate([igate_b, fgate_b], axis=2).reshape(n_rec, N_GATES * H)
    return {
        "x_prompt": normal(0, (BATCH, SEQ, D_MODEL)),
        "x_sample": normal(1, (DEC_BATCH, DEC_SEQ, D_MODEL)),
        "c": normal(2, (DEC_BATCH, D_MODEL)),
        "cache_k": normal(3, (DEC_BATCH, n_attn, DIFF_HEADS, PAST_LEN, 2 * DIFF_DH)),
        "cache_v": normal(4, (DEC_BATCH, n_attn, DIFF_HEADS, PAST_LEN, 2 * DIFF_DH)),
        "state_C": normal(5, (DEC_BATCH, n_rec, 2, H, MLSTM_DH, MLSTM_DH), 0.1),
        "state_n": normal(6, (DEC_BATCH, n_rec, 2, H, MLSTM_DH), 0.1),
        "state_m": normal(7, (DEC_BATCH, n_rec, 2, H)),
        "c_ctx": normal(8, (D_MODEL,)),
        "ada_w": normal(9, (DEPTH, D_MODEL, 6 * D_MODEL), D_MODEL ** -0.5),
        "ada_b": normal(10, (DEPTH, 6 * D_MODEL), 0.02),
        "ln_g": 1.0 + normal(11, (DEPTH, 2, D_MODEL), 0.02),
        "ln_b": normal(12, (DEPTH, 2, D_MODEL), 0.02),
        "w_in_a": normal(13, (n_attn, D_MODEL, W_IN_A), D_MODEL ** -0.5),
        "diff_lambda": normal(14, (n_attn, 4, DIFF_DH), 0.1),
        "diff_norm_g": 1.0 + normal(15, (n_attn, 2 * DIFF_DH), 0.02),
        "pool_w": normal(16, (n_attn, POOL_GROUPS, POOL_GC, POOL_GC), POOL_GC ** -0.5),
        "pool_scale": 1.0 + normal(17, (n_attn, POOL_WIDTH), 0.1),
        "w_out_a": normal(18, (n_attn, D_MODEL, D_MODEL), beta * D_MODEL ** -0.5),
        "ffn_w_gu": normal(19, (n_attn, D_MODEL, 2 * D_FF), D_MODEL ** -0.5),
        "ffn_w_down": normal(20, (n_attn, D_FF, D_MODEL), beta * D_FF ** -0.5),
        "w_in_c": normal(21, (n_rec, D_MODEL, W_IN_C), D_MODEL ** -0.5),
        "b_gates_c": b_gates_c,
        "mlstm_norm_g": 1.0 + normal(22, (n_rec, D_MODEL), 0.02),
        "w_out_c": normal(23, (n_rec, D_MODEL, D_MODEL), beta * D_MODEL ** -0.5),
        "router_w": normal(24, (n_rec, D_MODEL, N_EXPERTS), D_MODEL ** -0.5),
        "router_b": normal(25, (n_rec, N_EXPERTS), 0.01),
        "moe_w_gu": normal(26, (n_rec, N_EXPERTS, D_MODEL, 2 * D_FF_EXPERT), D_MODEL ** -0.5),
        "moe_w_down": normal(27, (n_rec, N_EXPERTS, D_FF_EXPERT, D_MODEL), beta * D_FF_EXPERT ** -0.5),
    }

def reference(x_prompt, x_sample, c, cache_k, cache_v, state_C, state_n, state_m, c_ctx,
              ada_w, ada_b, ln_g, ln_b,
              w_in_a, diff_lambda, diff_norm_g, pool_w, pool_scale, w_out_a, ffn_w_gu, ffn_w_down,
              w_in_c, b_gates_c, mlstm_norm_g, w_out_c, router_w, router_b, moe_w_gu, moe_w_down):
    alpha = (2.0 * DEPTH) ** 0.25
    Bp = x_prompt.shape[0]
    xp, xs = x_prompt, x_sample
    zero_C = jnp.zeros((Bp, 2, MLSTM_HEADS, MLSTM_DH, MLSTM_DH), jnp.float32)
    zero_n = jnp.zeros((Bp, 2, MLSTM_HEADS, MLSTM_DH), jnp.float32)
    zero_m = jnp.zeros((Bp, 2, MLSTM_HEADS), jnp.float32)
    new_k, new_v, new_C, new_n, new_m = [], [], [], [], []
    for l in range(DEPTH):
        p_mod = _modulation(c_ctx, ada_w[l], ada_b[l])
        s_mod = _modulation(c[:, None, :], ada_w[l], ada_b[l])
        hp = _modulate(xp, p_mod[0], p_mod[1])
        hs = _modulate(xs, s_mod[0], s_mod[1])
        j = l // 2
        if l % 2 == 0:
            lam, lam_init = _diff_lambda(diff_lambda[j], l)
            args = (w_in_a[j], lam, lam_init, diff_norm_g[j], pool_w[j], pool_scale[j], w_out_a[j])
            out_p, k_ctx, v_ctx = _attn_pool_context(hp, *args)
            out_s = _attn_pool_latent(hs, cache_k[:, j], cache_v[:, j], *args)
            new_k.append(k_ctx)
            new_v.append(v_ctx)
        else:
            args = (w_in_c[j], b_gates_c[j], mlstm_norm_g[j], w_out_c[j])
            out_p, Cc, nc, mc = _mlstm_mixer(hp, *args, zero_C, zero_n, zero_m)
            out_s, _, _, _ = _mlstm_mixer(hs, *args, state_C[:, j], state_n[:, j], state_m[:, j])
            new_C.append(Cc)
            new_n.append(nc)
            new_m.append(mc)
        xp = _post_norm(xp, out_p, p_mod[2], ln_g[l, 0], ln_b[l, 0], alpha)
        xs = _post_norm(xs, out_s, s_mod[2], ln_g[l, 0], ln_b[l, 0], alpha)
        hp = _modulate(xp, p_mod[3], p_mod[4])
        hs = _modulate(xs, s_mod[3], s_mod[4])
        if l % 2 == 0:
            ff_p = _swiglu(hp, ffn_w_gu[j], ffn_w_down[j])
            ff_s = _swiglu(hs, ffn_w_gu[j], ffn_w_down[j])
        else:
            ff_p = _moe_swiglu(hp, router_w[j], router_b[j], moe_w_gu[j], moe_w_down[j])
            ff_s = _moe_swiglu(hs, router_w[j], router_b[j], moe_w_gu[j], moe_w_down[j])
        xp = _post_norm(xp, ff_p, p_mod[5], ln_g[l, 1], ln_b[l, 1], alpha)
        xs = _post_norm(xs, ff_s, s_mod[5], ln_g[l, 1], ln_b[l, 1], alpha)
    return (xp, xs, jnp.stack(new_k, axis=1), jnp.stack(new_v, axis=1),
            jnp.stack(new_C, axis=1), jnp.stack(new_n, axis=1), jnp.stack(new_m, axis=1))


_drawn_inputs = setup_inputs


def setup_inputs(seed=0):
    import zlib

    import numpy as np

    out = dict(_drawn_inputs(seed))
    spreads = {}
    factors = {'state_C': 4.453,
     'state_n': 7.092,
     'state_m': 6.631,
     'diff_lambda': 3.255,
     'diff_norm_g': 8.0,
     'pool_scale': 2.884,
     'mlstm_norm_g': 62.012,
     'router_b': 4.48}
    for name, (base, spread) in spreads.items():
        noise = np.random.default_rng([zlib.crc32(name.encode()), seed]).standard_normal(out[name].shape)
        drawn = base * np.exp(spread * noise) if base else spread * noise
        out[name] = __import__('jax').numpy.asarray(drawn.astype(out[name].dtype))
    for name, factor in factors.items():
        out[name] = (out[name] * factor).astype(out[name].dtype)
    return out
```

```python
import math
from contextlib import ExitStack

import numpy as np

import concourse.bass as bass
from concourse import mybir

D = 1024
KT = D // 128
T = 384
TT = T // 128
HA = 4
HM = 8
FF = 2816
FC = FF // 128
NE = 8
FE = 1792
MC = FE // 256
NBMAX = (2 * T + NE * 127) // 128
ALPHA = 4.0 ** 0.25
EPS = 1e-5
LAM_INIT = 0.8 - 0.6 * math.exp(0.0)
BIG_NEG = -1e30
WINDOWS = (2, 4, 8, 16)
NU = HA * TT
NM = HM * 2

RING = 6
UA = 6 * KT
U_ADA0 = 0
U_INA_T = U_ADA0 + UA
U_INA_N = U_INA_T + 8
U_OUTA = U_INA_N + KT
U_FFN = U_OUTA + KT
U_ADA1 = U_FFN + 3 * FC
U_INC_T = U_ADA1 + UA
U_INC_N = U_INC_T + 24
U_OUTC = U_INC_N + KT
U_MOE = U_OUTC + KT
UB = 6 * MC
assert UB % RING == 0

W_H = [0, 0, 0, 0]
W_INA = 8
W_H[1] = W_INA + 8
W_FFN = W_H[1] + 8
W_H[2] = W_FFN + 2 * FC
W_INC = W_H[2] + 8
W_H[3] = W_INC + 24
W_HN = W_H[3] + 8
W_END = W_HN + 6


def constants():
    p = np.arange(128)
    cols = {}
    cols["ident"] = np.eye(128)
    cols["ones"] = np.ones((128, 128))
    t = np.arange(256)
    axis, half, freq = (p // 32) % 2, (p // 16) % 2, p % 16
    inv = np.power(np.float32(10000.0), -np.arange(16, dtype=np.float32) / np.float32(16)).astype(np.float32)
    pos = np.where(axis[:, None] == 0, (t // 64)[None], (t % 64)[None]).astype(np.float32)
    ang = pos * inv[freq][:, None]
    cols["cos"] = np.cos(ang)
    cols["sin"] = np.sin(ang)
    rot = np.zeros((128, 128))
    for d in range(128):
        rot[d + 16 if half[d] == 0 else d - 16, d] = -1.0 if half[d] == 0 else 1.0
    cols["rot"] = rot
    s, q = p[:, None], p[None]
    cols["mask_f"] = np.where(s <= q, 0.0, BIG_NEG)
    cols["mask_b"] = np.where(s >= q, 0.0, BIG_NEG)
    cols["strict"] = (s < q)
    comb = np.zeros((128, 2))
    comb[[0, 1, 4], 0] = 1.0
    comb[[2, 3, 4], 1] = 1.0
    cols["comb"] = comb
    cols["sel"] = np.repeat(comb, 128, 1)
    cols["dir"] = np.stack([(p < 8), (p >= 8)], 1)
    cols["iota8"] = np.tile(np.arange(8), (128, 1))
    cols["iota16"] = np.tile(np.arange(16), (128, 1))
    cols["small"] = np.tile(np.array([EPS, 1.0, 0.0]), (128, 1))
    at, parts, n = {}, [], 0
    for k, v in cols.items():
        at[k] = (n, v.shape[1])
        parts.append(v.astype(np.float32))
        n += v.shape[1]

    def pool(n_tokens):
        m = np.zeros((4, n_tokens, n_tokens), np.float32)
        for g, w in enumerate(WINDOWS):
            for to in range(n_tokens):
                lo, hi = max(to - w // 2, 0), min(to + w // 2 - 1, n_tokens - 1)
                m[g, lo:hi + 1, to] = 1.0 / (hi - lo + 1)
                m[g, to, to] -= 1.0
        return m
    mp, ms = pool(128), pool(256)
    pm = np.zeros((128, 4, 640), np.float32)
    for g in range(4):
        pm[:, g, 0:128] = mp[g]
        pm[:, g, 128:384] = ms[g, 0:128]
        pm[:, g, 384:640] = ms[g, 128:256]
    return np.concatenate(parts, 1), at, pm.reshape(128, -1)


CONST, CAT, POOLM = constants()


class Chain:

    def __init__(self, eng, sem):
        self.eng, self.sem, self.base, self.n = eng, sem, 0, 0

    def step(self, ins):
        ins.then_inc(self.sem, 1)
        self.n += 1
        self.eng.wait_ge(self.sem, self.base + self.n)


def backbone_step(nc, a, out, scr):
    f32, f32r, i32, u32 = mybir.dt.float32, mybir.dt.float32r, mybir.dt.int32, mybir.dt.uint32
    ALU, ACT, AX = mybir.AluOpType, mybir.ActivationFunctionType, mybir.AxisListType
    ctx = ExitStack()
    with ctx:
        def sb(name, shape, dt=f32):
            return ctx.enter_context(nc.sbuf_tensor(name, shape, dt))

        def sem(name):
            return ctx.enter_context(nc.semaphore(name))

        raw = sb("raw", [128, RING, 1024])
        whi = sb("whi", [128, RING, 1024], f32r)
        wlo = sb("wlo", [128, RING, 1024], f32r)
        X = sb("X", [128, TT, D])
        Hh = sb("Hh", [128, KT, T], f32r)
        Hl = sb("Hl", [128, KT, T], f32r)
        gate_bc = sb("gate_bc", [128, 2, 2, D])
        cst = sb("cst", [128, CONST.shape[1]])
        modc = sb("modc", [128, 4, KT, 2])
        adaw = sb("adaw", [128, KT, 128], f32r)
        gu_h = sb("gu_h", [128, 2, T], f32r)
        gu_l = sb("gu_l", [128, 2, T], f32r)
        stats = sb("stats", [128, TT, 2, 6])
        mv = sb("mv", [128, TT, 2])
        rstd = sb("rstd", [128, TT])
        pcol = sb("pcol", [128, 13])
        psc, hgc, ngc = pcol[:, 0:4], pcol[:, 4:12], pcol[:, 12:13]
        rbb = sb("rbb", [128, NE])
        rwt = sb("rwt", [128, KT, NE])
        bgi = sb("bgi", [16, 1])
        bgf = sb("bgf", [16, 1])
        m0c = sb("m0c", [16, 1])
        lamc = sb("lamc", [128, 1])
        lams = sb("lams", [1, 4])
        att = sb("att", [128, 2, 12])
        ctl_f = sb("ctl_f", [1, 17])
        ctl = sb("ctl", [1, 17], i32)
        slot_u = sb("slot_u", [128, TT, 2], u32)
        wts = sb("wts", [128, TT, 2])
        idx_u = sb("idx_u", [128, TT, 8], u32)
        NBIG = 16800
        BIG = sb("BIG", [128, NBIG])

        def C(name, parts=128, lo=0, n=None):
            o, w = CAT[name]
            n = w - lo if n is None else n
            return cst[0:parts, o + lo:o + lo + n]

        top = [0]

        def area(shape, at=None):
            if at is not None:
                top[0] = at
            n = int(np.prod(shape[1:]))
            v = BIG[0:shape[0], top[0]:top[0] + n]
            top[0] += n
            assert top[0] <= NBIG, top[0]
            if len(shape) == 2:
                return v
            names = "abcd"[:len(shape) - 1]
            kw = {names[i]: shape[1 + i] for i in range(1, len(names))}
            return v.rearrange(f"p ({' '.join(names)}) -> p {' '.join(names)}", **kw)

        lng = area([128, D], 0)
        lnb = area([128, D])
        ltmp = area([128, D])
        H32 = area([128, KT, T], 3072)
        ftmp = area([128, 2, T], 6144)
        crow = area([29, 128], 14000)
        ccol = area([128, 16])
        arow = area([5, 2, D])
        lamr = area([1, 512])
        qT = area([128, HA, T], 0)
        kT = area([128, HA, T])
        Vn = area([128, TT, 512])
        Pn = area([128, TT, 512])
        kn = area([128, HA, 128])
        ck = area([128, HA, 128])
        cv = area([128, HA, 128])
        ckT = area([128, HA, 128])
        pw = area([128, 4, 128])
        pm = area([128, 4, 640])
        pr = area([128, 2, 2, T])
        aT = area([128, 2, T])
        oN = area([128, 2, 128])
        pT = area([128, T])
        o32 = area([128, 2, T])
        qM = area([128, HM, T], 0)
        kM = area([128, HM, T])
        sg = area([128, HM, T])
        V1 = area([128, TT, HM, 129])
        negM = area([16, T])
        nat = area([128, 8, 16])
        wint = area([16, 256])
        nfin = area([128, 16])
        Z = top[0]
        CN = area([128, 2, 129], Z)
        E = area([128, 2, 512])
        qw = area([128, 2, 256])
        hs = area([128, TT, 128])
        hn = area([128, TT, 128])
        ht = area([128, T])
        kw = area([128, 2, 128])
        Co = area([128, 2, 129])
        rd = area([128, 2, TT])
        hst = area([128, TT, 6])
        hmv = area([128, TT, 2])
        hrs = area([128, TT])
        g = [area([16, T], Z)] + [area([16, T]) for _ in range(5)]
        n0r = area([16, 128])
        gm = area([16, 8])
        wg = area([128, KT, 32])
        wgi = area([128, KT, 16])
        wgf = area([128, KT, 16])
        nfT = area([16, 128], Z)
        Hn = area([128, TT, D], 6144)
        lg = area([128, TT, NE])
        top8 = area([128, TT, 8])
        idxf = area([128, TT, 8])
        oh = area([128, 2, TT, NE])
        asum = area([128, TT, NE])
        rk = area([128, TT, NE])
        bb = area([128, 4, NE])
        wk = area([128, 2, TT, NE])
        slf = area([128, TT, 2])
        e2 = area([128, TT, 2])
        eid = area([1, 16, NE])
        zero = area([128, D], 0)
        hsn = area([128, D], 0)
        gp = area([128, 2, 512])
        yb = area([128, D])
        Yg = area([128, TT, 2, D], 3072)

        PS = ctx.enter_context(nc.psum_tensor("PS", [128, 8, 512], f32))

        raw_full = [sem(f"raw_full{r}") for r in range(RING)]
        hi_made = sem("hi_made")
        lo_made = sem("lo_made")
        unit_used = sem("unit_used")
        x_loaded = sem("x_loaded")
        cst_loaded = sem("cst_loaded")
        par_loaded = sem("par_loaded")
        att_loaded = sem("att_loaded")
        act_step = sem("act_step")
        dve_step = sem("dve_step")
        pool_step = sem("pool_step")
        zeroed = sem("zeroed")
        crow_t = sem("crow_t")
        crow_s = sem("crow_s")
        cc_made = sem("cc_made")
        adaw_zero = sem("adaw_zero")
        adaw_hi = sem("adaw_hi")
        adaw_lo = sem("adaw_lo")
        bias_in = [sem("bias_in0"), sem("bias_in1")]
        arow_made = sem("arow_made")
        ada_small = sem("ada_small")
        modc_made = sem("modc_made")
        gate_made = sem("gate_made")
        turned = sem("turned")
        hh_made = sem("hh_made")
        hl_made = sem("hl_made")
        free67 = [sem("free6"), sem("free7")]
        v_made = sem("v_made")
        p_made = sem("p_made")
        rot_made = sem("rot_made")
        roped = sem("roped")
        ck_turned = sem("ck_turned")
        ck_copied = sem("ck_copied")
        pool_a = sem("pool_a")
        pool_c = sem("pool_c")
        pool_b = sem("pool_b")
        pool_s = sem("pool_s")
        pool_hi = sem("pool_hi")
        pool_lo = sem("pool_lo")
        lam_part = sem("lam_part")
        lam_exp = sem("lam_exp")
        lam_row = sem("lam_row")
        lam_bc = sem("lam_bc")
        lam_made = sem("lam_made")
        s_made = sem("s_made")
        mx_made = sem("mx_made")
        ex_made = sem("ex_made")
        mix_made = sem("mix_made")
        at_turned = sem("at_turned")
        at_made = sem("at_made")
        o_made = sem("o_made")
        o_sq = sem("o_sq")
        o_norm = sem("o_norm")
        o_turned = sem("o_turned")
        o_hi = sem("o_hi")
        o_lo = sem("o_lo")
        cache_out = sem("cache_out")
        nat_read = sem("nat_read")
        var_made = sem("var_made")
        rstd_made = sem("rstd_made")
        normed = sem("normed")
        x_done = sem("x_done")
        ln_in = sem("ln_in")
        guh_made = sem("guh_made")
        gul_made = sem("gul_made")
        x_out = sem("x_out")

        def b67(w):
            return 6 + w % 2, free67[w % 2], w // 2

        def t_unit(w, col):
            return w[:, col:col + 128].rearrange("(k p) n -> p k n", p=128)

        def source(n):
            if n < U_INA_T or U_ADA1 <= n < U_INC_T:
                layer, i = (0, n - U_ADA0) if n < U_INA_T else (1, n - U_ADA1)
                gi, k = i // KT, i % KT
                return a["ada_w"][layer, 128 * k:128 * k + 128, D * gi:D * gi + D]
            if n < U_INA_N:
                return t_unit(a["w_in_a"][0], 128 * (n - U_INA_T))
            if n < U_OUTA:
                k = n - U_INA_N
                return a["w_in_a"][0, 128 * k:128 * k + 128, D:2 * D]
            if n < U_FFN:
                k = n - U_OUTA
                return a["w_out_a"][0, 128 * k:128 * k + 128, :]
            if n < U_ADA1:
                kind, c = FFN_ORDER[n - U_FFN]
                if kind == "d":
                    return a["ffn_w_down"][0, 128 * c:128 * c + 128, :]
                return t_unit(a["ffn_w_gu"][0], 128 * c + (FF if kind == "u" else 0))
            if n < U_INC_N:
                m = n - U_INC_T
                return t_unit(a["w_in_c"][0], 128 * m + (D if m >= 16 else 0))
            if n < U_OUTC:
                k = n - U_INC_N
                return a["w_in_c"][0, 128 * k:128 * k + 128, 2 * D:3 * D]
            k = n - U_OUTC
            return a["w_out_c"][0, 128 * k:128 * k + 128, :]

        FFN_ORDER = [("g", 0), ("u", 0)]
        for c in range(1, FC):
            FFN_ORDER += [("g", c), ("u", c), ("d", c - 1)]
        FFN_ORDER += [("d", FC - 1)]
        FFN_AT = {x: U_FFN + i for i, x in enumerate(FFN_ORDER)}

        def stream(sp, first, last):
            for n in range(first, last):
                if n >= RING:
                    sp.wait_ge(lo_made, n - RING + 1)
                src = source(n)
                dst = raw[:, n % RING, :]
                if len(src.shape) == 3:
                    dst = dst.rearrange("p (k n) -> p k n", k=KT)
                sp.dma_start(dst, src).then_inc(raw_full[n % RING], 16)

        class Splits:
            def __init__(self, eng, upper):
                self.eng, self.upper, self.n = eng, upper, 0

            def upto(self, last):
                while self.n <= min(last, U_MOE - 1):
                    n, s = self.n, self.n % RING
                    if self.upper:
                        if n >= RING:
                            self.eng.wait_ge(unit_used, n - RING + 1)
                        self.eng.wait_ge(raw_full[s], 16 * (n // RING + 1))
                        self.eng.activation(whi[:, s, :], raw[:, s, :], ACT.Copy).then_inc(hi_made, 1)
                    else:
                        self.eng.wait_ge(hi_made, n + 1)
                        self.eng.tensor_tensor(wlo[:, s, :], raw[:, s, :], whi[:, s, :].bitcast(f32),
                                               ALU.subtract).then_inc(lo_made, 1)
                    self.n += 1

        def t_product(pe, n, w):
            b, freed, before = b67(w)
            s = n % RING
            if before:
                pe.wait_ge(freed, before)
            pe.wait_ge(lo_made, n + 1)
            for k in range(KT):
                wh, wl = whi[:, s, 128 * k:128 * k + 128], wlo[:, s, 128 * k:128 * k + 128]
                pe.matmul(PS[:, b, 0:T], wh, Hh[:, k, :], start=(k == 0), stop=False)
                pe.matmul(PS[:, b, 0:T], wh, Hl[:, k, :], start=False, stop=False)
                last = pe.matmul(PS[:, b, 0:T], wl, Hh[:, k, :], start=False, stop=(k == KT - 1))
            last.then_inc(unit_used, 1)

        def n_product(pe, n, sh, sl, first, final):
            s = n % RING
            pe.wait_ge(lo_made, n + 1)
            for t in range(TT):
                h, l = sh[:, 128 * t:128 * t + 128], sl[:, 128 * t:128 * t + 128]
                for lhs, w in ((h, whi), (h, wlo), (l, whi)):
                    for half in range(2):
                        last = pe.matmul(PS[:, 2 * t + half, :], lhs, w[:, s, 512 * half:512 * half + 512],
                                         start=(first and lhs is h and w is whi), stop=(final and lhs is l))
            last.then_inc(unit_used, 1)

        def pe_ada_vectors(pe):
            pe.wait_ge(crow_s, 1)
            pe.wait_ge(cst_loaded, 96)
            pe.transpose(PS[:, 4, 0:29], crow, C("ident", 29, 0, 29)).then_inc(crow_t, 1)

        def pe_ada(pe, layer):
            base = (U_ADA0, U_ADA1)[layer]

            def spread(gi):
                i = 6 * layer + gi
                pe.wait_ge(arow_made, i + 1)
                pe.wait_ge(bias_in[i % 2], 16 * (i // 2 + 1))
                cols = 4 * layer + (0, 1, 2, 2, 3, 4)[gi]
                gates = 2 * layer + (0, 0, 0, 1, 1, 1)[gi]
                if cols:
                    pe.wait_ge(modc_made, cols)
                if gates:
                    pe.wait_ge(gate_made, 2 * gates)
                if gi % 3 < 2:
                    for c in range(KT):
                        last = pe.matmul(PS[:, 4, 2 * c:2 * c + 2], arow[:, gi % 2, 128 * c:128 * c + 128],
                                         C("comb", 5), start=True, stop=True)
                else:
                    for grp in range(2):
                        for half in range(2):
                            last = pe.matmul(PS[:, 4 + 2 * grp + half, :], C("sel", 5, 128 * grp, 128),
                                             arow[:, gi % 2, 512 * half:512 * half + 512], start=True, stop=True)
                last.then_inc(ada_small, 1)

            for gi in range(6):
                for k in range(KT):
                    n = base + KT * gi + k
                    if k == 0 and 6 * layer + gi >= 2:
                        pe.wait_ge(arow_made, 6 * layer + gi - 1)
                    pe.wait_ge(lo_made, n + 1)
                    for w in (whi, wlo):
                        for half in range(2):
                            last = pe.matmul(PS[:, 2 * (gi % 2) + half, :], adaw[:, k, :],
                                             w[:, n % RING, 512 * half:512 * half + 512],
                                             start=(k == 0 and w is whi), stop=(k == KT - 1 and w is wlo))
                    last.then_inc(unit_used, 1)
                if gi:
                    spread(gi - 1)
            spread(5)

        def act_ada(act, sp_, layer):
            base = (U_ADA0, U_ADA1)[layer]

            def gates(gi):
                if gi % 3 == 2:
                    act.wait_ge(ada_small, 6 * layer + gi + 1)
                    for grp in range(2):
                        act.activation(gate_bc[:, gi // 3, grp, :].rearrange("p (a n) -> p a n", a=2),
                                       PS[:, 4 + 2 * grp:6 + 2 * grp, :], ACT.Copy).then_inc(gate_made, 1)
            for gi in range(6):
                sp_.upto(base + KT * gi + KT - 1)
                act.wait_ge(unit_used, base + KT * gi + KT)
                if 6 * layer + gi >= 2:
                    act.wait_ge(ada_small, 6 * layer + gi - 1)
                act.activation(arow[0:4, gi % 2, :].rearrange("p (a n) -> p a n", a=2),
                               PS[0:4, 2 * (gi % 2):2 * (gi % 2) + 2, :], ACT.Copy).then_inc(arow_made, 1)
                if gi:
                    gates(gi - 1)
            gates(5)

        def dve_ada(dve, sp_, layer):
            base = (U_ADA0, U_ADA1)[layer]

            def cols(gi):
                if gi % 3 < 2:
                    dve.wait_ge(ada_small, 6 * layer + gi + 1)
                    dve.tensor_scalar(modc[:, 2 * (gi // 3) + gi % 3, :, :].rearrange("p k g -> p (k g)"),
                                      PS[:, 4, 0:16], float(gi % 3), None, ALU.add).then_inc(modc_made, 1)
            for gi in range(6):
                sp_.upto(base + KT * gi + KT - 1)
                if gi:
                    cols(gi - 1)
            cols(5)

        def pool_ada(pool, layer):
            for gi in range(6):
                i = 6 * layer + gi
                if i >= 2:
                    pool.wait_ge(ada_small, i - 1)
                pool.dma_start(arow[4:5, gi % 2, :], a["ada_b"][layer:layer + 1, D * gi:D * gi + D]
                               ).then_inc(bias_in[i % 2], 16)

        def pe_turn(pe, st):
            if st == 0:
                pe.wait_ge(x_loaded, 48)
            pe.wait_ge(gate_made, 4 * (st // 2 + 1))
            for i in range(KT):
                b, freed, before = b67(W_H[st] + i)
                if before:
                    pe.wait_ge(freed, before)
                for t in range(TT):
                    if st and i == 0:
                        pe.wait_ge(x_done, TT * (st - 1) + t + 1)
                    last = pe.transpose(PS[:, b, 128 * t:128 * t + 128], X[:, t, 128 * i:128 * i + 128], C("ident"))
                last.then_inc(turned, 1)

        def act_turn(act, ch, sp_, st, first):
            sub = st % 2
            act.wait_ge(modc_made, 4 * (st // 2) + 4)
            for i in range(KT):
                b, freed, _ = b67(W_H[st] + i)
                act.wait_ge(turned, KT * st + i + 1)
                if st and i == 0:
                    act.wait_ge(hl_made, KT * st)
                act.activation(H32[:, i, 0:128], PS[:, b, 0:128], ACT.Identity,
                               bias=modc[:, 2 * sub, i, 1:2], scale=modc[:, 2 * sub + 1, i, 1:2])
                act.activation(H32[:, i, 128:T], PS[:, b, 128:T], ACT.Identity, bias=modc[:, 2 * sub, i, 0:1],
                               scale=modc[:, 2 * sub + 1, i, 0:1]).then_inc(freed, 1)
                act.wait_ge(freed, (W_H[st] + i) // 2 + 1)
                act.activation(Hh[:, i, :], H32[:, i, :], ACT.Copy).then_inc(hh_made, 1)
            sp_.upto(first + RING - 1)

        def dve_turn(dve, sp_, st, first):
            for i in range(KT):
                dve.wait_ge(hh_made, KT * st + i + 1)
                dve.tensor_tensor(Hl[:, i, :], H32[:, i, :], Hh[:, i, :].bitcast(f32),
                                  ALU.subtract).then_inc(hl_made, 1)
            sp_.upto(first + RING - 1)

        def dve_norm(dve, ch, st, ready, from_=None):
            sub = st % 2
            for t in range(TT):
                if t == 0:
                    ready()
                grp = 1 if t == 0 else 0
                lt = ltmp.rearrange("p (a n) -> p a n", a=2)
                src = PS[:, 2 * t:2 * t + 2, :] if from_ is None else from_(t)
                dve.tensor_tensor(lt, src, gate_bc[:, sub, grp, :].rearrange("p (a n) -> p a n", a=2),
                                  ALU.mult).then_inc(nat_read, 1)
                dve.wait_ge(nat_read, TT * st + t + 1)
                ch.step(dve.scalar_tensor_tensor(X[:, t, :], X[:, t, :], ALPHA, ltmp, ALU.mult, ALU.add))
                for half in range(2):
                    last = dve.bn_stats(stats[:, t, half, :], X[:, t, 512 * half:512 * half + 512])
                ch.step(last)
                dve.bn_aggr(mv[:, t, :], stats[:, t, :, :].rearrange("p a b -> p (a b)")).then_inc(var_made, 1)
                dve.wait_ge(rstd_made, TT * st + t + 1)
                dve.tensor_scalar(X[:, t, :], X[:, t, :], mv[:, t, 0:1], rstd[:, t:t + 1],
                                  ALU.subtract, ALU.mult).then_inc(normed, 1)

        def act_norm(act, ch, st):
            for t in range(TT):
                act.wait_ge(var_made, TT * st + t + 1)
                ch.step(act.activation(rstd[:, t:t + 1], mv[:, t, 1:2], ACT.Ln, bias=C("small", 128, 0, 1)))
                act.activation(rstd[:, t:t + 1], rstd[:, t:t + 1], ACT.Exp, scale=-0.5).then_inc(rstd_made, 1)

        def pool_norm_load(pool, st):
            if st:
                pool.wait_ge(x_done, TT * st)
            for i, (dst, name) in enumerate(((lng, "ln_g"), (lnb, "ln_b"))):
                pool.dma_start(dst, a[name][st // 2, st % 2:st % 2 + 1, :].to_broadcast([128, D])
                               ).then_inc(ln_in, 16)

        def pool_norm(pool, ch, st):
            pool.wait_ge(ln_in, 32 * (st + 1))
            for t in range(TT):
                pool.wait_ge(normed, TT * st + t + 1)
                ch.step(pool.tensor_tensor(X[:, t, :], X[:, t, :], lng, ALU.mult))
                pool.tensor_tensor(X[:, t, :], X[:, t, :], lnb, ALU.add).then_inc(x_done, 1)

        def pe_mixer0(pe):
            for m in range(8):
                if m == 0:
                    pe.wait_ge(hl_made, KT)
                t_product(pe, U_INA_T + m, W_INA + m)
            for k in range(KT):
                n_product(pe, U_INA_N + k, Hh[:, k, :], Hl[:, k, :], k == 0, k == KT - 1)
            pe.wait_ge(free67[0], (W_INA + 8) // 2)
            pe.wait_ge(free67[1], (W_INA + 8) // 2)
            pe.wait_ge(v_made, TT)
            pe.wait_ge(p_made, TT)
            for h in range(HA):
                pe.matmul(PS[:, h, 0:256], C("rot"), qT[:, h, 128:T], start=True, stop=True)
                pe.matmul(PS[:, h, 256:512], C("rot"), kT[:, h, 128:T], start=True, stop=True).then_inc(rot_made, 1)
            pe.wait_ge(att_loaded, 64)
            for h in range(HA):
                last = pe.transpose(PS[:, 4, 128 * h:128 * h + 128], ck[:, h, :], C("ident"))
            last.then_inc(ck_turned, 1)
            for h in range(HA):
                last = pe.transpose(PS[:, 5, 128 * h:128 * h + 128], kT[:, h, 0:128], C("ident"))
            last.then_inc(ck_turned, 1)
            for g_ in range(5):
                if g_ < 4:
                    b = 6 + g_ % 2
                    if g_ >= 2:
                        pe.wait_ge(pool_c, g_ - 1)
                    u = Pn[:, :, 128 * g_:128 * g_ + 128]
                    pe.matmul(PS[:, b, 0:128], u[:, 0, :], pm[:, g_, 0:128], start=True, stop=True)
                    pe.matmul(PS[:, b, 128:T], u[:, 1, :], pm[:, g_, 128:384], start=True, stop=False)
                    pe.matmul(PS[:, b, 128:T], u[:, 2, :], pm[:, g_, 384:640], start=False, stop=True
                              ).then_inc(pool_a, 1)
                if g_ >= 1:
                    pe.wait_ge(pool_c, g_)
                    if g_ == 1:
                        pe.wait_ge(ck_copied, 1)
                    if g_ >= 2:
                        pe.wait_ge(pool_s, g_ - 1)
                    pe.matmul(PS[:, 4, 0:T], pw[:, g_ - 1, :], pT, start=True, stop=True).then_inc(pool_b, 1)
            for i in range(NU + 3):
                if i < NU:
                    h, qt, r = i // TT, i % TT, i % 2
                    if i == 0:
                        pe.wait_ge(roped, HA)
                        pe.wait_ge(ck_copied, 2)
                    if i >= 2:
                        pe.wait_ge(ex_made, 2 * (i - 1))
                    for j in range(2):
                        lhs = qT[64 * j:64 * j + 64, h, 128 * qt:128 * qt + 128]
                        dst = PS[:, 2 * r + j, :]
                        if qt == 0:
                            last = pe.matmul(dst[:, 0:128], lhs, kT[64 * j:64 * j + 64, h, 0:128], start=True, stop=True)
                        else:
                            pe.matmul(dst[:, 0:128], lhs, ckT[64 * j:64 * j + 64, h, :], start=True, stop=True)
                            last = pe.matmul(dst[:, 128:T], lhs, kT[64 * j:64 * j + 64, h, 128:T], start=True, stop=True)
                    last.then_inc(s_made, 1)
                if 0 <= i - 1 < NU:
                    u = i - 1
                    pe.wait_ge(mix_made, u + 1)
                    if u < 2:
                        pe.wait_ge(pool_s, 4)
                    else:
                        pe.wait_ge(at_made, u - 1)
                    for kt in range(1 if u % TT == 0 else TT):
                        last = pe.transpose(PS[:, 4 + u % 2, 128 * kt:128 * kt + 128],
                                            pr[:, u % 2, 0, 128 * kt:128 * kt + 128], C("ident"))
                    last.then_inc(at_turned, 1)
                if 0 <= i - 2 < NU:
                    u = i - 2
                    h, qt = u // TT, u % TT
                    pe.wait_ge(at_made, u + 1)
                    if u == 0:
                        pe.wait_ge(pool_c, 4)
                    else:
                        pe.wait_ge(o_norm, u)
                    dst = PS[:, 6, 0:128]
                    if qt == 0:
                        last = pe.matmul(dst, aT[:, u % 2, 0:128], Vn[:, 0, 128 * h:128 * h + 128], start=True, stop=True)
                    else:
                        pe.matmul(dst, aT[:, u % 2, 0:128], cv[:, h, :], start=True, stop=False)
                        for kt in range(1, TT):
                            last = pe.matmul(dst, aT[:, u % 2, 128 * kt:128 * kt + 128],
                                             Vn[:, kt, 128 * h:128 * h + 128], start=False, stop=(kt == TT - 1))
                    last.then_inc(o_made, 1)
                if 0 <= i - 3 < NU:
                    u = i - 3
                    pe.wait_ge(o_norm, u + 1)
                    if u >= 1:
                        pe.wait_ge(o_hi, u)
                    pe.transpose(PS[:, 7, 0:128], oN[:, u % 2, :], C("ident")
                                 ).then_inc(o_turned, 1)

        def act_mixer0(act, ch, sp_):
            for m in range(8):
                act.wait_ge(unit_used, U_INA_T + m + 1)
                if m == 0:
                    act.wait_ge(zeroed, 16 * (NBMAX + 1))
                b, freed, _ = b67(W_INA + m)
                act.activation((qT if m < 4 else kT)[:, m % 4, :], PS[:, b, 0:T], ACT.Copy).then_inc(freed, 1)
                sp_.upto(U_INA_T + m + RING)
            sp_.upto(U_OUTA - 1)
            act.wait_ge(unit_used, U_OUTA)
            for t in range(TT):
                act.activation(Vn[:, t, :], PS[:, 2 * t, :], ACT.Copy).then_inc(v_made, 1)
            sp_.upto(U_OUTA + RING - 1)
            act.wait_ge(ck_turned, 1)
            act.activation(ckT.rearrange("p h n -> p (h n)"), PS[:, 4, :], ACT.Copy).then_inc(ck_copied, 1)
            act.wait_ge(ck_turned, 2)
            act.activation(kn.rearrange("p h n -> p (h n)"), PS[:, 5, :], ACT.Copy).then_inc(ck_copied, 1)
            for g_ in range(5):
                if g_ < 4:
                    act.wait_ge(pool_a, g_ + 1)
                    if g_:
                        act.wait_ge(pool_b, g_)
                    act.activation(pT, PS[:, 6 + g_ % 2, 0:T], ACT.Copy).then_inc(pool_c, 1)
                if g_:
                    act.wait_ge(pool_s, g_)
                    act.activation(Hh[:, 3 + g_, :], o32[:, (g_ - 1) % 2, :], ACT.Copy).then_inc(pool_hi, 1)
            for i in range(NU + 3):
                if i < NU:
                    r, nk = i % 2, (128 if i % TT == 0 else T)
                    act.wait_ge(mx_made, i + 1)
                    if i >= 2:
                        act.wait_ge(at_turned, i - 1)
                    for j in range(2):
                        act.activation(pr[:, r, j, 0:nk], PS[:, 2 * r + j, 0:nk], ACT.Exp, scale=0.125,
                                       bias=att[:, r, 2 + j:3 + j], accum_out=att[:, r, 4 + j:5 + j]).then_inc(ex_made, 1)
                if 0 <= i - 1 < NU:
                    u = i - 1
                    nk = 128 if u % TT == 0 else T
                    act.wait_ge(at_turned, u + 1)
                    if u >= 2:
                        act.wait_ge(o_made, u - 1)
                    act.activation(aT[:, u % 2, 0:nk], PS[:, 4 + u % 2, 0:nk], ACT.Copy).then_inc(at_made, 1)
                if 0 <= i - 2 < NU:
                    u = i - 2
                    r = u % 2
                    act.wait_ge(o_made, u + 1)
                    if u >= 2:
                        act.wait_ge(o_turned, u - 1)
                    ch.step(act.activation(oN[:, r, :], PS[:, 6, 0:128], ACT.Square,
                                           accum_out=att[:, r, 8:9]))
                    ch.step(act.activation(att[:, r, 9:10], att[:, r, 8:9], ACT.Ln, scale=1.0 / 128,
                                           bias=C("small", 128, 0, 1)))
                    act.activation(att[:, r, 10:11], att[:, r, 9:10], ACT.Exp, scale=-0.5).then_inc(o_sq, 1)
                if 0 <= i - 3 < NU:
                    u = i - 3
                    h, qt, r = u // TT, u % TT, u % 2
                    act.wait_ge(o_turned, u + 1)
                    if u >= 2:
                        act.wait_ge(o_lo, u - 1)
                    else:
                        act.wait_ge(pool_lo, 4)
                    ch.step(act.activation(o32[:, r, 0:128], PS[:, 7, 0:128], ACT.Identity,
                                           scale=ngc[:, 0:1], bias=C("small", 128, 2, 1)))
                    act.activation(Hh[:, h, 128 * qt:128 * qt + 128], o32[:, r, 0:128], ACT.Copy).then_inc(o_hi, 1)

        def dve_mixer0(dve, ch, sp_):
            for m in range(8):
                sp_.upto(U_INA_T + m + RING)
            sp_.upto(U_OUTA - 1)
            dve.wait_ge(unit_used, U_OUTA)
            for t in range(TT):
                dve.tensor_copy(Pn[:, t, :], PS[:, 2 * t + 1, :]).then_inc(p_made, 1)
            sp_.upto(U_OUTA + RING - 1)
            qk = BIG[:, 0:2 * HA * T].rearrange("p (s h n) -> p s h n", s=2, h=HA)
            tmp = pr.rearrange("p a b n -> p (a b n)")[:, 0:512].rearrange("p (s n) -> p s n", s=2)
            for h in range(HA):
                dve.wait_ge(rot_made, h + 1)
                x = qk[:, :, h, 128:T]
                dve.tensor_tensor(tmp, PS[:, h, :].rearrange("p (s n) -> p s n", s=2),
                                  C("sin").unsqueeze(1).to_broadcast([128, 2, 256]), ALU.mult)
                ch.step(dve.tensor_tensor(x, x, C("cos").unsqueeze(1).to_broadcast([128, 2, 256]), ALU.mult))
                dve.tensor_tensor(x, x, tmp, ALU.add).then_inc(roped, 1)
                dve.wait_ge(roped, h + 1)
            for g_ in range(4):
                dve.wait_ge(pool_b, g_ + 1)
                dve.tensor_scalar(o32[:, g_ % 2, :], PS[:, 4, 0:T], psc[:, g_:g_ + 1], None,
                                  ALU.mult).then_inc(pool_s, 1)
                dve.wait_ge(pool_hi, g_ + 1)
                dve.tensor_tensor(Hl[:, 4 + g_, :], o32[:, g_ % 2, :], Hh[:, 4 + g_, :].bitcast(f32),
                                  ALU.subtract).then_inc(pool_lo, 1)
            for i in range(NU + 3):
                if i < NU:
                    r, nk = i % 2, (128 if i % TT == 0 else T)
                    dve.wait_ge(s_made, i + 1)
                    ch.step(dve.tensor_reduce(att[:, r, 0:2], PS[:, 2 * r:2 * r + 2, 0:nk], AX.X, ALU.max))
                    dve.tensor_scalar(att[:, r, 2:4], att[:, r, 0:2], -0.125, None, ALU.mult).then_inc(mx_made, 1)
                    dve.wait_ge(ex_made, 2 * i + 2)
                    ch.step(dve.reciprocal(att[:, r, 6:8], att[:, r, 4:6]))
                    ch.step(dve.tensor_scalar(att[:, r, 7:8], att[:, r, 7:8], lamc[:, 0:1], None, ALU.mult))
                    ch.step(dve.tensor_scalar(pr[:, r, 0, 0:nk], pr[:, r, 0, 0:nk], att[:, r, 6:7], None, ALU.mult))
                    dve.scalar_tensor_tensor(pr[:, r, 0, 0:nk], pr[:, r, 1, 0:nk], att[:, r, 7:8],
                                             pr[:, r, 0, 0:nk], ALU.mult, ALU.add).then_inc(mix_made, 1)
                if 0 <= i - 2 < NU:
                    u = i - 2
                    r = u % 2
                    dve.wait_ge(o_sq, u + 1)
                    dve.tensor_scalar(oN[:, r, :], PS[:, 6, 0:128], att[:, r, 10:11], None,
                                      ALU.mult).then_inc(o_norm, 1)
                if 0 <= i - 3 < NU:
                    u = i - 3
                    h, qt, r = u // TT, u % TT, u % 2
                    dve.wait_ge(o_hi, u + 1)
                    dve.tensor_tensor(Hl[:, h, 128 * qt:128 * qt + 128], o32[:, r, 0:128],
                                      Hh[:, h, 128 * qt:128 * qt + 128].bitcast(f32), ALU.subtract).then_inc(o_lo, 1)

        def pe_out(pe, first):
            for k in range(KT):
                n_product(pe, first + k, Hh[:, k, :], Hl[:, k, :], k == 0, k == KT - 1)

        def pe_ffn(pe):
            pe.wait_ge(hl_made, 2 * KT)
            for kind, c in FFN_ORDER:
                n = FFN_AT[kind, c]
                if kind == "d":
                    if c == 0:
                        pe.wait_ge(x_done, TT)
                    pe.wait_ge(gul_made, c + 1)
                    n_product(pe, n, gu_h[:, c % 2, :], gu_l[:, c % 2, :], c == 0, c == FC - 1)
                else:
                    t_product(pe, n, W_FFN + 2 * c + (kind == "u"))

        def act_ffn(act, ch, sp_):
            for c in range(FC):
                act.wait_ge(unit_used, FFN_AT["g", c] + 1)
                if c >= 2:
                    act.wait_ge(guh_made, c - 1)
                    act.wait_ge(gul_made, c - 1)
                b, freed, _ = b67(W_FFN + 2 * c)
                act.activation(ftmp[:, c % 2, :], PS[:, b, 0:T], ACT.Silu).then_inc(freed, 1)
                sp_.upto(FFN_AT["g", c] + RING)
                act.wait_ge(free67[1], (W_FFN + 2 * c + 1) // 2 + 1)
                act.activation(gu_h[:, c % 2, :], ftmp[:, c % 2, :], ACT.Copy).then_inc(guh_made, 1)
                sp_.upto(FFN_AT["u", c] + RING)
            sp_.upto(FFN_AT["d", FC - 1] + RING)

        def dve_ffn(dve, ch, sp_):
            for c in range(FC):
                sp_.upto(FFN_AT["g", c] + RING)
                dve.wait_ge(unit_used, FFN_AT["u", c] + 1)
                dve.wait_ge(free67[0], (W_FFN + 2 * c) // 2 + 1)
                b, freed, _ = b67(W_FFN + 2 * c + 1)
                dve.tensor_tensor(ftmp[:, c % 2, :], ftmp[:, c % 2, :], PS[:, b, 0:T], ALU.mult).then_inc(freed, 1)
                dve.wait_ge(freed, (W_FFN + 2 * c + 1) // 2 + 1)
                dve.wait_ge(guh_made, c + 1)
                dve.tensor_tensor(gu_l[:, c % 2, :], ftmp[:, c % 2, :], gu_h[:, c % 2, :].bitcast(f32),
                                  ALU.subtract).then_inc(gul_made, 1)
                sp_.upto(FFN_AT["u", c] + RING)
            sp_.upto(FFN_AT["d", FC - 1] + RING)

        gates_mm = sem("gates_mm")
        wg_in = sem("wg_in")
        wg_cut = sem("wg_cut")
        n0_in = sem("n0_in")
        ones_set = sem("ones_set")
        gi_made = sem("gi_made")
        nab_made = sem("nab_made")
        soft_made = sem("soft_made")
        rows_made = sem("rows_made")
        rows_exp = sem("rows_exp")
        nat_turned = sem("nat_turned")
        nat_copied = sem("nat_copied")
        v1_act = sem("v1_act")
        v1_dve = sem("v1_dve")
        m_out = sem("m_out")
        st_made = sem("st_made")
        d_made = sem("d_made")
        wb_made = sem("wb_made")
        e_made = sem("e_made")
        qw_made = sem("qw_made")
        p_done = sem("p_done")
        km_turned = sem("km_turned")
        kw_made = sem("kw_made")
        cn_in = [sem("cn_in0"), sem("cn_in1")]
        cn_col = sem("cn_col")
        num_made = sem("num_made")
        rd_done = sem("rd_done")
        c_made = sem("c_made")
        co_made = sem("co_made")
        c_out = [sem("c_out0"), sem("c_out1")]
        hvar = sem("hvar")
        hrstd = sem("hrstd")
        hn_made = sem("hn_made")
        ht_turned = sem("ht_turned")
        ht_made = sem("ht_made")
        mh_hi = sem("mh_hi")
        mh_lo = sem("mh_lo")
        nf_turned = sem("nf_turned")
        nf_made = sem("nf_made")
        SCL = 128.0 ** -0.5
        KEYS = {0: ((0, 0, 128), (1, 128, 384), (2, 384, 512)), 1: ((0, 0, 128), (1, 128, 256), (2, 256, 512))}

        def unit(u):
            h, d = u // 2, u % 2
            return h, d, 8 * d + h

        def pe_mixer1(pe):
            pe.wait_ge(hh_made, 3 * KT)
            pe.wait_ge(wg_cut, 2)
            for dst, w in ((4, wgi), (5, wgf)):
                for k in range(KT):
                    last = pe.matmul(PS[0:16, dst, 0:T], w[:, k, :], H32[:, k, :], start=(k == 0), stop=(k == KT - 1))
            last.then_inc(gates_mm, 1)
            for m in range(24):
                if m == 0:
                    pe.wait_ge(hl_made, 3 * KT)
                t_product(pe, U_INC_T + m, W_INC + m)
            pe.wait_ge(rows_exp, 3)
            pe.wait_ge(n0_in, 16)
            rows = [(g[0], t) for t in range(TT)] + [(g[4], t) for t in range(TT)] + [(g[5], 0), (n0r, 0)]
            for i, (x, t) in enumerate(rows):
                last = pe.transpose(PS[:, 3, 16 * i:16 * i + 16], x[:, 128 * t:128 * t + 128], C("ident", 16, 0, 16))
            last.then_inc(nat_turned, 1)
            pe.wait_ge(nat_copied, 1)
            for k in range(KT):
                n_product(pe, U_INC_N + k, Hh[:, k, :], Hl[:, k, :], k == 0, k == KT - 1)
            for i in range(NM + 3):
                if i < NM:
                    h, d, r = unit(i)
                    if d == 0:
                        if i == 0:
                            for b in range(2):
                                pe.wait_ge(free67[b], (W_INC + 24) // 2)
                            pe.wait_ge(v1_act, TT)
                            pe.wait_ge(v1_dve, TT)
                            pe.wait_ge(ones_set, 1)
                        else:
                            pe.wait_ge(p_done, i)
                        pe.matmul(PS[:, 0, 0:128], kM[:, h, 0:128], qM[:, h, 0:128], start=True, stop=True)
                        pe.matmul(PS[:, 0, 128:T], kM[:, h, 128:256], qM[:, h, 128:T], start=True, stop=True)
                        pe.matmul(PS[:, 1, 0:256], kM[:, h, 256:T], qM[:, h, 128:T], start=True, stop=True
                                  ).then_inc(st_made, 1)
                    if i >= 2:
                        pe.wait_ge(e_made, i - 1)
                    row = C("ident", 16, r, 1).to_broadcast([16, 128])
                    b = 2 + i % 2
                    spans = ((0, 384, 0), (384, 512, 256)) if d == 0 else ((0, 256, 0), (256, 512, 128))
                    for lo, hi, tok in spans:
                        pe.matmul(PS[:, b, lo:hi], row, negM[:, tok:tok + hi - lo], start=(lo == 0), stop=False,
                                  skip_group_check=True)
                    for lo in (0, 128, 384):
                        last = pe.matmul(PS[:, b, lo:lo + 128], C("ident"), C("mask_f" if d == 0 else "mask_b"),
                                         start=False, stop=(lo == 384), skip_group_check=True)
                    last.then_inc(d_made, 1)
                    if i >= 1:
                        pe.wait_ge(qw_made, i)
                    pe.matmul(PS[:, 6, 0:256], row, wint, start=True, stop=True).then_inc(wb_made, 1)
                if 0 <= i - 1 < NM:
                    u = i - 1
                    h, d, r = unit(u)
                    pe.wait_ge(p_done, u + 1)
                    pe.wait_ge(cn_in[d], 16 * (h + 1))
                    pe.wait_ge(cn_col, u + 1)
                    if u >= 2:
                        pe.wait_ge(rd_done, u - 1)
                    P_ = E[:, u % 2, :]
                    b = 4 + u % 2
                    spans = (((0, 0, 0),), ((128, 1, 0),), ((256, 1, 1), (384, 2, 1))) if d == 0 else \
                        (((0, 0, 0),), ((128, 1, 0), (256, 2, 0)), ((384, 2, 1),))
                    for t in range(TT):
                        dst = PS[:, b, 129 * t:129 * t + 129]
                        for j, (col, key, _) in enumerate(spans[t]):
                            last = pe.matmul(dst, P_[:, col:col + 128], V1[:, key, h, :], start=(j == 0),
                                             stop=(t == 0))
                        if t:
                            last = pe.matmul(dst, qw[:, d, 128 * (t - 1):128 * t], CN[:, d, :], start=False, stop=True)
                    last.then_inc(num_made, 1)
                    pe.wait_ge(kw_made, h + 1)
                    if u % 2 == 1:
                        pe.wait_ge(co_made, u)
                    if u % 2 == 1 and h >= 1:
                        pe.wait_ge(ht_made, h)
                    pe.matmul(PS[:, 7, 0:129], kw[:, d, :], V1[:, 0, h, :], start=True, stop=True).then_inc(c_made, 1)
                if i < NM and i % 2 == 0:
                    h = i // 2
                    if h:
                        pe.wait_ge(co_made, 2 * h)
                    pe.transpose(PS[:, 7, 0:128], kM[:, h, 0:128], C("ident")).then_inc(km_turned, 1)
                if i >= 3 and i % 2 == 1:
                    h = (i - 3) // 2
                    pe.wait_ge(hn_made, h + 1)
                    pe.wait_ge(co_made, min(i, NM))
                    for t in range(TT):
                        last = pe.transpose(PS[:, 7, 128 * t:128 * t + 128], hn[:, t, :], C("ident"))
                    last.then_inc(ht_turned, 1)
            pe.wait_ge(ht_made, HM)
            pe.transpose(PS[0:16, 7, 0:128], nfin, C("ident")).then_inc(nf_turned, 1)

        def act_rows_a(act, ch):
            act.wait_ge(gates_mm, 1)
            act.activation(g[0], PS[0:16, 4, 0:T], ACT.Identity, bias=bgi[:, 0:1]).then_inc(gi_made, 1)

        def act_rows_b(act, ch):
            act.wait_ge(nab_made, 1)
            ch.step(act.activation(g[2], g[2], ACT.Exp))
            act.activation(g[2], g[2], ACT.Ln, bias=C("small", 16, 1, 1)).then_inc(soft_made, 1)

        def act_rows_c(act, ch):
            act.wait_ge(rows_made, 1)
            act.activation(g[4], g[3], ACT.Exp, scale=-1.0).then_inc(rows_exp, 1)
            act.activation(wint, g[2][:, 128:T], ACT.Exp, scale=-1.0, bias=m0c[:, 0:1]).then_inc(rows_exp, 1)
            act.activation(g[5][:, 0:128], g[0][:, 0:128], ACT.Exp, bias=gm[:, 1:2]).then_inc(rows_exp, 1)

        def dve_rows(dve, ch, sp_):
            F, B_ = C("dir", 16, 0, 1), C("dir", 16, 1, 1)
            one = C("small", 16, 1, 1)
            dve.wait_ge(gates_mm, 1)
            ch.step(dve.tensor_scalar(g[1], PS[0:16, 5, 0:T], bgf[:, 0:1], None, ALU.add))
            ch.step(dve.tensor_scalar(g[2], g[1], -1.0, None, ALU.mult))
            dve.tensor_tensor(g[2], g[2], g[1], ALU.min).then_inc(nab_made, 1)
            sp_.upto(U_INC_T + RING)
            dve.wait_ge(soft_made, 1)
            ch.step(dve.scalar_tensor_tensor(g[1], g[1], 0.0, g[2], ALU.min, ALU.subtract))

            def scans(op0, src, start, ones):
                for lo, hi, st_ in ((0, 128, 0.0), (128, T, start)):
                    d0 = one.to_broadcast([16, hi - lo]) if ones else src[:, lo:hi]
                    last = dve.tensor_tensor_scan(g[3][:, lo:hi], d0, src[:, lo:hi], st_, op0[0], op0[1])
                    back = slice(hi - 1, lo - 1 if lo else None, -1)
                    d0 = one.to_broadcast([16, hi - lo]) if ones else src[:, back]
                    last = dve.tensor_tensor_scan(g[4][:, back], d0, src[:, back], st_, op0[0], op0[1])
                ch.step(last)

            def pick(dst):
                ch.step(dve.tensor_scalar(g[3], g[3], F, None, ALU.mult))
                ch.step(dve.scalar_tensor_tensor(dst, g[4], B_, g[3], ALU.mult, ALU.add))

            scans((ALU.mult, ALU.add), g[1], 0.0, True)
            pick(g[1])
            dve.wait_ge(gi_made, 1)
            ch.step(dve.tensor_tensor(g[0], g[0], g[1], ALU.subtract))
            scans((ALU.max, ALU.max), g[0], m0c[:, 0:1], False)
            pick(g[2])
            dve.tensor_scalar(negM, g[2], -1.0, None, ALU.mult)
            ch.step(dve.tensor_tensor(g[3], g[1], g[2], ALU.add))
            for dst, src in ((0, g[2]), (2, g[3])):
                ch.step(dve.tensor_scalar(gm[:, dst:dst + 1], src[:, 127:128], F, None, ALU.mult))
                ch.step(dve.scalar_tensor_tensor(gm[:, dst:dst + 1], src[:, 0:1], B_, gm[:, dst:dst + 1],
                                                 ALU.mult, ALU.add))
            dve.tensor_scalar(gm[:, 1:2], gm[:, 0:1], -1.0, None, ALU.mult).then_inc(rows_made, 1)

        def act_mixer1(act, ch, sp_):
            act_rows_a(act, ch)
            for m in range(24):
                act.wait_ge(unit_used, U_INC_T + m + 1)
                b, freed, _ = b67(W_INC + m)
                dst = (qM, kM, sg)[m // 8][:, m % 8, :]
                if m >= 16:
                    act.activation(dst, PS[:, b, 0:T], ACT.Sigmoid).then_inc(freed, 1)
                else:
                    act.activation(dst, PS[:, b, 0:T], ACT.Copy, scale=(1.0, SCL)[m // 8]).then_inc(freed, 1)
                sp_.upto(U_INC_T + m + RING)
                if m == 0:
                    act_rows_b(act, ch)
                if m == 4:
                    act_rows_c(act, ch)
            sp_.upto(U_OUTC - 1)
            act.wait_ge(unit_used, U_OUTC)
            for t in range(TT):
                act.activation(V1[:, t, 0:4, 0:128], PS[:, 2 * t, :].rearrange("p (h n) -> p h n", h=4),
                               ACT.Copy).then_inc(v1_act, 1)
            sp_.upto(U_OUTC + RING - 1)
            act.wait_ge(nat_copied, 1)
            for i in range(NM + 3):
                if i < NM:
                    h, d, r = unit(i)
                    act.wait_ge(d_made, i + 1)
                    if i >= 2:
                        act.wait_ge(num_made, i - 1)
                    for t, lo, hi in KEYS[d]:
                        last = act.activation(E[:, i % 2, lo:hi], PS[:, 2 + i % 2, lo:hi], ACT.Exp,
                                              bias=nat[:, t, r:r + 1])
                    last.then_inc(e_made, 1)
                if 0 <= i - 1 < NM:
                    u = i - 1
                    h, d, r = unit(u)
                    act.wait_ge(c_made, u + 1)
                    if u >= 2:
                        act.wait_ge(c_out[d], 16 * h)
                    act.activation(Co[:, d, 0:128], PS[:, 7, 0:128], ACT.Copy)
                    act.activation(nfin[:, r:r + 1], PS[:, 7, 128:129], ACT.Copy).then_inc(co_made, 1)
                if i >= 2 and i % 2 == 0 and i // 2 <= HM:
                    h = i // 2 - 1
                    act.wait_ge(hvar, h + 1)
                    ch.step(act.activation(hrs, hmv[:, :, 1], ACT.Ln, bias=C("small", 128, 0, 1)))
                    act.activation(hrs, hrs, ACT.Exp, scale=-0.5).then_inc(hrstd, 1)
                if i >= 3 and i % 2 == 1:
                    h = (i - 3) // 2
                    act.wait_ge(ht_made, h + 1)
                    act.activation(Hh[:, h, :], ht, ACT.Copy).then_inc(mh_hi, 1)
            act.wait_ge(nf_turned, 1)
            act.activation(nfT, PS[0:16, 7, 0:128], ACT.Copy).then_inc(nf_made, 1)

        def dve_mixer1(dve, ch, sp_):
            dve_rows(dve, ch, sp_)
            for m in range(24):
                sp_.upto(U_INC_T + m + RING)
            dve.wait_ge(nat_turned, 1)
            dve.tensor_copy(nat.rearrange("p a b -> p (a b)"), PS[:, 3, 0:128]).then_inc(nat_copied, 1)
            sp_.upto(U_OUTC - 1)
            dve.wait_ge(unit_used, U_OUTC)
            for t in range(TT):
                dve.tensor_copy(V1[:, t, 4:8, 0:128], PS[:, 2 * t + 1, :].rearrange("p (h n) -> p h n", h=4)
                                ).then_inc(v1_dve, 1)
            sp_.upto(U_OUTC + RING - 1)
            dve.wait_ge(nat_copied, 1)
            for i in range(NM + 3):
                if i < NM:
                    h, d, r = unit(i)
                    dve.wait_ge(wb_made, i + 1)
                    if i >= 2:
                        dve.wait_ge(num_made, i - 1)
                    dve.tensor_tensor(qw[:, d, :], PS[:, 6, 0:256], qM[:, h, 128:T], ALU.mult).then_inc(qw_made, 1)
                    dve.wait_ge(st_made, h + 1)
                    dve.wait_ge(e_made, i + 1)
                    e = E[:, i % 2, :]
                    if d == 0:
                        dve.tensor_tensor(e[:, 0:384], e[:, 0:384], PS[:, 0, 0:384], ALU.mult)
                        last = dve.tensor_tensor(e[:, 384:512], e[:, 384:512], PS[:, 1, 128:256], ALU.mult)
                    else:
                        dve.tensor_tensor(e[:, 0:256], e[:, 0:256], PS[:, 0, 0:256], ALU.mult)
                        last = dve.tensor_tensor(e[:, 256:512], e[:, 256:512], PS[:, 1, 0:256], ALU.mult)
                    last.then_inc(p_done, 1)
                    if d == 0:
                        dve.wait_ge(km_turned, h + 1)
                        dve.tensor_scalar(kw[:, 0, :], PS[:, 7, 0:128], nat[:, 6, h:h + 1], None, ALU.mult)
                        dve.tensor_scalar(kw[:, 1, :], PS[:, 7, 0:128], nat[:, 6, 8 + h:9 + h], None,
                                          ALU.mult).then_inc(kw_made, 1)
                if 0 <= i - 1 < NM:
                    u = i - 1
                    h, d, r = unit(u)
                    dve.wait_ge(num_made, u + 1)
                    num = PS[:, 4 + u % 2, 0:387].rearrange("p (t n) -> p t n", t=TT)
                    den = rd[:, d, :].unsqueeze(2)
                    ch.step(dve.tensor_scalar(den, num[:, :, 128:129], -1.0, None, ALU.mult))
                    ch.step(dve.tensor_tensor(den, den, num[:, :, 128:129], ALU.max))
                    ch.step(dve.tensor_tensor(den, den, nat[:, 3:6, r:r + 1], ALU.max))
                    ch.step(dve.reciprocal(den, den))
                    rb = den.to_broadcast([128, TT, 128])
                    if d == 0:
                        dve.tensor_tensor(hs, num[:, :, 0:128], rb, ALU.mult).then_inc(rd_done, 1)
                    else:
                        if h:
                            dve.wait_ge(mh_hi, h)
                        ht3 = ht.rearrange("p (t n) -> p t n", t=TT)
                        dve.tensor_tensor(ht3, num[:, :, 0:128], rb, ALU.mult).then_inc(rd_done, 1)
                        dve.wait_ge(rd_done, u + 1)
                        ch.step(dve.tensor_tensor(hs, hs, ht3, ALU.add))
                        for t in range(TT):
                            last = dve.bn_stats(hst[:, t, :], hs[:, t, :])
                        ch.step(last)
                        for t in range(TT):
                            last = dve.bn_aggr(hmv[:, t, :], hst[:, t, :])
                        last.then_inc(hvar, 1)
                        dve.wait_ge(hrstd, h + 1)
                        if h:
                            dve.wait_ge(ht_turned, h)
                        for t in range(TT):
                            last = dve.tensor_scalar(hn[:, t, :], hs[:, t, :], hmv[:, t, 0:1], hrs[:, t:t + 1],
                                                     ALU.subtract, ALU.mult)
                        last.then_inc(hn_made, 1)
                if i >= 3 and i % 2 == 1:
                    h = (i - 3) // 2
                    dve.wait_ge(ht_turned, h + 1)
                    dve.scalar_tensor_tensor(ht, PS[:, 7, 0:T], hgc[:, h:h + 1], sg[:, h, :], ALU.mult,
                                             ALU.mult).then_inc(ht_made, 1)
                    dve.wait_ge(mh_hi, h + 1)
                    dve.tensor_tensor(Hl[:, h, :], ht, Hh[:, h, :].bitcast(f32), ALU.subtract).then_inc(mh_lo, 1)

        def pool_mixer1(pool, ch):
            pool.wait_ge(ada_small, 12)
            pool.dma_start(wg, a["w_in_c"][0][:, 4 * D:4 * D + 32].rearrange("(k p) n -> p k n", p=128)
                           ).then_inc(wg_in, 16)
            pool.dma_start(n0r, a["state_n"][0, 0].rearrange("d h n -> (d h) n")).then_inc(n0_in, 16)
            pool.memset(V1[:, :, :, 128:129], 1.0).then_inc(ones_set, 1)
            pool.wait_ge(wg_in, 16)
            w5 = wg.rearrange("p k (d s h) -> p k d s h", d=2, s=2)
            for s_, dst in ((0, wgi), (1, wgf)):
                pool.tensor_copy(dst.rearrange("p k (d h) -> p k d h", d=2), w5[:, :, :, s_, :]).then_inc(wg_cut, 1)
            pool.wait_ge(rows_made, 1)
            pool.dma_start(out["m"][0, 0].rearrange("d (h a) -> (d h) a", a=1), gm[:, 2:3]).then_inc(m_out, 16)
            pool.wait_ge(m_out, 16)
            pool.wait_ge(nat_copied, 1)

            def start_state(u):
                h, d, r = unit(u)
                if u >= 2:
                    pool.wait_ge(num_made, u - 1)
                pool.dma_start(CN[:, d, 0:128], a["state_C"][0, 0, d, h]).then_inc(cn_in[d], 16)
                pool.tensor_copy(CN[:, d, 128:129], nat[:, 7, r:r + 1]).then_inc(cn_col, 1)

            start_state(0)
            start_state(1)
            for u in range(NM):
                h, d, r = unit(u)
                pool.wait_ge(co_made, u + 1)
                pool.dma_start(out["C"][0, 0, d, h], Co[:, d, 0:128]).then_inc(c_out[d], 16)
                if u + 2 < NM:
                    start_state(u + 2)
            pool.wait_ge(nf_made, 1)
            pool.dma_start(out["n"][0, 0].rearrange("d h n -> (d h) n"), nfT).then_inc(m_out, 16)

        hn_turned = sem("hn_turned")
        hn_copied = sem("hn_copied")
        logit_made = sem("logit_made")
        gap_made = sem("gap_made")
        gap_exp = sem("gap_exp")
        chosen = sem("chosen")
        rank_made = sem("rank_made")
        slots_made = sem("slots_made")
        scattered = sem("scattered")
        tok_in = sem("tok_in")
        tok_turned = sem("tok_turned")
        hsh_made = sem("hsh_made")
        hsl_made = sem("hsl_made")
        esilu_made = sem("esilu_made")
        eprod_made = sem("eprod_made")
        etr_made = sem("etr_made")
        eguh_made = sem("eguh_made")
        egul_made = sem("egul_made")
        y_made = sem("y_made")
        yb_free = sem("yb_free")
        y_out = sem("y_out")
        y_back = sem("y_back")
        y_mixed = sem("y_mixed")
        pool_pass = sem("pool_pass")
        E_ORDER = [("gu", 0, q) for q in range(4)]
        for c in range(1, MC):
            E_ORDER += [("gu", c, q) for q in range(4)]
            if c < MC - 1:
                E_ORDER += [("dn", c - 1, q) for q in range(2)]
        E_ORDER += [("dn", c, q) for c in (MC - 2, MC - 1) for q in range(2)]
        assert len(E_ORDER) == UB
        FILLS = [sum(1 for n in range(U_MOE) if n % RING == s) for s in range(RING)]

        def pe_route(pe):
            for i in range(6):
                t, half = i // 2, i % 2
                b, freed, before = b67(W_HN + i)
                if i == 0:
                    for f in free67:
                        pe.wait_ge(f, W_HN // 2)
                pe.wait_ge(freed, before)
                for k in range(4):
                    last = pe.transpose(PS[:, b, 128 * k:128 * k + 128], H32[:, 4 * half + k, 128 * t:128 * t + 128],
                                        C("ident"))
                last.then_inc(hn_turned, 1)
            for t in range(TT):
                for k in range(KT):
                    last = pe.matmul(PS[:, 0, NE * t:NE * t + NE], H32[:, k, 128 * t:128 * t + 128], rwt[:, k, :],
                                     start=(k == 0), stop=(k == KT - 1))
            last.then_inc(logit_made, 1)
            pe.wait_ge(chosen, 1)
            for t in range(TT):
                for j in range(t + 1):
                    pe.matmul(PS[:, 1, NE * t:NE * t + NE], C("strict" if j == t else "ones"), asum[:, j, :],
                              start=(j == 0), stop=(j == t))
            for j in range(TT):
                last = pe.matmul(PS[:, 1, 3 * NE:4 * NE], C("ones"), asum[:, j, :], start=(j == 0), stop=(j == TT - 1))
            last.then_inc(rank_made, 1)

        def act_route(act, ch):
            act.wait_ge(modc_made, 8)
            for i in range(KT):
                b, freed, _ = b67(W_H[3] + i)
                act.wait_ge(turned, 3 * KT + i + 1)
                act.activation(H32[:, i, 0:128], PS[:, b, 0:128], ACT.Identity,
                               bias=modc[:, 2, i, 1:2], scale=modc[:, 3, i, 1:2])
                act.activation(H32[:, i, 128:T], PS[:, b, 128:T], ACT.Identity, bias=modc[:, 2, i, 0:1],
                               scale=modc[:, 3, i, 0:1]).then_inc(freed, 1)
            for i in range(6):
                t, half = i // 2, i % 2
                b, freed, _ = b67(W_HN + i)
                act.wait_ge(hn_turned, i + 1)
                act.activation(Hn[:, t, 512 * half:512 * half + 512], PS[:, b, :], ACT.Copy).then_inc(freed, 1)
            act.wait_ge(gap_made, 1)
            act.activation(e2[:, :, 1:2], e2[:, :, 0:1], ACT.Exp).then_inc(gap_exp, 1)

        def dve_route(dve, ch):
            bc3 = lambda x: x.unsqueeze(1).to_broadcast([128, TT, NE])
            dve.wait_ge(logit_made, 1)
            ch.step(dve.tensor_tensor(lg, PS[:, 0, 0:3 * NE].rearrange("p (t e) -> p t e", t=TT), bc3(rbb[:, :]),
                                      ALU.add))
            for t in range(TT):
                last = dve.max(top8[:, t, :], lg[:, t, :])
            ch.step(last)
            dve.tensor_tensor(e2[:, :, 0:1], top8[:, :, 1:2], top8[:, :, 0:1], ALU.subtract).then_inc(gap_made, 1)
            for t in range(TT):
                last = dve.max_index(idx_u[:, t, :], top8[:, t, :], lg[:, t, :])
            ch.step(last)
            ch.step(dve.tensor_copy(idxf, idx_u[:, :, :]))
            for kk in range(2):
                for t in range(TT):
                    last = dve.tensor_scalar(oh[:, kk, t, :], C("iota8"), idxf[:, t, kk:kk + 1], None, ALU.is_equal)
            ch.step(last)
            dve.tensor_tensor(asum, oh[:, 0], oh[:, 1], ALU.add).then_inc(chosen, 1)
            dve.wait_ge(gap_exp, 1)
            ch.step(dve.tensor_scalar(wts[:, :, 1:2], e2[:, :, 1:2], 1.0, None, ALU.add))
            ch.step(dve.reciprocal(wts[:, :, 0:1], wts[:, :, 1:2]))
            ch.step(dve.tensor_tensor(wts[:, :, 1:2], wts[:, :, 0:1], e2[:, :, 1:2], ALU.mult))
            dve.wait_ge(rank_made, 1)
            ch.step(dve.tensor_copy(bb[:, 0, :], PS[:, 1, 3 * NE:4 * NE]))
            ch.step(dve.tensor_scalar(bb[:, 1, :], bb[:, 0, :], 0.0, None, ALU.is_gt))
            for least in (128.0, 256.0):
                ch.step(dve.scalar_tensor_tensor(bb[:, 1, :], bb[:, 0, :], least, bb[:, 1, :], ALU.is_gt, ALU.add))
            ch.step(dve.tensor_tensor_scan(bb[:, 2, :], C("small", 128, 1, 1).to_broadcast([128, NE]), bb[:, 1, :],
                                           0.0, ALU.mult, ALU.add))
            ch.step(dve.tensor_tensor(bb[:, 3, :], bb[:, 2, :], bb[:, 1, :], ALU.subtract))
            ch.step(dve.scalar_tensor_tensor(rk, bc3(bb[:, 3, :]), 128.0,
                                             PS[:, 1, 0:3 * NE].rearrange("p (t e) -> p t e", t=TT), ALU.mult, ALU.add))
            for kk in range(2):
                last = dve.tensor_tensor(wk[:, kk], oh[:, kk], rk, ALU.mult)
            ch.step(last)
            for kk in range(2):
                last = dve.tensor_reduce(slf[:, :, kk:kk + 1], wk[:, kk], AX.X, ALU.add)
            ch.step(last)
            dve.tensor_copy(slot_u[:, :, :], slf)
            ch.step(dve.tensor_tensor(eid, C("iota16", 1).unsqueeze(2).to_broadcast([1, 16, NE]),
                                      bb[0:1, 2, :].unsqueeze(1).to_broadcast([1, 16, NE]), ALU.is_ge))
            ch.step(dve.tensor_reduce(ctl_f[0:1, 1:17].unsqueeze(2), eid, AX.X, ALU.add))
            ch.step(dve.tensor_scalar(ctl_f[0:1, 1:17], ctl_f[0:1, 1:17], float(NE - 1), None, ALU.min))
            ch.step(dve.tensor_copy(ctl_f[0:1, 0:1], bb[0:1, 2, NE - 1:NE]))
            dve.tensor_copy(ctl[:, :], ctl_f[:, :]).then_inc(slots_made, 1)

        def blocks(eng):
            eng.wait_ge(slots_made, 1)
            return eng.value_load(ctl[0:1, 0:1], min_val=1, max_val=NBMAX)

        def sp_experts(sp):
            nb = blocks(sp)

            def load(e, v):
                kind, c, q = E_ORDER[v]
                s = v % RING
                if kind == "gu":
                    for side in range(2):
                        src = a["moe_w_gu"][0, bass.ds(e, 1), 256 * q:256 * q + 256,
                                            FE * side + 256 * c:FE * side + 256 * c + 256]
                        dst = raw[:, s, :].rearrange("p (k n) -> p k n", k=2)[:, :, 256 * side:256 * side + 256]
                        yield dst, src.rearrange("a (k p) n -> p (a k) n", p=128)
                else:
                    row = 256 * c + 128 * q
                    yield raw[:, s, :], a["moe_w_down"][0, bass.ds(e, 1), row:row + 128, :].rearrange("a p n -> p (a n)")

            e0 = sp.value_load(ctl[0:1, 1:2], min_val=0, max_val=NE - 1)
            sp.wait_ge(lo_made, U_MOE)
            for v in range(RING):
                for dst, src in load(e0, v):
                    sp.dma_start(dst, src).then_inc(raw_full[v % RING], 16)
            with sp.Fori(0, nb) as j:
                e = sp.value_load(ctl[0:1, bass.ds(j + 1, 1)], min_val=0, max_val=NE - 1)
                en = sp.value_load(ctl[0:1, bass.ds(j + 2, 1)], min_val=0, max_val=NE - 1)
                for w in range(UB):
                    v = w + RING
                    sp.wait_ge(lo_made, j * UB + (U_MOE + w + 1))
                    for dst, src in load(e if v < UB else en, v % UB):
                        sp.dma_start(dst, src).then_inc(raw_full[v % RING], 16)

        def full_value(v):
            s = v % RING
            per = [32 if E_ORDER[x][0] == "gu" else 16 for x in range(UB)]
            total = sum(per[x] for x in range(UB) if x % RING == s)
            here = sum(per[x] for x in range(v % UB + 1) if x % RING == s)
            return 16 * FILLS[s] + here + (total if v >= UB else 0), total

        def act_experts(act):
            nb = blocks(act)
            act.wait_ge(unit_used, U_MOE)

            def hi(v, j):
                s = v % RING
                first, per = full_value(v)
                act.wait_ge(raw_full[s], j * per + first if j is not None else first)
                act.activation(whi[:, s, :], raw[:, s, :], ACT.Copy).then_inc(hi_made, 1)

            def tokens(j):
                act.wait_ge(tok_turned, j + 1)
                for b in range(2):
                    act.activation(Hh[:, 4 * b:4 * b + 4, 0:128],
                                   PS[:, 4 + b, :].rearrange("p (k n) -> p k n", k=4), ACT.Copy).then_inc(hsh_made, 1)

            def product_hi(c, j):
                act.wait_ge(etr_made, j * MC + (c + 1))
                act.activation(gu_h[:, c % 2, 0:256], PS[:, 6 + c % 2, 0:256], ACT.Copy).then_inc(eguh_made, 1)

            for v in range(RING):
                hi(v, None)
            tokens(0)
            with act.Fori(0, nb) as j:
                for w, (kind, c, q) in enumerate(E_ORDER):
                    act.wait_ge(unit_used, j * UB + (U_MOE + w + 1))
                    hi(w + RING, j)
                    if kind == "gu" and q == 3:
                        act.activation(gp[:, c % 2, 0:256], PS[:, c % 2, 0:256], ACT.Silu).then_inc(esilu_made, 1)
                        if c == MC - 1:
                            tokens(j + 1)
                    if kind == "gu" and q == 1 and c >= 1:
                        product_hi(c - 1, j)
                    if kind == "dn" and q == 0 and c == MC - 2:
                        product_hi(MC - 1, j)
                act.wait_ge(yb_free, j + 1)
                act.activation(yb.rearrange("p (a n) -> p a n", a=2), PS[:, 2:4, :], ACT.Copy).then_inc(y_made, 1)

        def dve_experts(dve):
            nb = blocks(dve)

            def lo(v, j):
                s = v % RING
                dve.wait_ge(hi_made, j * UB + (U_MOE + v + 1) if j is not None else U_MOE + v + 1)
                dve.tensor_tensor(wlo[:, s, :], raw[:, s, :], whi[:, s, :].bitcast(f32),
                                  ALU.subtract).then_inc(lo_made, 1)

            def tokens(j):
                for b in range(2):
                    dve.wait_ge(hsh_made, 2 * j + (b + 1))
                    dve.tensor_tensor(Hl[:, 4 * b:4 * b + 4, 0:128],
                                      PS[:, 4 + b, :].rearrange("p (k n) -> p k n", k=4),
                                      Hh[:, 4 * b:4 * b + 4, 0:128].bitcast(f32), ALU.subtract).then_inc(hsl_made, 1)

            def product_lo(c, j):
                dve.wait_ge(eguh_made, j * MC + (c + 1))
                dve.tensor_tensor(gu_l[:, c % 2, 0:256], PS[:, 6 + c % 2, 0:256],
                                  gu_h[:, c % 2, 0:256].bitcast(f32), ALU.subtract).then_inc(egul_made, 1)

            for v in range(RING):
                lo(v, None)
            tokens(0)
            with dve.Fori(0, nb) as j:
                for w, (kind, c, q) in enumerate(E_ORDER):
                    lo(w + RING, j)
                    if kind == "gu" and q == 3:
                        dve.wait_ge(esilu_made, j * MC + (c + 1))
                        dve.tensor_tensor(gp[:, c % 2, 0:256], gp[:, c % 2, 0:256], PS[:, c % 2, 256:512],
                                          ALU.mult).then_inc(eprod_made, 1)
                        if c == MC - 1:
                            tokens(j + 1)
                    if kind == "gu" and q == 1 and c >= 1:
                        product_lo(c - 1, j)
                    if kind == "dn" and q == 0 and c == MC - 2:
                        product_lo(MC - 1, j)

        def pe_experts(pe):
            nb = blocks(pe)

            def turn_tokens(j):
                pe.wait_ge(tok_in, j * 16 + 16)
                for k in range(KT):
                    last = pe.transpose(PS[:, 4 + k // 4, 128 * (k % 4):128 * (k % 4) + 128],
                                        hsn[:, 128 * k:128 * k + 128], C("ident"))
                last.then_inc(tok_turned, 1)

            def turn_product(c, j):
                pe.wait_ge(eprod_made, j * MC + (c + 1))
                for r in range(2):
                    last = pe.transpose(PS[:, 6 + c % 2, 128 * r:128 * r + 128],
                                        gp[:, c % 2, 128 * r:128 * r + 128], C("ident"))
                last.then_inc(etr_made, 1)

            pe.wait_ge(free67[0], W_END // 2)
            pe.wait_ge(free67[1], W_END // 2)
            turn_tokens(0)
            with pe.Fori(0, nb) as j:
                for w, (kind, c, q) in enumerate(E_ORDER):
                    s = w % RING
                    if w == 0:
                        pe.wait_ge(hsl_made, 2 * j + 2)
                    if kind == "dn" and q == 0:
                        pe.wait_ge(egul_made, j * MC + (c + 1))
                    pe.wait_ge(lo_made, j * UB + (U_MOE + w + 1))
                    if kind == "gu":
                        for k in range(2):
                            h, l = Hh[:, 2 * q + k, 0:128], Hl[:, 2 * q + k, 0:128]
                            for lhs, wt in ((h, whi), (h, wlo), (l, whi)):
                                last = pe.matmul(PS[:, c % 2, :], lhs, wt[:, s, 512 * k:512 * k + 512],
                                                 start=(q == 0 and k == 0 and lhs is h and wt is whi),
                                                 stop=(q == 3 and k == 1 and lhs is l))
                    else:
                        h, l = (x[:, c % 2, 128 * q:128 * q + 128] for x in (gu_h, gu_l))
                        for lhs, wt in ((h, whi), (h, wlo), (l, whi)):
                            for half in range(2):
                                last = pe.matmul(PS[:, 2 + half, :], lhs, wt[:, s, 512 * half:512 * half + 512],
                                                 start=(c == 0 and q == 0 and lhs is h and wt is whi),
                                                 stop=(c == MC - 1 and q == 1 and lhs is l))
                    last.then_inc(unit_used, 1)
                    if kind == "gu" and q == 1 and c >= 1:
                        turn_product(c - 1, j)
                    if kind == "gu" and q == 3 and c == MC - 1:
                        turn_tokens(j + 1)
                    if kind == "dn" and q == 0 and c == MC - 2:
                        turn_product(MC - 1, j)

        def pool_experts(pool, ch):
            pool.wait_ge(free67[0], W_END // 2)
            pool.wait_ge(free67[1], W_END // 2)
            nb = blocks(pool)
            pool.wait_ge(zeroed, 16 * (NBMAX + 1))
            for t in range(TT):
                for kk in range(2):
                    pool.indirect_dma_start(scr["tok"], bass.IndirectOffsetOnAxis(ap=slot_u[:, t, kk:kk + 1], axis=0),
                                            Hn[:, t, :], None).then_inc(scattered, 16)
            pool.wait_ge(scattered, 96)
            pool.dma_start(hsn, scr["tok"][0:128, :]).then_inc(tok_in, 16)
            pool.sem_inc(yb_free, 1)
            with pool.Fori(0, nb) as j:
                pool.wait_ge(tok_turned, j + 1)
                pool.sem_inc(pool_pass, 1)
                pool.dma_start(hsn, scr["tok"][bass.ds(j * 128 + 128, 128), :]).then_inc(tok_in, 16)
                pool.wait_ge(y_made, j + 1)
                pool.sem_inc(pool_pass, 1)
                pool.dma_start(scr["tok"][bass.ds(j * 128, 128), :], yb).then_inc(y_out, 16)
                pool.wait_ge(y_out, j * 16 + 16)
                pool.sem_inc(yb_free, 1)
            pool.wait_ge(tok_turned, nb + 1)
            pool.sem_inc(pool_pass, 1)
            for t in range(TT):
                for kk in range(2):
                    pool.indirect_dma_start(Yg[:, t, kk, :], None, scr["tok"],
                                            bass.IndirectOffsetOnAxis(ap=slot_u[:, t, kk:kk + 1], axis=0)
                                            ).then_inc(y_back, 16)

        def dve_mix(dve, ch):
            dve.wait_ge(y_back, 96)
            for t in range(TT):
                dve.tensor_scalar(Yg[:, t, 0, :], Yg[:, t, 0, :], wts[:, t, 0:1], None, ALU.mult).then_inc(y_mixed, 1)
                dve.wait_ge(y_mixed, t + 1)
                ch.step(dve.scalar_tensor_tensor(Yg[:, t, 0, :], Yg[:, t, 1, :], wts[:, t, 1:2], Yg[:, t, 0, :],
                                                 ALU.mult, ALU.add))

        def tail_sp(sp):
            sp_experts(sp)
            sp.wait_ge(x_done, 12)
            sp.dma_start(out["yp"][0], X[:, 0, :]).then_inc(x_out, 16)
            for t in range(2):
                sp.dma_start(out["ys"][0, 128 * t:128 * t + 128, :], X[:, 1 + t, :]).then_inc(x_out, 16)
            sp.wait_ge(x_out, 48)
        def tail_act(act, ch, sp_):
            act_ada(act, sp_, 1)
            act_turn(act, ch, sp_, 2, U_INC_T)
            act_mixer1(act, ch, sp_)
            sp_.upto(U_MOE - 1)
            act_norm(act, ch, 2)
            act_route(act, ch)
            act_experts(act)
            act_norm(act, ch, 3)

        def tail_dve(dve, ch, sp_):
            dve_ada(dve, sp_, 1)
            dve_turn(dve, sp_, 2, U_INC_T)
            dve_mixer1(dve, ch, sp_)
            sp_.upto(U_MOE - 1)
            dve_norm(dve, ch, 2, lambda: dve.wait_ge(unit_used, U_MOE))
            dve_route(dve, ch)
            dve_experts(dve)
            dve_mix(dve, ch)
            dve_norm(dve, ch, 3, lambda: None, lambda t: Yg[:, t, 0, :].rearrange("p (a n) -> p a n", a=2))

        def tail_pool(pool, ch):
            pool_ada(pool, 1)
            pool_mixer1(pool, ch)
            pool.wait_ge(c_out[0], 16 * HM)
            pool.wait_ge(c_out[1], 16 * HM)
            pool.wait_ge(m_out, 32)
            pool.wait_ge(mh_lo, HM)
            pool_norm_load(pool, 2)
            pool_norm(pool, ch, 2)
            pool_experts(pool, ch)
            pool_norm_load(pool, 3)
            pool_norm(pool, ch, 3)

        def tail_pe(pe):
            pe.wait_ge(nat_read, 2 * TT)
            pe_ada(pe, 1)
            pe_turn(pe, 2)
            pe_mixer1(pe)
            pe.wait_ge(mh_lo, HM)
            pe_out(pe, U_OUTC)
            pe_turn(pe, 3)
            pe_route(pe)
            pe_experts(pe)

        block = ctx.enter_context(nc.Block())

        @block.sync
        def _(sp):
            sp.dma_start(crow[0:8, :], a["c"][0, :].rearrange("(k p) -> k p", p=128)).then_inc(cst_loaded, 16)
            sp.dma_start(crow[8:16, :], a["c_ctx"].rearrange("(k p) -> k p", p=128)).then_inc(cst_loaded, 16)
            sp.dma_start(crow[16:20, :], a["pool_scale"][0].rearrange("(k p) -> k p", p=128)).then_inc(cst_loaded, 16)
            sp.dma_start(crow[20:28, :], a["mlstm_norm_g"][0].rearrange("(k p) -> k p", p=128)).then_inc(cst_loaded, 16)
            sp.dma_start(crow[28:29, :], a["diff_norm_g"]).then_inc(cst_loaded, 16)
            sp.dma_start(cst[:, :], a["const"]).then_inc(cst_loaded, 16)
            stream(sp, 0, 2 * RING)
            sp.dma_start(X[:, 0, :], a["x_prompt"][0]).then_inc(x_loaded, 16)
            for t in range(2):
                sp.dma_start(X[:, 1 + t, :], a["x_sample"][0, 128 * t:128 * t + 128, :]).then_inc(x_loaded, 16)
            stream(sp, 2 * RING, U_MOE)
            tail_sp(sp)

        @block.scalar
        def _(act):
            ch = Chain(act, act_step)
            sp_ = Splits(act, True)
            act.dma_start(lamr[0:1, 0:256], a["diff_lambda"][0].rearrange("(a j) d -> a (j d)", a=1)).then_inc(par_loaded, 16)
            act.dma_start(rbb[:, :], a["router_b"][0:1, :].to_broadcast([128, NE])).then_inc(par_loaded, 16)
            act.dma_start(rwt[:, :, :], a["router_w"][0].rearrange("(k p) e -> p k e", p=128)).then_inc(par_loaded, 16)
            for d in range(2):
                for dst, o in ((bgi, 0), (bgf, 8)):
                    act.dma_start(dst[8 * d:8 * d + 8, :],
                                  a["b_gates_c"][0, 16 * d + o:16 * d + o + 8].rearrange("(p a) -> p a", a=1)
                                  ).then_inc(par_loaded, 16)
            act.dma_start(m0c[:, :], a["state_m"][0, 0].rearrange("d (h a) -> (d h) a", a=1)).then_inc(par_loaded, 16)
            act.wait_ge(cst_loaded, 96)
            act.activation(crow[0:16, :], crow[0:16, :], ACT.Silu).then_inc(crow_s, 1)
            act.wait_ge(crow_t, 1)
            act.activation(ccol, PS[:, 4, 0:16], ACT.Copy)
            act.activation(pcol[:, :], PS[:, 4, 16:29], ACT.Copy).then_inc(cc_made, 1)
            act.wait_ge(cc_made, 1)
            act.wait_ge(adaw_zero, 1)
            act.activation(adaw[:, :, 0:4:2], ccol.rearrange("p (g k) -> p k g", g=2), ACT.Copy).then_inc(adaw_hi, 1)
            sp_.upto(RING - 1)
            act.wait_ge(lam_part, 1)
            act.activation(lams[0:1, 2:4], lams[0:1, 0:2], ACT.Exp).then_inc(lam_exp, 1)
            act_ada(act, sp_, 0)
            act_turn(act, ch, sp_, 0, U_INA_T)
            act_mixer0(act, ch, sp_)
            sp_.upto(U_FFN + RING - 1)
            act_norm(act, ch, 0)
            act_turn(act, ch, sp_, 1, U_FFN)
            act_ffn(act, ch, sp_)
            act_norm(act, ch, 1)
            tail_act(act, ch, sp_)

        @block.vector
        def _(dve):
            ch = Chain(dve, dve_step)
            sp_ = Splits(dve, False)
            dve.wait_ge(par_loaded, 16 * 8)
            lp = lamr[0:1, 0:256].rearrange("p (s j d) -> p s j d", s=2, j=2)
            lq = lamr[0:1, 256:384].rearrange("p (s d) -> p s d", s=2)
            ch.step(dve.tensor_tensor(lq, lp[:, :, 0, :], lp[:, :, 1, :], ALU.mult))
            dve.tensor_reduce(lams[0:1, 0:2], lq, AX.X, ALU.add).then_inc(lam_part, 1)
            dve.wait_ge(cc_made, 1)
            dve.tensor_scalar(ngc, ngc, 1.0 - LAM_INIT, None, ALU.mult)
            dve.wait_ge(adaw_hi, 1)
            dve.tensor_tensor(adaw[:, :, 1:4:2], ccol.rearrange("p (g k) -> p k g", g=2),
                              adaw[:, :, 0:4:2].bitcast(f32), ALU.subtract).then_inc(adaw_lo, 1)
            sp_.upto(RING - 1)
            dve.wait_ge(lam_exp, 1)
            ch.step(dve.tensor_tensor(lams[0:1, 0:1], lams[0:1, 3:4], lams[0:1, 2:3], ALU.subtract))
            dve.tensor_scalar(lams[0:1, 1:2], lams[0:1, 0:1], -LAM_INIT, None, ALU.add).then_inc(lam_row, 1)
            dve.wait_ge(lam_bc, 1)
            dve.tensor_copy(lamc[:, :], PS[:, 5, 0:1]).then_inc(lam_made, 1)
            dve_ada(dve, sp_, 0)
            dve_turn(dve, sp_, 0, U_INA_T)
            dve.wait_ge(lam_made, 1)
            dve_mixer0(dve, ch, sp_)
            sp_.upto(U_FFN + RING - 1)
            dve_norm(dve, ch, 0, lambda: dve.wait_ge(unit_used, U_OUTA + KT))
            dve_turn(dve, sp_, 1, U_FFN)
            dve_ffn(dve, ch, sp_)
            dve_norm(dve, ch, 1, lambda: dve.wait_ge(unit_used, U_ADA1))
            tail_dve(dve, ch, sp_)

        @block.gpsimd
        def _(pool):
            ch = Chain(pool, pool_step)
            pool.memset(adaw[:, :, :].bitcast(f32), 0.0).then_inc(adaw_zero, 1)
            ch.step(pool.memset(zero, 0.0))
            for j in range(NBMAX + 1):
                pool.dma_start(scr["tok"][128 * j:128 * j + 128, :], zero).then_inc(zeroed, 16)
            pool_ada(pool, 0)
            pool.dma_start(ck, a["cache_k"][0, 0].rearrange("h t d -> t h d")).then_inc(att_loaded, 16)
            pool.dma_start(cv, a["cache_v"][0, 0].rearrange("h t d -> t h d")).then_inc(att_loaded, 16)
            pool.dma_start(pw, a["pool_w"][0].rearrange("g c d -> c g d")).then_inc(att_loaded, 16)
            pool.dma_start(pm.rearrange("p g n -> p (g n)"), a["poolm"]).then_inc(att_loaded, 16)
            pool.wait_ge(v_made, 1)
            pool.dma_start(out["v"][0, 0].rearrange("h t d -> t h d"),
                           Vn[:, 0, :].rearrange("p (h n) -> p h n", h=HA)).then_inc(cache_out, 16)
            pool.wait_ge(ck_copied, 2)
            pool.dma_start(out["k"][0, 0].rearrange("h t d -> t h d"), kn).then_inc(cache_out, 16)
            pool.wait_ge(o_lo, NU)
            pool_norm_load(pool, 0)
            pool_norm(pool, ch, 0)
            pool.wait_ge(cache_out, 32)
            pool_norm_load(pool, 1)
            pool_norm(pool, ch, 1)
            tail_pool(pool, ch)

        @block.tensor
        def _(pe):
            pe_ada_vectors(pe)
            pe.wait_ge(lam_row, 1)
            pe.matmul(PS[:, 5, 0:1], C("ones", 1), lams[0:1, 1:2], start=True, stop=True).then_inc(lam_bc, 1)
            pe.wait_ge(adaw_lo, 1)
            pe.wait_ge(lam_made, 1)
            pe_ada(pe, 0)
            pe_turn(pe, 0)
            pe_mixer0(pe)
            pe.wait_ge(pool_lo, 4)
            pe.wait_ge(o_lo, NU)
            pe_out(pe, U_OUTA)
            pe_turn(pe, 1)
            pe_ffn(pe)
            tail_pe(pe)


_INS = ["x_prompt", "x_sample", "c", "cache_k", "cache_v", "state_C", "state_n", "state_m", "c_ctx", "ada_w",
        "ada_b", "ln_g", "ln_b", "w_in_a", "diff_lambda", "diff_norm_g", "pool_w", "pool_scale", "w_out_a",
        "ffn_w_gu", "ffn_w_down", "w_in_c", "b_gates_c", "mlstm_norm_g", "w_out_c", "router_w", "router_b",
        "moe_w_gu", "moe_w_down"]
_OUTS = {"yp": (1, 128, D), "ys": (1, 256, D), "k": (1, 1, HA, 128, 128), "v": (1, 1, HA, 128, 128),
         "C": (1, 1, 2, HM, 128, 128), "n": (1, 1, 2, HM, 128), "m": (1, 1, 2, HM)}


def kernel(**inputs):
    import concourse.bacc as bacc
    from concourse.bass_utils import run_bass_kernel_spmd

    nc = bacc.Bacc("TRN2", target_bir_lowering=False, num_devices=1)
    arrays, a = {}, {}
    for name in _INS:
        arrays[f"in_{name}"] = np.ascontiguousarray(inputs[name])
    arrays["in_const"], arrays["in_poolm"] = CONST, POOLM
    for name, x in arrays.items():
        a[name[3:]] = nc.dram_tensor(name, x.shape, mybir.dt.from_np(x.dtype), kind="ExternalInput").ap()
    out = {n: nc.dram_tensor(f"out_{n}", s, mybir.dt.float32, kind="ExternalOutput").ap() for n, s in _OUTS.items()}
    scr = {n: nc.dram_tensor(f"scr_{n}", (128 * (NBMAX + 1), D), mybir.dt.float32).ap() for n in ("tok",)}
    backbone_step(nc, a, out, scr)
    r = run_bass_kernel_spmd(nc, [arrays], core_ids=[0])
    return tuple(r.results[0][f"out_{n}"] for n in _OUTS)
```

```python
import math
from contextlib import ExitStack

import numpy as np

import concourse.bass as bass
from concourse import mybir

D = 1024
KT = D // 128
T = 384
TT = T // 128
HA = 4
HM = 8
FF = 2816
FC = FF // 128
NE = 8
FE = 1792
MC = FE // 256
NBMAX = (2 * T + NE * 127) // 128
ALPHA = 4.0 ** 0.25
EPS = 1e-5
LAM_INIT = 0.8 - 0.6 * math.exp(0.0)
BIG_NEG = -1e30
WINDOWS = (2, 4, 8, 16)
NU = HA * TT
NM = HM * 2

RING = 6
FIRST, MID, EARLY, LATE = (0, 2), (2, 5), (5, 8), (8, 12)
U_ADA_FIRST = 0
U_INA_T = U_ADA_FIRST + KT * (FIRST[1] - FIRST[0])
INA_ORDER = []
for _m in range(8):
    INA_ORDER += [("t", _m)] + [("a", 0)] * (4 if _m < 6 else 0)
assert sum(1 for x in INA_ORDER if x[0] == "a") == KT * (MID[1] - MID[0])
U_INA_N = U_INA_T + len(INA_ORDER)
U_ADA_EARLY = U_INA_N + KT
U_OUTA = U_ADA_EARLY + KT * (EARLY[1] - EARLY[0])
U_FFN = U_OUTA + KT
U_INC_T = U_FFN + 3 * FC
INC_ORDER = []
for _m in range(24):
    INC_ORDER += [("t", _m)] + [("a", 0)] * ((2 if _m % 2 == 0 or _m < 4 else 1) if _m < 20 else 0)
assert sum(1 for x in INC_ORDER if x[0] == "a") == KT * (LATE[1] - LATE[0])
U_INC_N = U_INC_T + len(INC_ORDER)
U_OUTC = U_INC_N + KT
U_MOE = U_OUTC + KT
ADA_UNITS = {FIRST: [U_ADA_FIRST + i for i in range(KT * (FIRST[1] - FIRST[0]))],
             MID: [U_INA_T + i for i, x in enumerate(INA_ORDER) if x[0] == "a"],
             EARLY: [U_ADA_EARLY + i for i in range(KT * (EARLY[1] - EARLY[0]))],
             LATE: [U_INC_T + i for i, x in enumerate(INC_ORDER) if x[0] == "a"]}
UB = 6 * MC
assert UB % RING == 0
assert 1 + (2 * T + (NE - 1) * 127) // 128 <= NBMAX

W_INA = 0
W_FFN = W_INA + 8
W_INC = W_FFN + 2 * FC


def constants():
    p = np.arange(128)
    cols = {}
    cols["ident"] = np.eye(128)
    cols["ones"] = np.ones((128, 128))
    t = np.arange(256)
    axis, half, freq = (p // 32) % 2, (p // 16) % 2, p % 16
    inv = np.power(np.float32(10000.0), -np.arange(16, dtype=np.float32) / np.float32(16)).astype(np.float32)
    pos = np.where(axis[:, None] == 0, (t // 64)[None], (t % 64)[None]).astype(np.float32)
    ang = pos * inv[freq][:, None]
    cols["cos"] = np.cos(ang)
    cols["sin"] = np.sin(ang)
    rot = np.zeros((128, 128))
    for d in range(128):
        rot[d + 16 if half[d] == 0 else d - 16, d] = -1.0 if half[d] == 0 else 1.0
    cols["rot"] = rot
    s, q = p[:, None], p[None]
    cols["mask_f"] = np.where(s <= q, 0.0, BIG_NEG)
    cols["mask_b"] = np.where(s >= q, 0.0, BIG_NEG)
    cols["strict"] = (s < q)
    comb = np.zeros((128, 2))
    comb[[0, 1, 4], 0] = 1.0
    comb[[2, 3, 4], 1] = 1.0
    cols["comb"] = comb
    cols["dir"] = np.stack([(p < 8), (p >= 8)], 1)
    cols["iota8"] = np.tile(np.arange(8), (128, 1))
    cols["iota16"] = np.tile(np.arange(16), (128, 1))
    cols["small"] = np.tile(np.array([EPS, 1.0, 0.0]), (128, 1))
    at, parts, n = {}, [], 0
    for k, v in cols.items():
        at[k] = (n, v.shape[1])
        parts.append(v.astype(np.float32))
        n += v.shape[1]

    def pool(n_tokens):
        m = np.zeros((4, n_tokens, n_tokens), np.float32)
        for g, w in enumerate(WINDOWS):
            for to in range(n_tokens):
                lo, hi = max(to - w // 2, 0), min(to + w // 2 - 1, n_tokens - 1)
                m[g, lo:hi + 1, to] = 1.0 / (hi - lo + 1)
                m[g, to, to] -= 1.0
        return m
    mp, ms = pool(128), pool(256)
    pm = np.zeros((128, 4, 640), np.float32)
    for g in range(4):
        pm[:, g, 0:128] = mp[g]
        pm[:, g, 128:384] = ms[g, 0:128]
        pm[:, g, 384:640] = ms[g, 128:256]
    return np.concatenate(parts, 1), at, pm.reshape(128, -1)


CONST, CAT, POOLM = constants()


class Chain:

    def __init__(self, eng, sem):
        self.eng, self.sem, self.base, self.n = eng, sem, 0, 0

    def step(self, ins):
        ins.then_inc(self.sem, 1)
        self.n += 1
        self.eng.wait_ge(self.sem, self.base + self.n)


def backbone_step(nc, a, out, scr):
    f32, f32r, i32, u32 = mybir.dt.float32, mybir.dt.float32r, mybir.dt.int32, mybir.dt.uint32
    ALU, ACT, AX = mybir.AluOpType, mybir.ActivationFunctionType, mybir.AxisListType
    ctx = ExitStack()
    with ctx:
        def sb(name, shape, dt=f32):
            return ctx.enter_context(nc.sbuf_tensor(name, shape, dt))

        def sem(name):
            return ctx.enter_context(nc.semaphore(name))

        raw = sb("raw", [128, RING, 1024])
        whi = sb("whi", [128, RING, 1024], f32r)
        wlo = sb("wlo", [128, RING, 1024], f32r)
        X = sb("X", [128, TT, D])
        Hh = sb("Hh", [128, KT, T], f32r)
        Hl = sb("Hl", [128, KT, T], f32r)
        gate_bc = sb("gate_bc", [128, 2, 2, D])
        cst = sb("cst", [128, CONST.shape[1]])
        modc = sb("modc", [128, 4, KT, 2])
        lncol = sb("lncol", [128, 2, 4, KT])
        cr = sb("cr", [128, 3, 128], f32r)
        adaw = sb("adaw", [128, KT, 128], f32r)
        gu_h = sb("gu_h", [128, 2, T], f32r)
        gu_l = sb("gu_l", [128, 2, T], f32r)
        stats = sb("stats", [128, TT, 2, 6])
        mv = sb("mv", [128, TT, 2])
        rstd = sb("rstd", [128, TT])
        lnt = sb("lnt", [128, KT, 2])
        pcol = sb("pcol", [128, 13])
        psc, hgc, ngc = pcol[:, 0:4], pcol[:, 4:12], pcol[:, 12:13]
        rbb = sb("rbb", [128, NE])
        rwt = sb("rwt", [128, KT, NE])
        bgi = sb("bgi", [16, 1])
        bgf = sb("bgf", [16, 1])
        m0c = sb("m0c", [16, 1])
        lamc = sb("lamc", [128, 1])
        lams = sb("lams", [1, 4])
        att = sb("att", [128, 2, 12])
        ctl_f = sb("ctl_f", [1, 17])
        ctl = sb("ctl", [1, 17], i32)
        slot_u = sb("slot_u", [128, TT, 2], u32)
        wts = sb("wts", [128, TT, 2])
        idx_u = sb("idx_u", [128, TT, 8], u32)
        NBIG = 16600
        BIG = sb("BIG", [128, NBIG])

        def C(name, parts=128, lo=0, n=None):
            o, w = CAT[name]
            n = w - lo if n is None else n
            return cst[0:parts, o + lo:o + lo + n]

        top = [0]

        def area(shape, at=None):
            if at is not None:
                top[0] = at
            n = int(np.prod(shape[1:]))
            v = BIG[0:shape[0], top[0]:top[0] + n]
            top[0] += n
            assert top[0] <= NBIG, top[0]
            if len(shape) == 2:
                return v
            names = "abcd"[:len(shape) - 1]
            kw = {names[i]: shape[1 + i] for i in range(1, len(names))}
            return v.rearrange(f"p ({' '.join(names)}) -> p {' '.join(names)}", **kw)

        lng = area([128, D], 9216)
        lnb = area([128, D])
        ltmp = area([128, 2, D], 0)
        H32 = area([128, KT, T], 3072)
        ftmp = area([128, 2, T], 6144)
        crow = area([29, 128], 13700)
        ccol = area([128, 16])
        lamr = area([1, 512])
        lnrow = area([64, 128])
        arow = area([5, D], 15560)
        qT = area([128, HA, T], 0)
        kT = area([128, HA, T])
        Vn = area([128, TT, 512])
        Pn = area([128, TT, 512])
        kn = area([128, HA, 128])
        ck = area([128, HA, 128])
        cv = area([128, HA, 128])
        ckT = area([128, HA, 128])
        pw = area([128, 4, 128])
        pm = area([128, 4, 640])
        pr = area([128, 2, 2, T])
        aT = area([128, 2, T])
        oN = area([128, 2, 128])
        pT = area([128, T])
        o32 = area([128, 2, T])
        qM = area([128, HM, T], 0)
        kM = area([128, HM, T])
        sg = area([128, HM, T])
        V1 = area([128, TT, HM, 129])
        negM = area([16, T])
        nat = area([128, 8, 16])
        wint = area([16, 256])
        nfin = area([128, 16])
        Z = top[0]
        CN = area([128, 2, 129], Z)
        E = area([128, 2, 512])
        qw = area([128, 2, 256])
        hs = area([128, TT, 128])
        hn = area([128, TT, 128])
        ht = area([128, T])
        kw = area([128, 2, 128])
        Co = area([128, 2, 129])
        rd = area([128, 2, TT])
        hst = area([128, TT, 6])
        hmv = area([128, TT, 2])
        hrs = area([128, TT])
        g = [area([16, T], Z)] + [area([16, T]) for _ in range(5)]
        n0r = area([16, 128])
        gm = area([16, 8])
        assert top[0] <= 15560
        wg = area([128, KT, 32], 11264)
        wgi = area([128, KT, 16])
        wgf = area([128, KT, 16])
        nfT = area([16, 128], Z)
        Hn = area([128, TT, D], 6144)
        lg = area([128, TT, NE], 11300)
        top8 = area([128, TT, 8])
        idxf = area([128, TT, 8])
        oh = area([128, 2, TT, NE])
        asum = area([128, TT, NE])
        rk = area([128, TT, NE])
        bb = area([128, 4, NE])
        wk = area([128, 2, TT, NE])
        slf = area([128, TT, 2])
        e2 = area([128, TT, 2])
        eid = area([1, 16, NE])
        zero = area([128, D], 11776)
        hsn = area([128, D], 0)
        gp = area([128, 2, 512])
        yb = area([128, D])
        Yg = area([128, TT, 2, D], 3072)

        PS = ctx.enter_context(nc.psum_tensor("PS", [128, 8, 512], f32))

        raw_full = [sem(f"raw_full{r}") for r in range(RING)]
        hi_made = sem("hi_made")
        lo_made = sem("lo_made")
        unit_used = sem("unit_used")
        x_loaded = sem("x_loaded")
        cst_loaded = sem("cst_loaded")
        par_loaded = sem("par_loaded")
        att_loaded = sem("att_loaded")
        act_step = sem("act_step")
        dve_step = sem("dve_step")
        pool_step = sem("pool_step")
        zeroed = sem("zeroed")
        crow_t = sem("crow_t")
        crow_s = sem("crow_s")
        cc_made = sem("cc_made")
        adaw_zero = sem("adaw_zero")
        adaw_hi = sem("adaw_hi")
        adaw_lo = sem("adaw_lo")
        bias_in = sem("bias_in")
        arow_made = sem("arow_made")
        ada_small = sem("ada_small")
        gate_spread = sem("gate_spread")
        modc_read = sem("modc_read")
        modc_made = sem("modc_made")
        crow_read = sem("crow_read")
        h32_act = sem("h32_act")
        h32_dve = sem("h32_dve")
        gate_made = sem("gate_made")
        turned = sem("turned")
        hh_made = sem("hh_made")
        hl_made = sem("hl_made")
        free67 = [sem("free6"), sem("free7")]
        v_made = sem("v_made")
        p_made = sem("p_made")
        rot_made = sem("rot_made")
        roped = sem("roped")
        ck_turned = sem("ck_turned")
        ck_copied = sem("ck_copied")
        pool_a = sem("pool_a")
        pool_c = sem("pool_c")
        pool_b = sem("pool_b")
        pool_s = sem("pool_s")
        pool_hi = sem("pool_hi")
        pool_lo = sem("pool_lo")
        lam_part = sem("lam_part")
        lam_exp = sem("lam_exp")
        lam_row = sem("lam_row")
        lam_bc = sem("lam_bc")
        lam_made = sem("lam_made")
        s_made = sem("s_made")
        mx_made = sem("mx_made")
        ex_made = sem("ex_made")
        mix_made = sem("mix_made")
        at_turned = sem("at_turned")
        at_made = sem("at_made")
        o_made = sem("o_made")
        o_sq = sem("o_sq")
        o_norm = sem("o_norm")
        o_turned = sem("o_turned")
        o_hi = sem("o_hi")
        o_lo = sem("o_lo")
        cache_out = sem("cache_out")
        nat_read = sem("nat_read")
        var_made = sem("var_made")
        rstd_made = sem("rstd_made")
        normed = sem("normed")
        x_done = sem("x_done")
        ln_in = sem("ln_in")
        guh_made = sem("guh_made")
        gul_made = sem("gul_made")
        x_out = sem("x_out")

        def b67(w):
            return 6 + w % 2, free67[w % 2], w // 2

        def t_unit(w, col):
            return w[:, col:col + 128].rearrange("(k p) n -> p k n", p=128)

        def source(n):
            for groups, at in ADA_UNITS.items():
                if n in at:
                    q, k = groups[0] + at.index(n) // KT, at.index(n) % KT
                    return a["ada_w"][q // 6, 128 * k:128 * k + 128, D * (q % 6):D * (q % 6) + D]
            if n < U_INA_N:
                return t_unit(a["w_in_a"][0], 128 * INA_ORDER[n - U_INA_T][1])
            if n < U_ADA_EARLY:
                k = n - U_INA_N
                return a["w_in_a"][0, 128 * k:128 * k + 128, D:2 * D]
            if n < U_FFN:
                k = n - U_OUTA
                return a["w_out_a"][0, 128 * k:128 * k + 128, :]
            if n < U_INC_T:
                kind, c = FFN_ORDER[n - U_FFN]
                if kind == "d":
                    return a["ffn_w_down"][0, 128 * c:128 * c + 128, :]
                return t_unit(a["ffn_w_gu"][0], 128 * c + (FF if kind == "u" else 0))
            if n < U_INC_N:
                m = INC_ORDER[n - U_INC_T][1]
                return t_unit(a["w_in_c"][0], 128 * m + (D if m >= 16 else 0))
            if n < U_OUTC:
                k = n - U_INC_N
                return a["w_in_c"][0, 128 * k:128 * k + 128, 2 * D:3 * D]
            k = n - U_OUTC
            return a["w_out_c"][0, 128 * k:128 * k + 128, :]

        FFN_ORDER = [("g", 0), ("u", 0)]
        for c in range(1, FC):
            FFN_ORDER += [("g", c), ("u", c), ("d", c - 1)]
        FFN_ORDER += [("d", FC - 1)]
        FFN_AT = {x: U_FFN + i for i, x in enumerate(FFN_ORDER)}

        def stream(sp, first, last):
            for n in range(first, last):
                if n >= RING:
                    sp.wait_ge(lo_made, n - RING + 1)
                src = source(n)
                dst = raw[:, n % RING, :]
                if len(src.shape) == 3:
                    dst = dst.rearrange("p (k n) -> p k n", k=KT)
                sp.dma_start(dst, src).then_inc(raw_full[n % RING], 16)

        class Splits:
            def __init__(self, eng, upper):
                self.eng, self.upper, self.n = eng, upper, 0

            def upto(self, last):
                while self.n <= min(last, U_MOE - 1):
                    n, s = self.n, self.n % RING
                    if self.upper:
                        if n >= RING:
                            self.eng.wait_ge(unit_used, n - RING + 1)
                        self.eng.wait_ge(raw_full[s], 16 * (n // RING + 1))
                        self.eng.activation(whi[:, s, :], raw[:, s, :], ACT.Copy).then_inc(hi_made, 1)
                    else:
                        self.eng.wait_ge(hi_made, n + 1)
                        self.eng.tensor_tensor(wlo[:, s, :], raw[:, s, :], whi[:, s, :].bitcast(f32),
                                               ALU.subtract).then_inc(lo_made, 1)
                    self.n += 1

        def t_product(pe, n, w):
            b, freed, before = b67(w)
            s = n % RING
            if before:
                pe.wait_ge(freed, before)
            pe.wait_ge(lo_made, n + 1)
            for k in range(KT):
                wh, wl = whi[:, s, 128 * k:128 * k + 128], wlo[:, s, 128 * k:128 * k + 128]
                pe.matmul(PS[:, b, 0:T], wh, Hh[:, k, :], start=(k == 0), stop=False)
                pe.matmul(PS[:, b, 0:T], wh, Hl[:, k, :], start=False, stop=False)
                last = pe.matmul(PS[:, b, 0:T], wl, Hh[:, k, :], start=False, stop=(k == KT - 1))
            last.then_inc(unit_used, 1)

        def n_product(pe, n, sh, sl, first, final):
            s = n % RING
            pe.wait_ge(lo_made, n + 1)
            for t in range(TT):
                h, l = sh[:, 128 * t:128 * t + 128], sl[:, 128 * t:128 * t + 128]
                for lhs, w in ((h, whi), (h, wlo), (l, whi)):
                    for half in range(2):
                        last = pe.matmul(PS[:, 2 * t + half, :], lhs, w[:, s, 512 * half:512 * half + 512],
                                         start=(first and lhs is h and w is whi), stop=(final and lhs is l))
            last.then_inc(unit_used, 1)

        def keep_clock(pe, n):
            for _ in range(n):
                pe.matmul(PS[:, 7, 0:384], cr[:, 0, :], cr[:, :, :].rearrange("p a b -> p (a b)"),
                          start=True, stop=True)

        def pe_ada_vectors(pe):
            pe.wait_ge(crow_s, 1)
            pe.wait_ge(cst_loaded, 16 * 8)
            pe.transpose(PS[:, 4, 0:29], crow, C("ident", 29, 0, 29))
            pe.transpose(PS[:, 4, 64:128], lnrow, C("ident", 64, 0, 64)).then_inc(crow_t, 1)

        GATES = [q for q in range(12) if q % 3 == 2]

        def cols_before(q):
            return sum(1 for x in range(q) if x % 3 < 2)

        class Ada:

            def __init__(self, eng, kind, sp_, groups, ch=None):
                self.eng, self.kind, self.sp_, self.ch = eng, kind, sp_, ch
                self.todo = [(groups[0] + i // KT, i % KT, n) for i, n in enumerate(ADA_UNITS[groups])]
                self.groups, self.at = groups, 0
                self.acc, self.spr = (0, 2) if groups in (MID, LATE) else (5, 7)

            def units(self, count):
                for _ in range(count):
                    if self.at < len(self.todo):
                        q, k, n = self.todo[self.at]
                        self.at += 1
                        ADA_UNIT[self.kind](self, q, k, n)
                        if q > self.groups[0]:
                            ADA_AFTER[self.kind](self, q - 1, k)

            def finish(self):
                self.units(len(self.todo))
                self.after_last(range(KT))

            def after_last(self, steps):
                for k in steps:
                    ADA_AFTER[self.kind](self, self.groups[1] - 1, k)

        def pe_ada_unit(s, q, k, n):
            pe = s.eng
            if k == 0 and q:
                pe.wait_ge(arow_made, q)
            pe.wait_ge(lo_made, n + 1)
            for w in (whi, wlo):
                for half in range(2):
                    last = pe.matmul(PS[:, s.acc + half, :], adaw[:, k, :], w[:, n % RING, 512 * half:512 * half + 512],
                                     start=(k == 0 and w is whi), stop=(k == KT - 1 and w is wlo))
            last.then_inc(unit_used, 1)

        def pe_ada_after(s, q, k):
            pe = s.eng
            gates = 4 * sum(1 for x in GATES if x < q)
            if k == 2:
                pe.wait_ge(arow_made, q + 1)
                pe.wait_ge(bias_in, 16 * (q + 1))
                if cols_before(q):
                    pe.wait_ge(modc_read, cols_before(q))
                if gates:
                    pe.wait_ge(gate_made, gates)
                if q % 3 < 2:
                    for c in range(KT):
                        last = pe.matmul(PS[:, s.spr, 2 * c:2 * c + 2], arow[:, 128 * c:128 * c + 128],
                                         C("comb", 5), start=True, stop=True)
                    last.then_inc(ada_small, 1)
            if q % 3 == 2 and 2 <= k <= 5:
                grp, half = (k - 2) // 2, (k - 2) % 2
                if k > 2:
                    pe.wait_ge(gate_made, gates + k - 2)
                pe.matmul(PS[:, s.spr, :], C("comb", 5, grp, 1).to_broadcast([5, 128]),
                          arow[:, 512 * half:512 * half + 512], start=True, stop=True).then_inc(gate_spread, 1)

        def act_ada_unit(s, q, k, n):
            act = s.eng
            act.wait_ge(unit_used, n + 1)
            if k == KT - 1:
                if q:
                    act.wait_ge(ada_small, cols_before(q))
                    spread = 4 * sum(1 for x in GATES if x < q)
                    if spread:
                        act.wait_ge(gate_spread, spread)
                act.activation(arow[0:4, :].rearrange("p (a n) -> p a n", a=2), PS[0:4, s.acc:s.acc + 2, :],
                               ACT.Copy).then_inc(arow_made, 1)
            s.sp_.upto(n + RING)

        def act_ada_after(s, q, k):
            if q % 3 == 2 and 2 <= k <= 5:
                grp, half = (k - 2) // 2, (k - 2) % 2
                s.eng.wait_ge(gate_spread, 4 * sum(1 for x in GATES if x < q) + k - 1)
                s.eng.activation(gate_bc[:, (q % 6) // 3, grp, 512 * half:512 * half + 512], PS[:, s.spr, :],
                                 ACT.Copy).then_inc(gate_made, 1)

        def dve_ada_unit(s, q, k, n):
            s.sp_.upto(n + RING)

        def dve_ada_after(s, q, k):
            if k != 2 or q % 3 == 2:
                return
            dve, e = s.eng, 2 * ((q % 6) // 3) + q % 3
            dve.wait_ge(ada_small, cols_before(q) + 1)
            dst = modc[:, e, :, :]
            ins = dve.tensor_scalar(dst, PS[:, s.spr, 0:16].rearrange("p (k g) -> p k g", k=KT), float(q % 3), None,
                                    ALU.add)
            ins.then_inc(modc_read, 1)
            if q % 3 == 0:
                return
            dve.wait_ge(modc_read, cols_before(q) + 1)
            norm = 2 * (q // 6) + (q % 6) // 3 - 1
            if norm < 0:
                dve.sem_inc(modc_made, 1)
                return
            ch = s.ch
            gcol, bcol = (lncol[:, x, norm, :].unsqueeze(2).to_broadcast([128, KT, 2]) for x in range(2))
            ch.step(dve.tensor_tensor(lnt[:, :, :], dst, bcol, ALU.mult))
            dve.tensor_tensor(modc[:, e - 1, :, :], modc[:, e - 1, :, :], lnt[:, :, :], ALU.add)
            dve.tensor_tensor(dst, dst, gcol, ALU.mult).then_inc(modc_made, 1)

        ADA_UNIT = {"pe": pe_ada_unit, "act": act_ada_unit, "dve": dve_ada_unit}
        ADA_AFTER = {"pe": pe_ada_after, "act": act_ada_after, "dve": dve_ada_after}

        def pool_ada(pool, groups):
            for q in range(*groups):
                if q:
                    pool.wait_ge(ada_small, cols_before(q))
                    spread = 4 * sum(1 for x in GATES if x < q)
                    if spread:
                        pool.wait_ge(gate_spread, spread)
                pool.dma_start(arow[4:5, :], a["ada_b"][q // 6:q // 6 + 1, D * (q % 6):D * (q % 6) + D]
                               ).then_inc(bias_in, 16)

        def pe_turn(pe, st):
            for t in range(TT):
                if st == 0:
                    pe.wait_ge(x_loaded, 48)
                    pe.wait_ge(crow_read, 2)
                    pe.wait_ge(arow_made, FIRST[1])
                else:
                    keep_clock(pe, (50, 16, 12)[t])
                    pe.wait_ge(normed, TT * (st - 1) + t + 1)
                for i in range(KT):
                    last = pe.transpose(PS[:, 2 * t + i // 4, 128 * (i % 4):128 * (i % 4) + 128],
                                        X[:, t, 128 * i:128 * i + 128], C("ident"))
                last.then_inc(turned, 1)

        def before_turn(eng, st, t):
            eng.wait_ge(modc_made, st + 1)
            eng.wait_ge(turned, TT * st + t + 1)
            if st == 1 and t == 0:
                eng.wait_ge(cache_out, 32)

        def act_mod(act, st, t):
            sub, grp = st % 2, (1 if t == 0 else 0)
            before_turn(act, st, t)
            for i in range(KT // 2):
                last = act.activation(H32[:, i, 128 * t:128 * t + 128], PS[:, 2 * t, 128 * i:128 * i + 128],
                                      ACT.Identity, bias=modc[:, 2 * sub, i, grp:grp + 1],
                                      scale=modc[:, 2 * sub + 1, i, grp:grp + 1])
            last.then_inc(h32_act, 1)

        def dve_mod(dve, st, t):
            sub, grp = st % 2, (1 if t == 0 else 0)
            before_turn(dve, st, t)
            for i in range(KT // 2, KT):
                k = i - KT // 2
                last = dve.tensor_scalar(H32[:, i, 128 * t:128 * t + 128], PS[:, 2 * t + 1, 128 * k:128 * k + 128],
                                         modc[:, 2 * sub + 1, i, grp:grp + 1], modc[:, 2 * sub, i, grp:grp + 1],
                                         ALU.mult, ALU.add)
            last.then_inc(h32_dve, 1)

        def wait_h32(eng, st, t):
            eng.wait_ge(h32_act, TT * st + t + 1)
            eng.wait_ge(h32_dve, TT * st + t + 1)

        def act_upper(act, st, t):
            wait_h32(act, st, t)
            act.activation(Hh[:, :, 128 * t:128 * t + 128], H32[:, :, 128 * t:128 * t + 128], ACT.Copy
                           ).then_inc(hh_made, 1)

        def dve_lower(dve, st, t):
            wait_h32(dve, st, t)
            dve.wait_ge(hh_made, TT * st + t + 1)
            dve.tensor_tensor(Hl[:, :, 128 * t:128 * t + 128], H32[:, :, 128 * t:128 * t + 128],
                              Hh[:, :, 128 * t:128 * t + 128].bitcast(f32), ALU.subtract).then_inc(hl_made, 1)

        def dve_norm_sum(dve, ch, st, t, src):
            sub, grp = st % 2, (1 if t == 0 else 0)
            lt = ltmp[:, t % 2, :].rearrange("p (a n) -> p a n", a=2)
            dve.tensor_tensor(lt, src, gate_bc[:, sub, grp, :].rearrange("p (a n) -> p a n", a=2),
                              ALU.mult).then_inc(nat_read, 1)
            if st:
                dve.wait_ge(x_done, TT * (st - 1) + t + 1)
            dve.wait_ge(nat_read, TT * st + t + 1)
            ch.step(dve.scalar_tensor_tensor(X[:, t, :], X[:, t, :], ALPHA, ltmp[:, t % 2, :], ALU.mult, ALU.add))
            for half in range(2):
                last = dve.bn_stats(stats[:, t, half, :], X[:, t, 512 * half:512 * half + 512])
            ch.step(last)
            dve.bn_aggr(mv[:, t, :], stats[:, t, :, :].rearrange("p a b -> p (a b)")).then_inc(var_made, 1)

        def dve_norm_scale(dve, st, t):
            dve.wait_ge(rstd_made, TT * st + t + 1)
            dve.tensor_scalar(X[:, t, :], X[:, t, :], mv[:, t, 0:1], rstd[:, t:t + 1],
                              ALU.subtract, ALU.mult).then_inc(normed, 1)

        def dve_norm(dve, ch, st, ready, turn=True, parts=True, from_=None):
            src = from_ or (lambda t: PS[:, 2 * t:2 * t + 2, :])
            ready()
            dve_norm_sum(dve, ch, st, 0, src(0))
            dve_norm_sum(dve, ch, st, 1, src(1))
            dve_norm_scale(dve, st, 0)
            dve_norm_sum(dve, ch, st, 2, src(2))
            dve_norm_scale(dve, st, 1)
            if turn:
                dve_mod(dve, st + 1, 0)
            dve_norm_scale(dve, st, 2)
            if turn:
                dve_mod(dve, st + 1, 1)
                if parts:
                    dve_lower(dve, st + 1, 0)
                dve_mod(dve, st + 1, 2)
                if parts:
                    dve_lower(dve, st + 1, 1)
                    dve_lower(dve, st + 1, 2)

        def act_rstd(act, ch, st, t):
            act.wait_ge(var_made, TT * st + t + 1)
            ch.step(act.activation(rstd[:, t:t + 1], mv[:, t, 1:2], ACT.Ln, bias=C("small", 128, 0, 1)))
            act.activation(rstd[:, t:t + 1], rstd[:, t:t + 1], ACT.Exp, scale=-0.5).then_inc(rstd_made, 1)

        def act_norm(act, ch, st, turn=True, parts=True):
            log_exp(act)
            act_rstd(act, ch, st, 0)
            act_rstd(act, ch, st, 1)
            if turn:
                act_mod(act, st + 1, 0)
            act_rstd(act, ch, st, 2)
            if turn:
                if parts:
                    act_upper(act, st + 1, 0)
                for t in (1, 2):
                    act_mod(act, st + 1, t)
                    if parts:
                        act_upper(act, st + 1, t)

        def log_exp(act):
            act.preload_act_table_set("natural_log_exp_and_others")

        def pool_norm_load(pool, st):
            if st:
                pool.wait_ge(x_done, TT * st)
            for i, (dst, name) in enumerate(((lng, "ln_g"), (lnb, "ln_b"))):
                pool.dma_start(dst, a[name][st // 2, st % 2:st % 2 + 1, :].to_broadcast([128, D])
                               ).then_inc(ln_in, 16)

        def pool_norm(pool, ch, st):
            pool.wait_ge(ln_in, 32 * (st + 1))
            for t in range(TT if st < 3 else TT - 1):
                if st < 3:
                    pool.wait_ge(turned, TT * (st + 1) + t + 1)
                else:
                    pool.wait_ge(normed, TT * st + t + 1)
                ch.step(pool.tensor_tensor(X[:, t, :], X[:, t, :], lng, ALU.mult))
                pool.tensor_tensor(X[:, t, :], X[:, t, :], lnb, ALU.add).then_inc(x_done, 1)

        def pe_mixer0(pe):
            pe.wait_ge(hl_made, TT)
            ada = Ada(pe, "pe", None, MID)
            for i, (kind, m) in enumerate(INA_ORDER):
                if kind == "a":
                    ada.units(1)
                else:
                    t_product(pe, U_INA_T + i, W_INA + m)
                    if m == 6:
                        ada.after_last(range(KT))
            pe.wait_ge(modc_read, cols_before(MID[1]))
            for k in range(KT):
                n_product(pe, U_INA_N + k, Hh[:, k, :], Hl[:, k, :], k == 0, k == KT - 1)
            pe.wait_ge(free67[0], (W_INA + 8) // 2)
            pe.wait_ge(free67[1], (W_INA + 8) // 2)
            pe.wait_ge(v_made, TT)
            pe.wait_ge(p_made, TT)
            for h in range(HA):
                pe.matmul(PS[:, h, 0:256], C("rot"), qT[:, h, 128:T], start=True, stop=True)
                pe.matmul(PS[:, h, 256:512], C("rot"), kT[:, h, 128:T], start=True, stop=True).then_inc(rot_made, 1)
            pe.wait_ge(att_loaded, 64)
            for h in range(HA):
                last = pe.transpose(PS[:, 4, 128 * h:128 * h + 128], ck[:, h, :], C("ident"))
            last.then_inc(ck_turned, 1)
            for h in range(HA):
                last = pe.transpose(PS[:, 5, 128 * h:128 * h + 128], kT[:, h, 0:128], C("ident"))
            last.then_inc(ck_turned, 1)
            for g_ in range(5):
                if g_ < 4:
                    b = 6 + g_ % 2
                    if g_ >= 2:
                        pe.wait_ge(pool_c, g_ - 1)
                    u = Pn[:, :, 128 * g_:128 * g_ + 128]
                    pe.matmul(PS[:, b, 0:128], u[:, 0, :], pm[:, g_, 0:128], start=True, stop=True)
                    pe.matmul(PS[:, b, 128:T], u[:, 1, :], pm[:, g_, 128:384], start=True, stop=False)
                    pe.matmul(PS[:, b, 128:T], u[:, 2, :], pm[:, g_, 384:640], start=False, stop=True
                              ).then_inc(pool_a, 1)
                if g_ >= 1:
                    pe.wait_ge(pool_c, g_)
                    if g_ == 1:
                        pe.wait_ge(ck_copied, 1)
                    if g_ >= 2:
                        pe.wait_ge(pool_s, g_ - 1)
                    pe.matmul(PS[:, 4, 0:T], pw[:, g_ - 1, :], pT, start=True, stop=True).then_inc(pool_b, 1)
            ada = Ada(pe, "pe", None, EARLY)
            for i in range(NU + 3):
                if i < NU:
                    h, qt, r = i // TT, i % TT, i % 2
                    if i == 0:
                        pe.wait_ge(roped, HA)
                        pe.wait_ge(ck_copied, 2)
                    if i >= 1:
                        pe.wait_ge(ex_made, 2 * i)
                    for j in range(2):
                        lhs = qT[64 * j:64 * j + 64, h, 128 * qt:128 * qt + 128]
                        dst = PS[:, j, :]
                        if qt == 0:
                            last = pe.matmul(dst[:, 0:128], lhs, kT[64 * j:64 * j + 64, h, 0:128], start=True, stop=True)
                        else:
                            pe.matmul(dst[:, 0:128], lhs, ckT[64 * j:64 * j + 64, h, :], start=True, stop=True)
                            last = pe.matmul(dst[:, 128:T], lhs, kT[64 * j:64 * j + 64, h, 128:T], start=True, stop=True)
                    last.then_inc(s_made, 1)
                if 0 <= i - 1 < NU:
                    u = i - 1
                    pe.wait_ge(mix_made, u + 1)
                    if u == 0:
                        pe.wait_ge(pool_s, 4)
                    else:
                        pe.wait_ge(at_made, u)
                    for kt in range(1 if u % TT == 0 else TT):
                        last = pe.transpose(PS[:, 2, 128 * kt:128 * kt + 128],
                                            pr[:, u % 2, 0, 128 * kt:128 * kt + 128], C("ident"))
                    last.then_inc(at_turned, 1)
                if 0 <= i - 2 < NU:
                    u = i - 2
                    h, qt = u // TT, u % TT
                    pe.wait_ge(at_made, u + 1)
                    if u == 0:
                        pe.wait_ge(pool_c, 4)
                    else:
                        pe.wait_ge(o_norm, u)
                    dst = PS[:, 3, 0:128]
                    if qt == 0:
                        last = pe.matmul(dst, aT[:, u % 2, 0:128], Vn[:, 0, 128 * h:128 * h + 128], start=True, stop=True)
                    else:
                        pe.matmul(dst, aT[:, u % 2, 0:128], cv[:, h, :], start=True, stop=False)
                        for kt in range(1, TT):
                            last = pe.matmul(dst, aT[:, u % 2, 128 * kt:128 * kt + 128],
                                             Vn[:, kt, 128 * h:128 * h + 128], start=False, stop=(kt == TT - 1))
                    last.then_inc(o_made, 1)
                if 0 <= i - 3 < NU:
                    u = i - 3
                    pe.wait_ge(o_norm, u + 1)
                    if u >= 1:
                        pe.wait_ge(o_hi, u)
                    pe.transpose(PS[:, 4, 0:128], oN[:, u % 2, :], C("ident")
                                 ).then_inc(o_turned, 1)
                ada.units(ADA_EARLY_AT[i])
            ada.finish()

        ADA_EARLY_AT = [2] * 9 + [1] * 6

        def act_mixer0(act, ch, sp_):
            ada = Ada(act, "act", sp_, MID)
            for i, (kind, m) in enumerate(INA_ORDER):
                if kind == "a":
                    ada.units(1)
                    continue
                act.wait_ge(unit_used, U_INA_T + i + 1)
                b, freed, _ = b67(W_INA + m)
                act.activation((qT if m < 4 else kT)[:, m % 4, :], PS[:, b, 0:T], ACT.Copy).then_inc(freed, 1)
                sp_.upto(U_INA_T + i + RING)
                if m == 6:
                    ada.after_last(range(KT))
            sp_.upto(U_ADA_EARLY - 1)
            act.wait_ge(unit_used, U_ADA_EARLY)
            for t in range(TT):
                act.activation(Vn[:, t, :], PS[:, 2 * t, :], ACT.Copy).then_inc(v_made, 1)
            sp_.upto(U_ADA_EARLY + RING - 1)
            act.wait_ge(ck_turned, 1)
            act.activation(ckT.rearrange("p h n -> p (h n)"), PS[:, 4, :], ACT.Copy).then_inc(ck_copied, 1)
            act.wait_ge(ck_turned, 2)
            act.activation(kn.rearrange("p h n -> p (h n)"), PS[:, 5, :], ACT.Copy).then_inc(ck_copied, 1)
            for g_ in range(5):
                if g_ < 4:
                    act.wait_ge(pool_a, g_ + 1)
                    if g_:
                        act.wait_ge(pool_b, g_)
                    act.activation(pT, PS[:, 6 + g_ % 2, 0:T], ACT.Copy).then_inc(pool_c, 1)
                if g_:
                    act.wait_ge(pool_s, g_)
                    act.activation(Hh[:, 3 + g_, :], o32[:, (g_ - 1) % 2, :], ACT.Copy).then_inc(pool_hi, 1)
            log_exp(act)
            ada = Ada(act, "act", sp_, EARLY)
            for i in range(NU + 3):
                if i < NU:
                    r, nk = i % 2, (128 if i % TT == 0 else T)
                    act.wait_ge(mx_made, i + 1)
                    if i >= 2:
                        act.wait_ge(at_turned, i - 1)
                    for j in range(2):
                        act.activation(pr[:, r, j, 0:nk], PS[:, j, 0:nk], ACT.Exp, scale=0.125,
                                       bias=att[:, r, 2 + j:3 + j], accum_out=att[:, r, 4 + j:5 + j]).then_inc(ex_made, 1)
                if 0 <= i - 1 < NU:
                    u = i - 1
                    nk = 128 if u % TT == 0 else T
                    act.wait_ge(at_turned, u + 1)
                    if u >= 2:
                        act.wait_ge(o_made, u - 1)
                    act.activation(aT[:, u % 2, 0:nk], PS[:, 2, 0:nk], ACT.Copy).then_inc(at_made, 1)
                if 0 <= i - 2 < NU:
                    u = i - 2
                    r = u % 2
                    act.wait_ge(o_made, u + 1)
                    if u >= 2:
                        act.wait_ge(o_turned, u - 1)
                    ch.step(act.activation(oN[:, r, :], PS[:, 3, 0:128], ACT.Square,
                                           accum_out=att[:, r, 8:9]))
                    ch.step(act.activation(att[:, r, 9:10], att[:, r, 8:9], ACT.Ln, scale=1.0 / 128,
                                           bias=C("small", 128, 0, 1)))
                    act.activation(att[:, r, 10:11], att[:, r, 9:10], ACT.Exp, scale=-0.5).then_inc(o_sq, 1)
                if 0 <= i - 3 < NU:
                    u = i - 3
                    h, qt, r = u // TT, u % TT, u % 2
                    act.wait_ge(o_turned, u + 1)
                    if u >= 2:
                        act.wait_ge(o_lo, u - 1)
                    else:
                        act.wait_ge(pool_lo, 4)
                    ch.step(act.activation(o32[:, r, 0:128], PS[:, 4, 0:128], ACT.Identity,
                                           scale=ngc[:, 0:1], bias=C("small", 128, 2, 1)))
                    act.activation(Hh[:, h, 128 * qt:128 * qt + 128], o32[:, r, 0:128], ACT.Copy).then_inc(o_hi, 1)
                ada.units(ADA_EARLY_AT[i])
            ada.finish()

        def dve_mixer0(dve, ch, sp_):
            ada = Ada(dve, "dve", sp_, MID, ch)
            for i, (kind, m) in enumerate(INA_ORDER):
                if kind == "a":
                    ada.units(1)
                sp_.upto(U_INA_T + i + RING)
                if (kind, m) == ("t", 6):
                    ada.after_last(range(KT))
            sp_.upto(U_ADA_EARLY - 1)
            dve.wait_ge(unit_used, U_ADA_EARLY)
            for t in range(TT):
                dve.tensor_copy(Pn[:, t, :], PS[:, 2 * t + 1, :]).then_inc(p_made, 1)
            sp_.upto(U_ADA_EARLY + RING - 1)
            qk = BIG[:, 0:2 * HA * T].rearrange("p (s h n) -> p s h n", s=2, h=HA)
            tmp = pr.rearrange("p a b n -> p (a b n)")[:, 0:512].rearrange("p (s n) -> p s n", s=2)
            for h in range(HA):
                dve.wait_ge(rot_made, h + 1)
                x = qk[:, :, h, 128:T]
                dve.tensor_tensor(tmp, PS[:, h, :].rearrange("p (s n) -> p s n", s=2),
                                  C("sin").unsqueeze(1).to_broadcast([128, 2, 256]), ALU.mult)
                ch.step(dve.tensor_tensor(x, x, C("cos").unsqueeze(1).to_broadcast([128, 2, 256]), ALU.mult))
                dve.tensor_tensor(x, x, tmp, ALU.add).then_inc(roped, 1)
                dve.wait_ge(roped, h + 1)
            for g_ in range(4):
                dve.wait_ge(pool_b, g_ + 1)
                dve.tensor_scalar(o32[:, g_ % 2, :], PS[:, 4, 0:T], psc[:, g_:g_ + 1], None,
                                  ALU.mult).then_inc(pool_s, 1)
                dve.wait_ge(pool_hi, g_ + 1)
                dve.tensor_tensor(Hl[:, 4 + g_, :], o32[:, g_ % 2, :], Hh[:, 4 + g_, :].bitcast(f32),
                                  ALU.subtract).then_inc(pool_lo, 1)
            ada = Ada(dve, "dve", sp_, EARLY, ch)
            for i in range(NU + 3):
                if i < NU:
                    r, nk = i % 2, (128 if i % TT == 0 else T)
                    dve.wait_ge(s_made, i + 1)
                    ch.step(dve.tensor_reduce(att[:, r, 0:2], PS[:, 0:2, 0:nk], AX.X, ALU.max))
                    dve.tensor_scalar(att[:, r, 2:4], att[:, r, 0:2], -0.125, None, ALU.mult).then_inc(mx_made, 1)
                    dve.wait_ge(ex_made, 2 * i + 2)
                    ch.step(dve.reciprocal(att[:, r, 6:8], att[:, r, 4:6]))
                    ch.step(dve.tensor_scalar(att[:, r, 7:8], att[:, r, 7:8], lamc[:, 0:1], None, ALU.mult))
                    ch.step(dve.tensor_scalar(pr[:, r, 0, 0:nk], pr[:, r, 0, 0:nk], att[:, r, 6:7], None, ALU.mult))
                    dve.scalar_tensor_tensor(pr[:, r, 0, 0:nk], pr[:, r, 1, 0:nk], att[:, r, 7:8],
                                             pr[:, r, 0, 0:nk], ALU.mult, ALU.add).then_inc(mix_made, 1)
                if 0 <= i - 2 < NU:
                    u = i - 2
                    r = u % 2
                    dve.wait_ge(o_sq, u + 1)
                    dve.tensor_scalar(oN[:, r, :], PS[:, 3, 0:128], att[:, r, 10:11], None,
                                      ALU.mult).then_inc(o_norm, 1)
                if 0 <= i - 3 < NU:
                    u = i - 3
                    h, qt, r = u // TT, u % TT, u % 2
                    dve.wait_ge(o_hi, u + 1)
                    dve.tensor_tensor(Hl[:, h, 128 * qt:128 * qt + 128], o32[:, r, 0:128],
                                      Hh[:, h, 128 * qt:128 * qt + 128].bitcast(f32), ALU.subtract).then_inc(o_lo, 1)
                ada.units(ADA_EARLY_AT[i])
            ada.finish()

        def pe_out(pe, first):
            for k in range(KT):
                n_product(pe, first + k, Hh[:, k, :], Hl[:, k, :], k == 0, k == KT - 1)

        def pe_ffn(pe):
            pe.wait_ge(hl_made, 2 * TT)
            pe.wait_ge(modc_read, cols_before(EARLY[1]))
            for kind, c in FFN_ORDER:
                n = FFN_AT[kind, c]
                if kind == "d":
                    if c == 0:
                        pe.wait_ge(h32_act, 2 * TT)
                        pe.wait_ge(h32_dve, 2 * TT)
                    pe.wait_ge(gul_made, c + 1)
                    n_product(pe, n, gu_h[:, c % 2, :], gu_l[:, c % 2, :], c == 0, c == FC - 1)
                else:
                    t_product(pe, n, W_FFN + 2 * c + (kind == "u"))

        def act_ffn(act, ch, sp_):
            for c in range(FC):
                act.wait_ge(unit_used, FFN_AT["g", c] + 1)
                if c >= 2:
                    act.wait_ge(guh_made, c - 1)
                    act.wait_ge(gul_made, c - 1)
                b, freed, _ = b67(W_FFN + 2 * c)
                act.activation(ftmp[:, c % 2, :], PS[:, b, 0:T], ACT.Silu).then_inc(freed, 1)
                sp_.upto(FFN_AT["g", c] + RING)
                act.wait_ge(free67[1], (W_FFN + 2 * c + 1) // 2 + 1)
                act.activation(gu_h[:, c % 2, :], ftmp[:, c % 2, :], ACT.Copy).then_inc(guh_made, 1)
                sp_.upto(FFN_AT["u", c] + RING)
            sp_.upto(FFN_AT["d", FC - 1] + RING)

        def dve_ffn(dve, ch, sp_):
            for c in range(FC):
                sp_.upto(FFN_AT["g", c] + RING)
                dve.wait_ge(unit_used, FFN_AT["u", c] + 1)
                dve.wait_ge(free67[0], (W_FFN + 2 * c) // 2 + 1)
                b, freed, _ = b67(W_FFN + 2 * c + 1)
                dve.tensor_tensor(ftmp[:, c % 2, :], ftmp[:, c % 2, :], PS[:, b, 0:T], ALU.mult).then_inc(freed, 1)
                dve.wait_ge(freed, (W_FFN + 2 * c + 1) // 2 + 1)
                dve.wait_ge(guh_made, c + 1)
                dve.tensor_tensor(gu_l[:, c % 2, :], ftmp[:, c % 2, :], gu_h[:, c % 2, :].bitcast(f32),
                                  ALU.subtract).then_inc(gul_made, 1)
                sp_.upto(FFN_AT["u", c] + RING)
            sp_.upto(FFN_AT["d", FC - 1] + RING)

        gates_mm = sem("gates_mm")
        wg_in = sem("wg_in")
        wg_cut = sem("wg_cut")
        n0_in = sem("n0_in")
        ones_set = sem("ones_set")
        gi_made = sem("gi_made")
        nab_made = sem("nab_made")
        soft_made = sem("soft_made")
        rows_made = sem("rows_made")
        rows_exp = sem("rows_exp")
        nat_turned = sem("nat_turned")
        nat_copied = sem("nat_copied")
        v1_act = sem("v1_act")
        v1_dve = sem("v1_dve")
        m_out = sem("m_out")
        st_made = sem("st_made")
        d_made = sem("d_made")
        wb_made = sem("wb_made")
        e_made = sem("e_made")
        qw_made = sem("qw_made")
        p_done = sem("p_done")
        km_turned = sem("km_turned")
        kw_made = sem("kw_made")
        cn_in = [sem("cn_in0"), sem("cn_in1")]
        cn_col = sem("cn_col")
        num_made = sem("num_made")
        rd_done = sem("rd_done")
        c_made = sem("c_made")
        co_made = sem("co_made")
        c_out = [sem("c_out0"), sem("c_out1")]
        hvar = sem("hvar")
        hrstd = sem("hrstd")
        hn_made = sem("hn_made")
        ht_turned = sem("ht_turned")
        ht_made = sem("ht_made")
        mh_hi = sem("mh_hi")
        mh_lo = sem("mh_lo")
        nf_turned = sem("nf_turned")
        nf_made = sem("nf_made")
        minus_hi = sem("minus_hi")
        minus_lo = sem("minus_lo")
        SCL = 128.0 ** -0.5
        nmh, nml = gu_h[0:16, 0, :], gu_l[0:16, 0, :]
        wih, wil = gu_h[0:16, 1, 0:256], gu_l[0:16, 1, 0:256]
        KEYS = {0: ((0, 0, 128), (1, 128, 384), (2, 384, 512)), 1: ((0, 0, 128), (1, 128, 256), (2, 256, 512))}

        def unit(u):
            h, d = u // 2, u % 2
            return h, d, 8 * d + h

        def pe_mixer1(pe):
            pe.wait_ge(h32_act, 3 * TT)
            pe.wait_ge(h32_dve, 3 * TT)
            pe.wait_ge(wg_cut, 2)
            for dst, w in ((4, wgi), (5, wgf)):
                for k in range(KT):
                    last = pe.matmul(PS[0:16, dst, 0:T], w[:, k, :], H32[:, k, :], start=(k == 0), stop=(k == KT - 1))
            last.then_inc(gates_mm, 1)
            pe.wait_ge(hl_made, 3 * TT)
            ada = Ada(pe, "pe", None, LATE)
            for i, (kind, m) in enumerate(INC_ORDER):
                if kind == "a":
                    ada.units(1)
                else:
                    t_product(pe, U_INC_T + i, W_INC + m)
                    if m >= 20:
                        ada.after_last([m - 18])
            pe.wait_ge(rows_exp, 3)
            pe.wait_ge(n0_in, 16)
            rows = [(g[0], t) for t in range(TT)] + [(g[4], t) for t in range(TT)] + [(g[5], 0), (n0r, 0)]
            for i, (x, t) in enumerate(rows):
                last = pe.transpose(PS[:, 3, 16 * i:16 * i + 16], x[:, 128 * t:128 * t + 128], C("ident", 16, 0, 16))
            last.then_inc(nat_turned, 1)
            pe.wait_ge(nat_copied, 1)
            pe.wait_ge(gate_made, 4 * len(GATES))
            for k in range(KT):
                n_product(pe, U_INC_N + k, Hh[:, k, :], Hl[:, k, :], k == 0, k == KT - 1)
            pe.wait_ge(minus_lo, 2)
            for i in range(NM + 3):
                if i < NM:
                    h, d, r = unit(i)
                    if d == 0:
                        if i == 0:
                            for b in range(2):
                                pe.wait_ge(free67[b], (W_INC + 24) // 2)
                            pe.wait_ge(v1_act, TT)
                            pe.wait_ge(v1_dve, TT)
                            pe.wait_ge(ones_set, 1)
                        else:
                            pe.wait_ge(p_done, i)
                        pe.matmul(PS[:, 0, 0:128], kM[:, h, 0:128], qM[:, h, 0:128], start=True, stop=True)
                        pe.matmul(PS[:, 0, 128:T], kM[:, h, 128:256], qM[:, h, 128:T], start=True, stop=True)
                        pe.matmul(PS[:, 1, 0:256], kM[:, h, 256:T], qM[:, h, 128:T], start=True, stop=True
                                  ).then_inc(st_made, 1)
                    if i >= 1:
                        pe.wait_ge(e_made, i)
                    row = cr[0:16, 0, r:r + 1].to_broadcast([16, 128])
                    spans = ((0, 384, 0), (384, 512, 256)) if d == 0 else ((0, 256, 0), (256, 512, 128))
                    for lo, hi, tok in spans:
                        for part in (nmh, nml):
                            pe.matmul(PS[:, 2, lo:hi], row, part[:, tok:tok + hi - lo],
                                      start=(lo == 0 and part is nmh), stop=False, skip_group_check=True)
                    for lo in (0, 128, 384):
                        last = pe.matmul(PS[:, 2, lo:lo + 128], cr[:, 0, :], cr[:, 1 + d, :],
                                         start=False, stop=(lo == 384), skip_group_check=True)
                    last.then_inc(d_made, 1)
                    if i >= 1:
                        pe.wait_ge(qw_made, i)
                    pe.matmul(PS[:, 4, 0:256], row, wih, start=True, stop=False)
                    pe.matmul(PS[:, 4, 0:256], row, wil, start=False, stop=True).then_inc(wb_made, 1)
                if 0 <= i - 1 < NM:
                    u = i - 1
                    h, d, r = unit(u)
                    pe.wait_ge(p_done, u + 1)
                    pe.wait_ge(cn_in[d], 16 * (h + 1))
                    pe.wait_ge(cn_col, u + 1)
                    if u >= 1:
                        pe.wait_ge(rd_done, u)
                    P_ = E[:, u % 2, :]
                    b = 3
                    spans = (((0, 0, 0),), ((128, 1, 0),), ((256, 1, 1), (384, 2, 1))) if d == 0 else \
                        (((0, 0, 0),), ((128, 1, 0), (256, 2, 0)), ((384, 2, 1),))
                    for t in range(TT):
                        dst = PS[:, b, 129 * t:129 * t + 129]
                        for j, (col, key, _) in enumerate(spans[t]):
                            last = pe.matmul(dst, P_[:, col:col + 128], V1[:, key, h, :], start=(j == 0),
                                             stop=(t == 0))
                        if t:
                            last = pe.matmul(dst, qw[:, d, 128 * (t - 1):128 * t], CN[:, d, :], start=False, stop=True)
                    last.then_inc(num_made, 1)
                    pe.wait_ge(kw_made, h + 1)
                    if u % 2 == 1:
                        pe.wait_ge(co_made, u)
                    if u % 2 == 1 and h >= 1:
                        pe.wait_ge(ht_made, h)
                    pe.matmul(PS[:, 7, 0:129], kw[:, d, :], V1[:, 0, h, :], start=True, stop=True).then_inc(c_made, 1)
                if i < NM and i % 2 == 0:
                    h = i // 2
                    if h:
                        pe.wait_ge(co_made, 2 * h)
                    pe.transpose(PS[:, 7, 0:128], kM[:, h, 0:128], C("ident")).then_inc(km_turned, 1)
                if i >= 3 and i % 2 == 1:
                    h = (i - 3) // 2
                    pe.wait_ge(hn_made, h + 1)
                    pe.wait_ge(co_made, min(i, NM))
                    for t in range(TT):
                        last = pe.transpose(PS[:, 7, 128 * t:128 * t + 128], hn[:, t, :], C("ident"))
                    last.then_inc(ht_turned, 1)
            pe.wait_ge(ht_made, HM)
            pe.transpose(PS[0:16, 7, 0:128], nfin, C("ident")).then_inc(nf_turned, 1)

        def act_rows_a(act, ch):
            act.wait_ge(gates_mm, 1)
            act.activation(g[0], PS[0:16, 4, 0:T], ACT.Identity, bias=bgi[:, 0:1]).then_inc(gi_made, 1)

        def act_rows_b(act, ch):
            act.wait_ge(nab_made, 1)
            ch.step(act.activation(g[2], g[2], ACT.Exp))
            act.activation(g[2], g[2], ACT.Ln, bias=C("small", 16, 1, 1)).then_inc(soft_made, 1)

        def act_rows_c(act, ch):
            act.wait_ge(rows_made, 1)
            act.activation(g[4], g[3], ACT.Exp, scale=-1.0).then_inc(rows_exp, 1)
            act.activation(wint, g[2][:, 128:T], ACT.Exp, scale=-1.0, bias=m0c[:, 0:1]).then_inc(rows_exp, 1)
            act.activation(g[5][:, 0:128], g[0][:, 0:128], ACT.Exp, bias=gm[:, 1:2]).then_inc(rows_exp, 1)
            act.activation(nmh, negM, ACT.Copy).then_inc(minus_hi, 1)
            act.wait_ge(rows_exp, 2)
            act.activation(wih, wint, ACT.Copy).then_inc(minus_hi, 1)

        def dve_rows(dve, ch, sp_):
            F, B_ = C("dir", 16, 0, 1), C("dir", 16, 1, 1)
            one = C("small", 16, 1, 1)
            dve.wait_ge(gates_mm, 1)
            ch.step(dve.tensor_scalar(g[1], PS[0:16, 5, 0:T], bgf[:, 0:1], None, ALU.add))
            ch.step(dve.tensor_scalar(g[2], g[1], -1.0, None, ALU.mult))
            dve.tensor_tensor(g[2], g[2], g[1], ALU.min).then_inc(nab_made, 1)
            sp_.upto(U_INC_T + RING)
            dve.wait_ge(soft_made, 1)
            ch.step(dve.scalar_tensor_tensor(g[1], g[1], 0.0, g[2], ALU.min, ALU.subtract))

            def scans(op0, src, start, ones):
                for lo, hi, st_ in ((0, 128, 0.0), (128, T, start)):
                    d0 = one.to_broadcast([16, hi - lo]) if ones else src[:, lo:hi]
                    last = dve.tensor_tensor_scan(g[3][:, lo:hi], d0, src[:, lo:hi], st_, op0[0], op0[1])
                    back = slice(hi - 1, lo - 1 if lo else None, -1)
                    d0 = one.to_broadcast([16, hi - lo]) if ones else src[:, back]
                    last = dve.tensor_tensor_scan(g[4][:, back], d0, src[:, back], st_, op0[0], op0[1])
                ch.step(last)

            def pick(dst):
                ch.step(dve.tensor_scalar(g[3], g[3], F, None, ALU.mult))
                ch.step(dve.scalar_tensor_tensor(dst, g[4], B_, g[3], ALU.mult, ALU.add))

            scans((ALU.mult, ALU.add), g[1], 0.0, True)
            pick(g[1])
            dve.wait_ge(gi_made, 1)
            ch.step(dve.tensor_tensor(g[0], g[0], g[1], ALU.subtract))
            scans((ALU.max, ALU.max), g[0], m0c[:, 0:1], False)
            pick(g[2])
            dve.tensor_scalar(negM, g[2], -1.0, None, ALU.mult)
            ch.step(dve.tensor_tensor(g[3], g[1], g[2], ALU.add))
            for dst, src in ((0, g[2]), (2, g[3])):
                ch.step(dve.tensor_scalar(gm[:, dst:dst + 1], src[:, 127:128], F, None, ALU.mult))
                ch.step(dve.scalar_tensor_tensor(gm[:, dst:dst + 1], src[:, 0:1], B_, gm[:, dst:dst + 1],
                                                 ALU.mult, ALU.add))
            dve.tensor_scalar(gm[:, 1:2], gm[:, 0:1], -1.0, None, ALU.mult).then_inc(rows_made, 1)

        def act_mixer1(act, ch, sp_):
            act_rows_a(act, ch)
            ada = Ada(act, "act", sp_, LATE)
            for i, (kind, m) in enumerate(INC_ORDER):
                if kind == "a":
                    ada.units(1)
                    continue
                act.wait_ge(unit_used, U_INC_T + i + 1)
                b, freed, _ = b67(W_INC + m)
                dst = (qM, kM, sg)[m // 8][:, m % 8, :]
                if m >= 16:
                    act.activation(dst, PS[:, b, 0:T], ACT.Sigmoid).then_inc(freed, 1)
                else:
                    act.activation(dst, PS[:, b, 0:T], ACT.Copy, scale=(1.0, SCL)[m // 8]).then_inc(freed, 1)
                sp_.upto(U_INC_T + i + RING)
                if m >= 20:
                    ada.after_last([m - 18])
                if m == 0:
                    act_rows_b(act, ch)
                if m == 4:
                    act_rows_c(act, ch)
            sp_.upto(U_OUTC - 1)
            act.wait_ge(unit_used, U_OUTC)
            act.wait_ge(x_done, 2 * TT)
            for t in range(TT):
                act.activation(V1[:, t, 0:4, 0:128], PS[:, 2 * t, :].rearrange("p (h n) -> p h n", h=4),
                               ACT.Copy).then_inc(v1_act, 1)
            sp_.upto(U_OUTC + RING - 1)
            log_exp(act)
            act.wait_ge(nat_copied, 1)
            for i in range(NM + 3):
                if i < NM:
                    h, d, r = unit(i)
                    act.wait_ge(d_made, i + 1)
                    if i >= 2:
                        act.wait_ge(num_made, i - 1)
                    for t, lo, hi in KEYS[d]:
                        last = act.activation(E[:, i % 2, lo:hi], PS[:, 2, lo:hi], ACT.Exp,
                                              bias=nat[:, t, r:r + 1])
                    last.then_inc(e_made, 1)
                if 0 <= i - 1 < NM:
                    u = i - 1
                    h, d, r = unit(u)
                    act.wait_ge(c_made, u + 1)
                    if u >= 2:
                        act.wait_ge(c_out[d], 16 * h)
                    act.activation(Co[:, d, 0:128], PS[:, 7, 0:128], ACT.Copy)
                    act.activation(nfin[:, r:r + 1], PS[:, 7, 128:129], ACT.Copy).then_inc(co_made, 1)
                if i >= 2 and i % 2 == 0 and i // 2 <= HM:
                    h = i // 2 - 1
                    act.wait_ge(hvar, h + 1)
                    ch.step(act.activation(hrs, hmv[:, :, 1], ACT.Ln, bias=C("small", 128, 0, 1)))
                    act.activation(hrs, hrs, ACT.Exp, scale=-0.5).then_inc(hrstd, 1)
                if i >= 3 and i % 2 == 1:
                    h = (i - 3) // 2
                    act.wait_ge(ht_made, h + 1)
                    act.activation(Hh[:, h, :], ht, ACT.Copy).then_inc(mh_hi, 1)
            act.wait_ge(nf_turned, 1)
            act.activation(nfT, PS[0:16, 7, 0:128], ACT.Copy).then_inc(nf_made, 1)

        def dve_mixer1(dve, ch, sp_):
            dve_rows(dve, ch, sp_)
            ada = Ada(dve, "dve", sp_, LATE, ch)
            for i, (kind, m) in enumerate(INC_ORDER):
                if kind == "a":
                    ada.units(1)
                sp_.upto(U_INC_T + i + RING)
            for src, hi, lo in ((negM, nmh, nml), (wint, wih, wil)):
                dve.wait_ge(minus_hi, 2)
                dve.tensor_tensor(lo, src, hi.bitcast(f32), ALU.subtract).then_inc(minus_lo, 1)
            dve.wait_ge(nat_turned, 1)
            dve.tensor_copy(nat.rearrange("p a b -> p (a b)"), PS[:, 3, 0:128]).then_inc(nat_copied, 1)
            sp_.upto(U_OUTC - 1)
            dve.wait_ge(unit_used, U_OUTC)
            dve.wait_ge(x_done, 2 * TT)
            for t in range(TT):
                dve.tensor_copy(V1[:, t, 4:8, 0:128], PS[:, 2 * t + 1, :].rearrange("p (h n) -> p h n", h=4)
                                ).then_inc(v1_dve, 1)
            sp_.upto(U_OUTC + RING - 1)
            dve.wait_ge(nat_copied, 1)
            for i in range(NM + 3):
                if i < NM:
                    h, d, r = unit(i)
                    dve.wait_ge(wb_made, i + 1)
                    if i >= 2:
                        dve.wait_ge(num_made, i - 1)
                    dve.tensor_tensor(qw[:, d, :], PS[:, 4, 0:256], qM[:, h, 128:T], ALU.mult).then_inc(qw_made, 1)
                    dve.wait_ge(st_made, h + 1)
                    dve.wait_ge(e_made, i + 1)
                    e = E[:, i % 2, :]
                    if d == 0:
                        dve.tensor_tensor(e[:, 0:384], e[:, 0:384], PS[:, 0, 0:384], ALU.mult)
                        last = dve.tensor_tensor(e[:, 384:512], e[:, 384:512], PS[:, 1, 128:256], ALU.mult)
                    else:
                        dve.tensor_tensor(e[:, 0:256], e[:, 0:256], PS[:, 0, 0:256], ALU.mult)
                        last = dve.tensor_tensor(e[:, 256:512], e[:, 256:512], PS[:, 1, 0:256], ALU.mult)
                    last.then_inc(p_done, 1)
                    if d == 0:
                        dve.wait_ge(km_turned, h + 1)
                        dve.tensor_scalar(kw[:, 0, :], PS[:, 7, 0:128], nat[:, 6, h:h + 1], None, ALU.mult)
                        dve.tensor_scalar(kw[:, 1, :], PS[:, 7, 0:128], nat[:, 6, 8 + h:9 + h], None,
                                          ALU.mult).then_inc(kw_made, 1)
                if 0 <= i - 1 < NM:
                    u = i - 1
                    h, d, r = unit(u)
                    dve.wait_ge(num_made, u + 1)
                    num = PS[:, 3, 0:387].rearrange("p (t n) -> p t n", t=TT)
                    den = rd[:, d, :].unsqueeze(2)
                    ch.step(dve.tensor_scalar(den, num[:, :, 128:129], -1.0, None, ALU.mult))
                    ch.step(dve.tensor_tensor(den, den, num[:, :, 128:129], ALU.max))
                    ch.step(dve.tensor_tensor(den, den, nat[:, 3:6, r:r + 1], ALU.max))
                    ch.step(dve.reciprocal(den, den))
                    rb = den.to_broadcast([128, TT, 128])
                    if d == 0:
                        dve.tensor_tensor(hs, num[:, :, 0:128], rb, ALU.mult).then_inc(rd_done, 1)
                    else:
                        if h:
                            dve.wait_ge(mh_hi, h)
                        ht3 = ht.rearrange("p (t n) -> p t n", t=TT)
                        dve.tensor_tensor(ht3, num[:, :, 0:128], rb, ALU.mult).then_inc(rd_done, 1)
                        dve.wait_ge(rd_done, u + 1)
                        ch.step(dve.tensor_tensor(hs, hs, ht3, ALU.add))
                        for t in range(TT):
                            last = dve.bn_stats(hst[:, t, :], hs[:, t, :])
                        ch.step(last)
                        for t in range(TT):
                            last = dve.bn_aggr(hmv[:, t, :], hst[:, t, :])
                        last.then_inc(hvar, 1)
                        dve.wait_ge(hrstd, h + 1)
                        if h:
                            dve.wait_ge(ht_turned, h)
                        for t in range(TT):
                            last = dve.tensor_scalar(hn[:, t, :], hs[:, t, :], hmv[:, t, 0:1], hrs[:, t:t + 1],
                                                     ALU.subtract, ALU.mult)
                        last.then_inc(hn_made, 1)
                if i >= 3 and i % 2 == 1:
                    h = (i - 3) // 2
                    dve.wait_ge(ht_turned, h + 1)
                    dve.scalar_tensor_tensor(ht, PS[:, 7, 0:T], hgc[:, h:h + 1], sg[:, h, :], ALU.mult,
                                             ALU.mult).then_inc(ht_made, 1)
                    dve.wait_ge(mh_hi, h + 1)
                    dve.tensor_tensor(Hl[:, h, :], ht, Hh[:, h, :].bitcast(f32), ALU.subtract).then_inc(mh_lo, 1)

        def pool_gates_load(pool):
            pool.dma_start(wg, a["w_in_c"][0][:, 4 * D:4 * D + 32].rearrange("(k p) n -> p k n", p=128)
                           ).then_inc(wg_in, 16)
            pool.dma_start(n0r, a["state_n"][0, 0].rearrange("d h n -> (d h) n")).then_inc(n0_in, 16)
            pool.wait_ge(wg_in, 16)
            w5 = wg.rearrange("p k (d s h) -> p k d s h", d=2, s=2)
            for s_, dst in ((0, wgi), (1, wgf)):
                pool.tensor_copy(dst.rearrange("p k (d h) -> p k d h", d=2), w5[:, :, :, s_, :]).then_inc(wg_cut, 1)

        def pool_mixer1(pool, ch):
            pool.wait_ge(gates_mm, 1)
            pool.wait_ge(x_done, 2 * TT)
            pool.memset(V1[:, :, :, 128:129], 1.0).then_inc(ones_set, 1)
            pool.wait_ge(rows_made, 1)
            pool.dma_start(out["m"][0, 0].rearrange("d (h a) -> (d h) a", a=1), gm[:, 2:3]).then_inc(m_out, 16)
            pool.wait_ge(m_out, 16)
            pool.wait_ge(nat_copied, 1)

            def start_state(u):
                h, d, r = unit(u)
                if u >= 2:
                    pool.wait_ge(num_made, u - 1)
                pool.dma_start(CN[:, d, 0:128], a["state_C"][0, 0, d, h]).then_inc(cn_in[d], 16)
                pool.tensor_copy(CN[:, d, 128:129], nat[:, 7, r:r + 1]).then_inc(cn_col, 1)

            start_state(0)
            start_state(1)
            for u in range(NM):
                h, d, r = unit(u)
                pool.wait_ge(co_made, u + 1)
                pool.dma_start(out["C"][0, 0, d, h], Co[:, d, 0:128]).then_inc(c_out[d], 16)
                if u + 2 < NM:
                    start_state(u + 2)
            pool.wait_ge(nf_made, 1)
            pool.dma_start(out["n"][0, 0].rearrange("d h n -> (d h) n"), nfT).then_inc(m_out, 16)

        hn_turned = sem("hn_turned")
        hn_copied = sem("hn_copied")
        logit_made = sem("logit_made")
        gap_made = sem("gap_made")
        gap_exp = sem("gap_exp")
        chosen = sem("chosen")
        rank_made = sem("rank_made")
        slots_made = sem("slots_made")
        scattered = sem("scattered")
        tok_in = sem("tok_in")
        tok_turned = sem("tok_turned")
        hsh_made = sem("hsh_made")
        hsl_made = sem("hsl_made")
        esilu_made = sem("esilu_made")
        eprod_made = sem("eprod_made")
        etr_made = sem("etr_made")
        eguh_made = sem("eguh_made")
        egul_made = sem("egul_made")
        y_made = sem("y_made")
        yb_free = sem("yb_free")
        y_out = sem("y_out")
        y_back = [sem(f"y_back{t}") for t in range(TT)]
        y_mixed = sem("y_mixed")
        x_last = sem("x_last")
        sp_pass = sem("sp_pass")
        pool_pass = sem("pool_pass")
        E_ORDER = [("gu", 0, q) for q in range(4)]
        for c in range(1, MC):
            E_ORDER += [("gu", c, q) for q in range(4)]
            if c < MC - 1:
                E_ORDER += [("dn", c - 1, q) for q in range(2)]
        E_ORDER += [("dn", c, q) for c in (MC - 2, MC - 1) for q in range(2)]
        assert len(E_ORDER) == UB
        slot = lambda v: (U_MOE + v) % RING
        FILLS = [sum(1 for n in range(U_MOE) if n % RING == s) for s in range(RING)]

        def pe_route(pe):
            for t in range(TT):
                wait_h32(pe, 3, t)
                for k in range(KT):
                    last = pe.matmul(PS[:, 0, NE * t:NE * t + NE], H32[:, k, 128 * t:128 * t + 128], rwt[:, k, :],
                                     start=(k == 0), stop=(k == KT - 1))
            last.then_inc(logit_made, 1)
            for i in range(6):
                t, half = i // 2, i % 2
                for k in range(4):
                    last = pe.transpose(PS[:, 2 + i, 128 * k:128 * k + 128],
                                        H32[:, 4 * half + k, 128 * t:128 * t + 128], C("ident"))
                last.then_inc(hn_turned, 1)
            pe.wait_ge(chosen, 1)
            for t in range(TT):
                for j in range(t + 1):
                    pe.matmul(PS[:, 1, NE * t:NE * t + NE], C("strict" if j == t else "ones"), asum[:, j, :],
                              start=(j == 0), stop=(j == t))
            for j in range(TT):
                last = pe.matmul(PS[:, 1, 3 * NE:4 * NE], C("ones"), asum[:, j, :], start=(j == 0), stop=(j == TT - 1))
            last.then_inc(rank_made, 1)

        def act_route(act, ch):
            for i in range(6):
                t, half = i // 2, i % 2
                act.wait_ge(hn_turned, i + 1)
                act.activation(Hn[:, t, 512 * half:512 * half + 512], PS[:, 2 + i, :], ACT.Copy).then_inc(hn_copied, 1)
            act.wait_ge(gap_made, 1)
            act.activation(e2[:, :, 1:2], e2[:, :, 0:1], ACT.Exp).then_inc(gap_exp, 1)

        def dve_route(dve, ch):
            bc3 = lambda x: x.unsqueeze(1).to_broadcast([128, TT, NE])
            dve.wait_ge(logit_made, 1)
            ch.step(dve.tensor_tensor(lg, PS[:, 0, 0:3 * NE].rearrange("p (t e) -> p t e", t=TT), bc3(rbb[:, :]),
                                      ALU.add))
            for t in range(TT):
                last = dve.max(top8[:, t, :], lg[:, t, :])
            ch.step(last)
            dve.tensor_tensor(e2[:, :, 0:1], top8[:, :, 1:2], top8[:, :, 0:1], ALU.subtract).then_inc(gap_made, 1)
            for t in range(TT):
                last = dve.max_index(idx_u[:, t, :], top8[:, t, :], lg[:, t, :])
            ch.step(last)
            ch.step(dve.tensor_copy(idxf, idx_u[:, :, :]))
            for kk in range(2):
                for t in range(TT):
                    last = dve.tensor_scalar(oh[:, kk, t, :], C("iota8"), idxf[:, t, kk:kk + 1], None, ALU.is_equal)
            ch.step(last)
            dve.tensor_tensor(asum, oh[:, 0], oh[:, 1], ALU.add).then_inc(chosen, 1)
            dve.wait_ge(gap_exp, 1)
            ch.step(dve.tensor_scalar(wts[:, :, 1:2], e2[:, :, 1:2], 1.0, None, ALU.add))
            ch.step(dve.reciprocal(wts[:, :, 0:1], wts[:, :, 1:2]))
            ch.step(dve.tensor_tensor(wts[:, :, 1:2], wts[:, :, 0:1], e2[:, :, 1:2], ALU.mult))
            dve.wait_ge(rank_made, 1)
            ch.step(dve.tensor_copy(bb[:, 0, :], PS[:, 1, 3 * NE:4 * NE]))
            ch.step(dve.tensor_scalar(bb[:, 1, :], bb[:, 0, :], 0.0, None, ALU.is_gt))
            for least in (128.0, 256.0):
                ch.step(dve.scalar_tensor_tensor(bb[:, 1, :], bb[:, 0, :], least, bb[:, 1, :], ALU.is_gt, ALU.add))
            ch.step(dve.tensor_scalar(bb[:, 1, 0:1], bb[:, 1, 0:1], 1.0, None, ALU.max))
            ch.step(dve.tensor_tensor_scan(bb[:, 2, :], C("small", 128, 1, 1).to_broadcast([128, NE]), bb[:, 1, :],
                                           0.0, ALU.mult, ALU.add))
            ch.step(dve.tensor_tensor(bb[:, 3, :], bb[:, 2, :], bb[:, 1, :], ALU.subtract))
            ch.step(dve.scalar_tensor_tensor(rk, bc3(bb[:, 3, :]), 128.0,
                                             PS[:, 1, 0:3 * NE].rearrange("p (t e) -> p t e", t=TT), ALU.mult, ALU.add))
            for kk in range(2):
                last = dve.tensor_tensor(wk[:, kk], oh[:, kk], rk, ALU.mult)
            ch.step(last)
            for kk in range(2):
                last = dve.tensor_reduce(slf[:, :, kk:kk + 1], wk[:, kk], AX.X, ALU.add)
            ch.step(last)
            dve.tensor_copy(slot_u[:, :, :], slf)
            ch.step(dve.tensor_tensor(eid, C("iota16", 1).unsqueeze(2).to_broadcast([1, 16, NE]),
                                      bb[0:1, 2, :].unsqueeze(1).to_broadcast([1, 16, NE]), ALU.is_ge))
            ch.step(dve.tensor_reduce(ctl_f[0:1, 1:17].unsqueeze(2), eid, AX.X, ALU.add))
            ch.step(dve.tensor_scalar(ctl_f[0:1, 1:17], ctl_f[0:1, 1:17], float(NE - 1), None, ALU.min))
            ch.step(dve.tensor_copy(ctl_f[0:1, 0:1], bb[0:1, 2, NE - 1:NE]))
            dve.tensor_copy(ctl[:, :], ctl_f[:, :]).then_inc(slots_made, 1)

        def blocks(eng):
            eng.wait_ge(slots_made, 1)
            return eng.value_load(ctl[0:1, 0:1], min_val=1, max_val=NBMAX)

        def sp_experts(sp):

            def load(e, v):
                kind, c, q = E_ORDER[v]
                s = slot(v)
                if kind == "gu":
                    for side in range(2):
                        src = a["moe_w_gu"][0, bass.ds(e, 1), 256 * q:256 * q + 256,
                                            FE * side + 256 * c:FE * side + 256 * c + 256]
                        dst = raw[:, s, :].rearrange("p (k n) -> p k n", k=2)[:, :, 256 * side:256 * side + 256]
                        yield dst, src.rearrange("a (k p) n -> p (a k) n", p=128)
                else:
                    row = 256 * c + 128 * q
                    yield raw[:, s, :], a["moe_w_down"][0, bass.ds(e, 1), row:row + 128, :].rearrange("a p n -> p (a n)")

            def fill(v, j, e):
                sp.wait_ge(lo_made, j * UB + (U_MOE - RING + v + 1))
                if v == UB:
                    sp.sem_inc(sp_pass, 1)
                for dst, src in load(e, v % UB):
                    sp.dma_start(dst, src).then_inc(raw_full[slot(v)], 16)

            for v in range(2 * RING):
                fill(v, 0, 0)
            nb = blocks(sp)
            with sp.Fori(0, nb - 1) as j:
                e = sp.value_load(ctl[0:1, bass.ds(j + 1, 1)], min_val=0, max_val=NE - 1)
                en = sp.value_load(ctl[0:1, bass.ds(j + 2, 1)], min_val=0, max_val=NE - 1)
                for v in range(2 * RING, UB + 2 * RING):
                    fill(v, j, e if v < UB else en)
            with sp.Fori(nb - 1, nb) as j:
                e = sp.value_load(ctl[0:1, bass.ds(j + 1, 1)], min_val=0, max_val=NE - 1)
                for v in range(2 * RING, UB + RING):
                    fill(v, j, e)

        def full_value(v):
            s = slot(v)
            per = [32 if E_ORDER[x][0] == "gu" else 16 for x in range(UB)]
            total = sum(per[x] for x in range(UB) if slot(x) == s)
            here = sum(per[x] for x in range(v % UB + 1) if slot(x) == s)
            return 16 * FILLS[s] + here + (total if v >= UB else 0), total

        def act_unit_hi(act, v, j=None):
            s = slot(v)
            first, per = full_value(v)
            if j is None:
                act.wait_ge(unit_used, U_MOE - RING + v + 1)
            act.wait_ge(raw_full[s], j * per + first if j is not None else first)
            act.activation(whi[:, s, :], raw[:, s, :], ACT.Copy).then_inc(hi_made, 1)

        def dve_unit_lo(dve, v, j=None):
            s = slot(v)
            dve.wait_ge(hi_made, j * UB + (U_MOE + v + 1) if j is not None else U_MOE + v + 1)
            dve.tensor_tensor(wlo[:, s, :], raw[:, s, :], whi[:, s, :].bitcast(f32), ALU.subtract).then_inc(lo_made, 1)

        def act_experts(act):
            nb = blocks(act)

            def tokens(j):
                act.wait_ge(tok_turned, j + 1)
                for b in range(2):
                    act.activation(Hh[:, 4 * b:4 * b + 4, 0:128],
                                   PS[:, 4 + b, :].rearrange("p (k n) -> p k n", k=4), ACT.Copy).then_inc(hsh_made, 1)

            def product_hi(c, j):
                act.wait_ge(etr_made, j * MC + (c + 1))
                act.activation(gu_h[:, c % 2, 0:256], PS[:, 6 + c % 2, 0:256], ACT.Copy).then_inc(eguh_made, 1)

            tokens(0)
            with act.Fori(0, nb) as j:
                for w, (kind, c, q) in enumerate(E_ORDER):
                    act.wait_ge(unit_used, j * UB + (U_MOE + w + 1))
                    act_unit_hi(act, w + RING, j)
                    if kind == "gu" and q == 3:
                        act.activation(gp[:, c % 2, 0:256], PS[:, c % 2, 0:256], ACT.Silu).then_inc(esilu_made, 1)
                        if c == MC - 1:
                            tokens(j + 1)
                    if kind == "gu" and q == 1 and c >= 1:
                        product_hi(c - 1, j)
                    if kind == "dn" and q == 0 and c == MC - 2:
                        product_hi(MC - 1, j)
                act.wait_ge(yb_free, j + 1)
                act.activation(yb.rearrange("p (a n) -> p a n", a=2), PS[:, 2:4, :], ACT.Copy).then_inc(y_made, 1)

        def dve_experts(dve):
            nb = blocks(dve)

            def tokens(j):
                for b in range(2):
                    dve.wait_ge(hsh_made, 2 * j + (b + 1))
                    dve.tensor_tensor(Hl[:, 4 * b:4 * b + 4, 0:128],
                                      PS[:, 4 + b, :].rearrange("p (k n) -> p k n", k=4),
                                      Hh[:, 4 * b:4 * b + 4, 0:128].bitcast(f32), ALU.subtract).then_inc(hsl_made, 1)

            def product_lo(c, j):
                dve.wait_ge(eguh_made, j * MC + (c + 1))
                dve.tensor_tensor(gu_l[:, c % 2, 0:256], PS[:, 6 + c % 2, 0:256],
                                  gu_h[:, c % 2, 0:256].bitcast(f32), ALU.subtract).then_inc(egul_made, 1)

            tokens(0)
            with dve.Fori(0, nb) as j:
                for w, (kind, c, q) in enumerate(E_ORDER):
                    dve_unit_lo(dve, w + RING, j)
                    if kind == "gu" and q == 3:
                        dve.wait_ge(esilu_made, j * MC + (c + 1))
                        dve.tensor_tensor(gp[:, c % 2, 0:256], gp[:, c % 2, 0:256], PS[:, c % 2, 256:512],
                                          ALU.mult).then_inc(eprod_made, 1)
                        if c == MC - 1:
                            tokens(j + 1)
                    if kind == "gu" and q == 1 and c >= 1:
                        product_lo(c - 1, j)
                    if kind == "dn" and q == 0 and c == MC - 2:
                        product_lo(MC - 1, j)

        def pe_experts(pe):
            nb = blocks(pe)

            def turn_tokens(j):
                pe.wait_ge(tok_in, j * 16 + 16)
                for k in range(KT):
                    last = pe.transpose(PS[:, 4 + k // 4, 128 * (k % 4):128 * (k % 4) + 128],
                                        hsn[:, 128 * k:128 * k + 128], C("ident"))
                last.then_inc(tok_turned, 1)

            def turn_product(c, j):
                pe.wait_ge(eprod_made, j * MC + (c + 1))
                for r in range(2):
                    last = pe.transpose(PS[:, 6 + c % 2, 128 * r:128 * r + 128],
                                        gp[:, c % 2, 128 * r:128 * r + 128], C("ident"))
                last.then_inc(etr_made, 1)

            pe.wait_ge(hn_copied, 6)
            turn_tokens(0)
            with pe.Fori(0, nb) as j:
                for w, (kind, c, q) in enumerate(E_ORDER):
                    s = slot(w)
                    if w == 0:
                        pe.wait_ge(hsl_made, 2 * j + 2)
                    if kind == "dn" and q == 0:
                        pe.wait_ge(egul_made, j * MC + (c + 1))
                    pe.wait_ge(lo_made, j * UB + (U_MOE + w + 1))
                    if kind == "gu":
                        for k in range(2):
                            h, l = Hh[:, 2 * q + k, 0:128], Hl[:, 2 * q + k, 0:128]
                            for lhs, wt in ((h, whi), (h, wlo), (l, whi)):
                                last = pe.matmul(PS[:, c % 2, :], lhs, wt[:, s, 512 * k:512 * k + 512],
                                                 start=(q == 0 and k == 0 and lhs is h and wt is whi),
                                                 stop=(q == 3 and k == 1 and lhs is l))
                    else:
                        h, l = (x[:, c % 2, 128 * q:128 * q + 128] for x in (gu_h, gu_l))
                        for lhs, wt in ((h, whi), (h, wlo), (l, whi)):
                            for half in range(2):
                                last = pe.matmul(PS[:, 2 + half, :], lhs, wt[:, s, 512 * half:512 * half + 512],
                                                 start=(c == 0 and q == 0 and lhs is h and wt is whi),
                                                 stop=(c == MC - 1 and q == 1 and lhs is l))
                    last.then_inc(unit_used, 1)
                    if kind == "gu" and q == 1 and c >= 1:
                        turn_product(c - 1, j)
                    if kind == "gu" and q == 3 and c == MC - 1:
                        turn_tokens(j + 1)
                    if kind == "dn" and q == 0 and c == MC - 2:
                        turn_product(MC - 1, j)

        def pool_experts(pool, ch):
            pool.wait_ge(hn_copied, 6)
            nb = blocks(pool)
            pool.wait_ge(zeroed, 16 * (NBMAX + 1))
            for t in range(TT):
                for kk in range(2):
                    pool.indirect_dma_start(scr["tok"], bass.IndirectOffsetOnAxis(ap=slot_u[:, t, kk:kk + 1], axis=0),
                                            Hn[:, t, :], None).then_inc(scattered, 16)
            pool.wait_ge(scattered, 96)
            pool.dma_start(hsn, scr["tok"][0:128, :]).then_inc(tok_in, 16)
            pool.sem_inc(yb_free, 1)
            with pool.Fori(0, nb) as j:
                pool.wait_ge(tok_turned, j + 1)
                pool.sem_inc(pool_pass, 1)
                pool.dma_start(hsn, scr["tok"][bass.ds(j * 128 + 128, 128), :]).then_inc(tok_in, 16)
                pool.wait_ge(y_made, j + 1)
                pool.sem_inc(pool_pass, 1)
                pool.dma_start(scr["tok"][bass.ds(j * 128, 128), :], yb).then_inc(y_out, 16)
                pool.wait_ge(y_out, j * 16 + 16)
                pool.sem_inc(yb_free, 1)
            pool.wait_ge(tok_turned, nb + 1)
            pool.sem_inc(pool_pass, 1)
            for t in range(TT):
                for kk in range(2):
                    pool.indirect_dma_start(Yg[:, t, kk, :], None, scr["tok"],
                                            bass.IndirectOffsetOnAxis(ap=slot_u[:, t, kk:kk + 1], axis=0)
                                            ).then_inc(y_back[t], 16)

        def act_weight(act, t):
            act.wait_ge(y_back[t], 32)
            act.activation(Yg[:, t, 0, :], Yg[:, t, 0, :], ACT.Identity, scale=wts[:, t, 0:1],
                           bias=C("small", 128, 2, 1)).then_inc(y_mixed, 1)

        def mixed(dve, ch, t):
            dve.wait_ge(y_mixed, t + 1)
            ch.step(dve.scalar_tensor_tensor(Yg[:, t, 0, :], Yg[:, t, 1, :], wts[:, t, 1:2], Yg[:, t, 0, :],
                                             ALU.mult, ALU.add))
            return Yg[:, t, 0, :].rearrange("p (a n) -> p a n", a=2)

        def tail_sp(sp):
            sp_experts(sp)
            for t in range(TT):
                if t < TT - 1:
                    sp.wait_ge(x_done, 3 * TT + t + 1)
                else:
                    sp.wait_ge(x_last, 1)
                dst = out["yp"][0] if t == 0 else out["ys"][0, 128 * (t - 1):128 * t, :]
                sp.dma_start(dst, X[:, t, :]).then_inc(x_out, 16)
            sp.wait_ge(x_out, 48)

        def tail_act(act, ch, sp_):
            act_mixer1(act, ch, sp_)
            sp_.upto(U_MOE - 1)
            for v in range(RING - 1):
                act_unit_hi(act, v)
            act_norm(act, ch, 2, parts=False)
            act_unit_hi(act, RING - 1)
            act_route(act, ch)
            act_experts(act)
            for t in range(TT):
                act_weight(act, t)
            act_norm(act, ch, 3, turn=False)

        def tail_dve(dve, ch, sp_):
            dve_mixer1(dve, ch, sp_)
            sp_.upto(U_MOE - 1)
            for v in range(RING - 1):
                dve_unit_lo(dve, v)
            dve_norm(dve, ch, 2, lambda: dve.wait_ge(unit_used, U_MOE), parts=False)
            dve_unit_lo(dve, RING - 1)
            dve_route(dve, ch)
            dve_experts(dve)
            dve_norm(dve, ch, 3, lambda: None, turn=False, from_=lambda t: mixed(dve, ch, t))
            dve.wait_ge(ln_in, 32 * 4)
            dve.wait_ge(normed, 4 * TT)
            ch.step(dve.tensor_tensor(X[:, TT - 1, :], X[:, TT - 1, :], lng, ALU.mult))
            dve.tensor_tensor(X[:, TT - 1, :], X[:, TT - 1, :], lnb, ALU.add).then_inc(x_last, 1)

        def tail_pool(pool, ch):
            pool_ada(pool, LATE)
            pool_mixer1(pool, ch)
            pool.wait_ge(c_out[0], 16 * HM)
            pool.wait_ge(c_out[1], 16 * HM)
            pool.wait_ge(m_out, 32)
            pool.wait_ge(mh_lo, HM)
            pool_norm_load(pool, 2)
            pool_norm(pool, ch, 2)
            pool_norm_load(pool, 3)
            pool_experts(pool, ch)
            pool_norm(pool, ch, 3)

        def tail_pe(pe):
            pe_turn(pe, 2)
            pe_mixer1(pe)
            pe.wait_ge(mh_lo, HM)
            pe.wait_ge(nf_made, 1)
            pe_out(pe, U_OUTC)
            pe_turn(pe, 3)
            pe_route(pe)
            pe_experts(pe)

        block = ctx.enter_context(nc.Block())

        @block.sync
        def _(sp):
            sp.dma_start(crow[0:8, :], a["c"][0, :].rearrange("(k p) -> k p", p=128)).then_inc(cst_loaded, 16)
            sp.dma_start(crow[8:16, :], a["c_ctx"].rearrange("(k p) -> k p", p=128)).then_inc(cst_loaded, 16)
            sp.dma_start(crow[16:20, :], a["pool_scale"][0].rearrange("(k p) -> k p", p=128)).then_inc(cst_loaded, 16)
            sp.dma_start(crow[20:28, :], a["mlstm_norm_g"][0].rearrange("(k p) -> k p", p=128)).then_inc(cst_loaded, 16)
            sp.dma_start(crow[28:29, :], a["diff_norm_g"]).then_inc(cst_loaded, 16)
            for i, name in enumerate(("ln_g", "ln_b")):
                sp.dma_start(lnrow[32 * i:32 * i + 32, :], a[name].rearrange("l s (k p) -> (l s k) p", p=128)
                             ).then_inc(cst_loaded, 16)
            sp.dma_start(cst[:, :], a["const"]).then_inc(cst_loaded, 16)
            stream(sp, 0, 2 * RING)
            sp.dma_start(X[:, 0, :], a["x_prompt"][0]).then_inc(x_loaded, 16)
            for t in range(2):
                sp.dma_start(X[:, 1 + t, :], a["x_sample"][0, 128 * t:128 * t + 128, :]).then_inc(x_loaded, 16)
            stream(sp, 2 * RING, U_MOE)
            tail_sp(sp)

        @block.scalar
        def _(act):
            ch = Chain(act, act_step)
            sp_ = Splits(act, True)
            act.dma_start(lamr[0:1, 0:256], a["diff_lambda"][0].rearrange("(a j) d -> a (j d)", a=1)).then_inc(par_loaded, 16)
            act.dma_start(rbb[:, :], a["router_b"][0:1, :].to_broadcast([128, NE])).then_inc(par_loaded, 16)
            act.dma_start(rwt[:, :, :], a["router_w"][0].rearrange("(k p) e -> p k e", p=128)).then_inc(par_loaded, 16)
            for d in range(2):
                for dst, o in ((bgi, 0), (bgf, 8)):
                    act.dma_start(dst[8 * d:8 * d + 8, :],
                                  a["b_gates_c"][0, 16 * d + o:16 * d + o + 8].rearrange("(p a) -> p a", a=1)
                                  ).then_inc(par_loaded, 16)
            act.dma_start(m0c[:, :], a["state_m"][0, 0].rearrange("d (h a) -> (d h) a", a=1)).then_inc(par_loaded, 16)
            act.wait_ge(cst_loaded, 16 * 8)
            act.activation(crow[0:16, :], crow[0:16, :], ACT.Silu).then_inc(crow_s, 1)
            act.wait_ge(crow_t, 1)
            act.activation(ccol, PS[:, 4, 0:16], ACT.Copy)
            act.activation(pcol[:, :], PS[:, 4, 16:29], ACT.Copy).then_inc(cc_made, 1)
            act.activation(lncol[:, :, :, :].rearrange("p a b c -> p (a b c)"), PS[:, 4, 64:128], ACT.Copy
                           ).then_inc(crow_read, 1)
            act.wait_ge(cc_made, 1)
            act.wait_ge(adaw_zero, 1)
            act.activation(adaw[:, :, 0:4:2], ccol.rearrange("p (g k) -> p k g", g=2), ACT.Copy).then_inc(adaw_hi, 1)
            for i, name in enumerate(("ident", "mask_f", "mask_b")):
                last = act.activation(cr[:, i, :], C(name), ACT.Copy)
            last.then_inc(crow_read, 1)
            sp_.upto(RING - 1)
            act.wait_ge(lam_part, 1)
            act.activation(lams[0:1, 2:4], lams[0:1, 0:2], ACT.Exp).then_inc(lam_exp, 1)
            Ada(act, "act", sp_, FIRST).finish()
            for t in range(TT):
                act_mod(act, 0, t)
                act_upper(act, 0, t)
            act_mixer0(act, ch, sp_)
            sp_.upto(U_FFN + RING - 1)
            act_norm(act, ch, 0)
            act_ffn(act, ch, sp_)
            act_norm(act, ch, 1)
            tail_act(act, ch, sp_)

        @block.vector
        def _(dve):
            ch = Chain(dve, dve_step)
            sp_ = Splits(dve, False)
            dve.wait_ge(par_loaded, 16 * 8)
            lp = lamr[0:1, 0:256].rearrange("p (s j d) -> p s j d", s=2, j=2)
            lq = lamr[0:1, 256:384].rearrange("p (s d) -> p s d", s=2)
            ch.step(dve.tensor_tensor(lq, lp[:, :, 0, :], lp[:, :, 1, :], ALU.mult))
            dve.tensor_reduce(lams[0:1, 0:2], lq, AX.X, ALU.add).then_inc(lam_part, 1)
            dve.wait_ge(cc_made, 1)
            dve.tensor_scalar(ngc, ngc, 1.0 - LAM_INIT, None, ALU.mult)
            dve.wait_ge(adaw_hi, 1)
            dve.tensor_tensor(adaw[:, :, 1:4:2], ccol.rearrange("p (g k) -> p k g", g=2),
                              adaw[:, :, 0:4:2].bitcast(f32), ALU.subtract).then_inc(adaw_lo, 1)
            sp_.upto(RING - 1)
            dve.wait_ge(lam_exp, 1)
            ch.step(dve.tensor_tensor(lams[0:1, 0:1], lams[0:1, 3:4], lams[0:1, 2:3], ALU.subtract))
            dve.tensor_scalar(lams[0:1, 1:2], lams[0:1, 0:1], -LAM_INIT, None, ALU.add).then_inc(lam_row, 1)
            dve.wait_ge(lam_bc, 1)
            dve.tensor_copy(lamc[:, :], PS[:, 5, 0:1]).then_inc(lam_made, 1)
            dve.wait_ge(crow_read, 2)
            Ada(dve, "dve", sp_, FIRST, ch).finish()
            for t in range(TT):
                dve_mod(dve, 0, t)
                dve_lower(dve, 0, t)
            dve.wait_ge(lam_made, 1)
            dve_mixer0(dve, ch, sp_)
            sp_.upto(U_FFN + RING - 1)
            dve_norm(dve, ch, 0, lambda: dve.wait_ge(unit_used, U_FFN))
            dve_ffn(dve, ch, sp_)
            dve_norm(dve, ch, 1, lambda: dve.wait_ge(unit_used, U_INC_T))
            tail_dve(dve, ch, sp_)

        @block.gpsimd
        def _(pool):
            ch = Chain(pool, pool_step)
            pool.memset(adaw[:, :, :].bitcast(f32), 0.0).then_inc(adaw_zero, 1)
            pool_ada(pool, FIRST)
            pool.dma_start(ck, a["cache_k"][0, 0].rearrange("h t d -> t h d")).then_inc(att_loaded, 16)
            pool.dma_start(cv, a["cache_v"][0, 0].rearrange("h t d -> t h d")).then_inc(att_loaded, 16)
            pool.dma_start(pw, a["pool_w"][0].rearrange("g c d -> c g d")).then_inc(att_loaded, 16)
            pool.dma_start(pm.rearrange("p g n -> p (g n)"), a["poolm"]).then_inc(att_loaded, 16)
            pool_ada(pool, MID)
            pool.wait_ge(v_made, 1)
            pool.dma_start(out["v"][0, 0].rearrange("h t d -> t h d"),
                           Vn[:, 0, :].rearrange("p (h n) -> p h n", h=HA)).then_inc(cache_out, 16)
            pool.wait_ge(ck_copied, 2)
            pool.dma_start(out["k"][0, 0].rearrange("h t d -> t h d"), kn).then_inc(cache_out, 16)
            pool_ada(pool, EARLY)
            pool.wait_ge(o_lo, NU)
            pool_norm_load(pool, 0)
            pool_norm(pool, ch, 0)
            pool.wait_ge(cache_out, 32)
            ch.step(pool.memset(zero, 0.0))
            for j in range(NBMAX + 1):
                pool.dma_start(scr["tok"][128 * j:128 * j + 128, :], zero).then_inc(zeroed, 16)
            pool.wait_ge(zeroed, 16 * (NBMAX + 1))
            pool_gates_load(pool)
            pool_norm_load(pool, 1)
            pool_norm(pool, ch, 1)
            tail_pool(pool, ch)

        @block.tensor
        def _(pe):
            pe_ada_vectors(pe)
            pe.wait_ge(lam_row, 1)
            pe.matmul(PS[:, 5, 0:1], C("ones", 1), lams[0:1, 1:2], start=True, stop=True).then_inc(lam_bc, 1)
            pe.wait_ge(adaw_lo, 1)
            pe.wait_ge(lam_made, 1)
            Ada(pe, "pe", None, FIRST).finish()
            pe_turn(pe, 0)
            pe_mixer0(pe)
            pe.wait_ge(pool_lo, 4)
            pe.wait_ge(o_lo, NU)
            pe_out(pe, U_OUTA)
            pe_turn(pe, 1)
            pe_ffn(pe)
            tail_pe(pe)


_INS = ["x_prompt", "x_sample", "c", "cache_k", "cache_v", "state_C", "state_n", "state_m", "c_ctx", "ada_w",
        "ada_b", "ln_g", "ln_b", "w_in_a", "diff_lambda", "diff_norm_g", "pool_w", "pool_scale", "w_out_a",
        "ffn_w_gu", "ffn_w_down", "w_in_c", "b_gates_c", "mlstm_norm_g", "w_out_c", "router_w", "router_b",
        "moe_w_gu", "moe_w_down"]
_OUTS = {"yp": (1, 128, D), "ys": (1, 256, D), "k": (1, 1, HA, 128, 128), "v": (1, 1, HA, 128, 128),
         "C": (1, 1, 2, HM, 128, 128), "n": (1, 1, 2, HM, 128), "m": (1, 1, 2, HM)}


def kernel(**inputs):
    import concourse.bacc as bacc
    from concourse.bass_utils import run_bass_kernel_spmd

    nc = bacc.Bacc("TRN2", target_bir_lowering=False, num_devices=1)
    arrays, a = {}, {}
    for name in _INS:
        arrays[f"in_{name}"] = np.ascontiguousarray(inputs[name])
    arrays["in_const"], arrays["in_poolm"] = CONST, POOLM
    for name, x in arrays.items():
        a[name[3:]] = nc.dram_tensor(name, x.shape, mybir.dt.from_np(x.dtype), kind="ExternalInput").ap()
    out = {n: nc.dram_tensor(f"out_{n}", s, mybir.dt.float32, kind="ExternalOutput").ap() for n, s in _OUTS.items()}
    scr = {n: nc.dram_tensor(f"scr_{n}", (128 * (NBMAX + 1), D), mybir.dt.float32).ap() for n in ("tok",)}
    backbone_step(nc, a, out, scr)
    r = run_bass_kernel_spmd(nc, [arrays], core_ids=[0])
    return tuple(r.results[0][f"out_{n}"] for n in _OUTS)
```
